# Optimizing a Trainium2 kernel written in Bass

```python
import math
import jax, jax.numpy as jnp
from jax import lax
import numpy as np

D_MODEL = 1024
BATCH = 1
SEQ = 512
DEPTH = 1

N_GROUPS = 4
GROUP_WIDTH = D_MODEL // N_GROUPS
HEAD_DIM = 64
GROUP_HEADS = GROUP_WIDTH // HEAD_DIM
CONV_CH = GROUP_WIDTH
CONV_WIDTH = 3
NSA_HEADS = GROUP_HEADS
CMP_LEN = 32
CMP_STRIDE = 16
SLC_LEN = 64
N_SLC = 16
WINDOW = 512
CMP_HIDDEN = GROUP_WIDTH
MLA_HEADS = GROUP_HEADS
Q_LORA = 3 * GROUP_WIDTH // 4
KV_LORA = GROUP_WIDTH // 2
NOPE_DIM = HEAD_DIM
ROPE_DIM = HEAD_DIM // 2
V_DIM = HEAD_DIM
ROPE_THETA = 10000.0
SB_HEADS = GROUP_HEADS
N_BUCKETS = 32
MAX_DISTANCE = 128
D_FF = 4 * D_MODEL
Q_BLOCK = 128
EPS = 1e-6

A_SIZES = [CONV_CH] * 3
NSA_SIZES = [NSA_HEADS * HEAD_DIM] + [HEAD_DIM] * 6 + [3 * NSA_HEADS]
MLA_SIZES = [Q_LORA, KV_LORA, ROPE_DIM]
SB_SIZES = [SB_HEADS * HEAD_DIM] * 3
IN_SIZES = A_SIZES + NSA_SIZES + MLA_SIZES + SB_SIZES
IN_COLS = sum(IN_SIZES)


f32 = jnp.float32

def rms_norm(x, w):
    x32 = x.astype(f32)
    y = x32 * lax.rsqrt(jnp.mean(x32 * x32, axis=-1, keepdims=True) + EPS)
    return (y * w.astype(f32)).astype(x.dtype)

def masked_softmax(logits, mask):
    logits = jnp.where(mask, logits, -jnp.inf)
    m = jnp.max(logits, axis=-1, keepdims=True)
    m = jnp.where(jnp.isfinite(m), m, 0.0)
    p = jnp.exp(logits - m)
    s = jnp.sum(p, axis=-1, keepdims=True)
    return p / jnp.where(s > 0, s, 1.0)

def t5_bucket(dist):
    max_exact = N_BUCKETS // 2
    d = jnp.maximum(dist, 0)
    large = max_exact + (jnp.log(jnp.maximum(d, 1).astype(f32) / max_exact)
                         / math.log(MAX_DISTANCE / max_exact) * (N_BUCKETS - max_exact)).astype(jnp.int32)
    large = jnp.minimum(large, N_BUCKETS - 1)
    return jnp.where(d < max_exact, d, large)

def rope_tables(S):
    inv = 1.0 / (ROPE_THETA ** (jnp.arange(0, ROPE_DIM, 2, dtype=f32) / ROPE_DIM))
    ang = jnp.arange(S, dtype=f32)[:, None] * inv[None, :]
    return jnp.cos(ang), jnp.sin(ang)

def apply_rope(x, cos, sin):
    x32 = x.astype(f32)
    x1, x2 = jnp.split(x32, 2, axis=-1)
    c = cos[:, None, :]
    s = sin[:, None, :]
    return jnp.concatenate([x1 * c - x2 * s, x1 * s + x2 * c], axis=-1).astype(x.dtype)

def split_cols(h, sizes):
    return jnp.split(h, np.cumsum(sizes)[:-1].tolist(), axis=-1)

def short_conv_mixer(b_gate, c_gate, u, conv_w, conv_b):
    v = c_gate * u
    y = lax.conv_general_dilated(v, conv_w[:, None, :].astype(v.dtype), window_strides=(1,),
                                 padding=[(CONV_WIDTH - 1, 0)], dimension_numbers=('NWC', 'WIO', 'NWC'),
                                 feature_group_count=v.shape[-1])
    return b_gate * (y + conv_b)

def compress_tokens(kv, cmp_idx, pos, w1, w2):
    B = kv.shape[0]
    blocks = kv[:, cmp_idx] + pos
    hdn = jax.nn.silu(blocks.reshape(B, blocks.shape[1], -1) @ w1)
    return hdn @ w2

def cmp_slc_overlap(n_cmp, n_slc):
    starts = np.arange(n_cmp) * CMP_STRIDE
    ends = starts + CMP_LEN
    s0 = np.arange(n_slc) * SLC_LEN
    s1 = s0 + SLC_LEN
    ov = np.clip(np.minimum(ends[:, None], s1[None]) - np.maximum(starts[:, None], s0[None]), 0, None)
    return (ov / CMP_LEN).astype(np.float32)

def nsa_mixer(q, kc_raw, vc_raw, ks, vs, kw, vw, gate_logits, qn, kn, cmp_pos, cmp_w1, cmp_w2, rel_bias):
    B, S, H, Dh = q.shape
    scale = Dh ** -0.5
    q = rms_norm(q, qn)
    tpos = jnp.arange(S)
    n_cmp = (S - CMP_LEN) // CMP_STRIDE + 1
    cmp_idx = np.arange(n_cmp)[:, None] * CMP_STRIDE + np.arange(CMP_LEN)[None, :]
    kc = rms_norm(compress_tokens(kc_raw, cmp_idx, cmp_pos[0], cmp_w1[0], cmp_w2[0]), kn[0])
    vc = compress_tokens(vc_raw, cmp_idx, cmp_pos[1], cmp_w1[1], cmp_w2[1])
    cmp_end = jnp.arange(n_cmp) * CMP_STRIDE + CMP_LEN - 1
    dist_c = tpos[:, None] - cmp_end[None, :]
    bias_c = rel_bias[t5_bucket(dist_c)].transpose(2, 0, 1)
    logits_c = jnp.einsum('bshd,bnd->bhsn', q, kc).astype(f32) * scale + bias_c
    p_c = masked_softmax(logits_c, dist_c >= 0)
    o_cmp = jnp.einsum('bhsn,bnd->bshd', p_c.astype(vc.dtype), vc)
    n_slc = S // SLC_LEN
    n_sel = min(N_SLC, n_slc)
    score = jnp.einsum('bhsn,nj->bsj', p_c, jnp.asarray(cmp_slc_overlap(n_cmp, n_slc)))
    blk = jnp.arange(n_slc)[None, :]
    t_blk = (tpos // SLC_LEN)[:, None]
    valid = blk * SLC_LEN <= tpos[:, None]
    forced = (blk == 0) | (blk == t_blk) | (blk == t_blk - 1)
    score = jnp.where(forced, jnp.inf, jnp.where(valid, score, -jnp.inf))
    _, sel = lax.top_k(score, n_sel)
    nq = S // Q_BLOCK
    ks_blocks = rms_norm(ks, kn[1]).reshape(B, n_slc, SLC_LEN, Dh)
    vs_blocks = vs.reshape(B, n_slc, SLC_LEN, Dh)
    kw_pad = jnp.pad(rms_norm(kw, kn[2]), ((0, 0), (WINDOW, 0), (0, 0)))
    vw_pad = jnp.pad(vw, ((0, 0), (WINDOW, 0), (0, 0)))
    band = WINDOW + Q_BLOCK
    qi = jnp.arange(Q_BLOCK)
    ki = jnp.arange(band)
    dist_w = qi[:, None] + WINDOW - ki[None, :]
    bias_w = rel_bias[t5_bucket(dist_w)].transpose(2, 0, 1)
    in_window = (dist_w >= 0) & (dist_w < WINDOW)
    bidx = jnp.arange(B)[:, None, None]

    def block(args):
        q_blk, sel_blk, t0 = args
        t_q = t0 + qi
        kg = ks_blocks[bidx, sel_blk]
        vg = vs_blocks[bidx, sel_blk]
        kpos = (sel_blk[..., None] * SLC_LEN + jnp.arange(SLC_LEN)).reshape(B, Q_BLOCK, -1)
        dist_s = t_q[None, :, None] - kpos
        bias_s = rel_bias[t5_bucket(dist_s)].transpose(0, 3, 1, 2)
        logits_s = jnp.einsum('bqhd,bqnkd->bhqnk', q_blk, kg).reshape(B, H, Q_BLOCK, -1).astype(f32) * scale + bias_s
        p_s = masked_softmax(logits_s, (dist_s >= 0)[:, None])
        o_s = jnp.einsum('bhqnk,bqnkd->bqhd', p_s.reshape(B, H, Q_BLOCK, n_sel, SLC_LEN).astype(vg.dtype), vg)
        kb = lax.dynamic_slice_in_dim(kw_pad, t0, band, axis=1)
        vb = lax.dynamic_slice_in_dim(vw_pad, t0, band, axis=1)
        mask_w = in_window & (t0 - WINDOW + ki >= 0)[None, :]
        logits_w = jnp.einsum('bqhd,bkd->bhqk', q_blk, kb).astype(f32) * scale + bias_w
        p_w = masked_softmax(logits_w, mask_w)
        o_w = jnp.einsum('bhqk,bkd->bqhd', p_w.astype(vb.dtype), vb)
        return o_s, o_w

    q_blocks = q.reshape(B, nq, Q_BLOCK, H, Dh).swapaxes(0, 1)
    sel_blocks = sel.reshape(B, nq, Q_BLOCK, n_sel).swapaxes(0, 1)
    o_slc, o_win = lax.map(block, (q_blocks, sel_blocks, jnp.arange(nq) * Q_BLOCK))
    o_slc = o_slc.swapaxes(0, 1).reshape(B, S, H, Dh)
    o_win = o_win.swapaxes(0, 1).reshape(B, S, H, Dh)
    g = jax.nn.sigmoid(gate_logits.astype(f32)).reshape(B, S, H, 3).astype(q.dtype)
    out = g[..., 0:1] * o_cmp + g[..., 1:2] * o_slc + g[..., 2:3] * o_win
    return out.reshape(B, S, H * Dh)

def causal_block_attention(q, k, v, scale):
    B, S, H, _ = q.shape
    nq = S // Q_BLOCK
    kpos = jnp.arange(S)

    def one(args):
        q_blk, t0 = args
        logits = jnp.einsum('bqhd,bkhd->bhqk', q_blk, k).astype(f32) * scale
        mask = kpos[None, :] <= (t0 + jnp.arange(Q_BLOCK))[:, None]
        p = masked_softmax(logits, mask)
        return jnp.einsum('bhqk,bkhd->bqhd', p.astype(v.dtype), v)

    qb = q.reshape(B, nq, Q_BLOCK, H, -1).swapaxes(0, 1)
    out = lax.map(one, (qb, jnp.arange(nq) * Q_BLOCK))
    return out.swapaxes(0, 1).reshape(B, S, H, -1)

def mla_mixer(c_q, c_kv, k_rope, qa_norm, kv_norm, wq_b, wkv_b, qn, kn, cos, sin):
    B, S, _ = c_q.shape
    q = (rms_norm(c_q, qa_norm) @ wq_b).reshape(B, S, MLA_HEADS, NOPE_DIM + ROPE_DIM)
    q = jnp.concatenate([q[..., :NOPE_DIM], apply_rope(q[..., NOPE_DIM:], cos, sin)], axis=-1)
    kv = (rms_norm(c_kv, kv_norm) @ wkv_b).reshape(B, S, MLA_HEADS, NOPE_DIM + V_DIM)
    k_nope, v = kv[..., :NOPE_DIM], kv[..., NOPE_DIM:]
    k_r = apply_rope(k_rope[:, :, None, :], cos, sin)
    k = jnp.concatenate([k_nope, jnp.broadcast_to(k_r, (B, S, MLA_HEADS, ROPE_DIM))], axis=-1)
    q = rms_norm(q, qn)
    k = rms_norm(k, kn)
    o = causal_block_attention(q, k, v, (NOPE_DIM + ROPE_DIM) ** -0.5)
    return o.reshape(B, S, MLA_HEADS * V_DIM)

def stick_breaking_mixer(q, k, v):
    B, S, H, Dh = q.shape
    scale = Dh ** -0.5
    nq = S // Q_BLOCK
    kpos = jnp.arange(S)

    def one(args):
        q_blk, t0 = args
        z = jnp.einsum('bqhd,bkhd->bhqk', q_blk, k).astype(f32) * scale
        strict = kpos[None, :] < (t0 + jnp.arange(Q_BLOCK))[:, None]
        log_1m = jnp.where(strict, jax.nn.log_sigmoid(-z), 0.0)
        rem = lax.cumsum(log_1m, axis=3, reverse=True) - log_1m
        a = jnp.where(strict, jnp.exp(jax.nn.log_sigmoid(z) + rem), 0.0)
        return jnp.einsum('bhqk,bkhd->bqhd', a.astype(v.dtype), v)

    qb = q.reshape(B, nq, Q_BLOCK, H, Dh).swapaxes(0, 1)
    out = lax.map(one, (qb, jnp.arange(nq) * Q_BLOCK))
    return out.swapaxes(0, 1).reshape(B, S, H * Dh)

def first_inputs(seed: int = 0) -> dict:
    key = jax.random.key(seed)
    ks = jax.random.split(key, 24)
    L = DEPTH
    nrm = lambda k, shape, s: jax.random.normal(k, shape, f32) * s
    gain = lambda k, shape: 1.0 + 0.02 * jax.random.normal(k, shape, f32)
    qk_dim = NOPE_DIM + ROPE_DIM
    return {
        "x": jax.random.normal(ks[0], (BATCH, SEQ, D_MODEL), f32),
        "rel_bias": nrm(ks[1], (N_BUCKETS, NSA_HEADS), 0.5),
        "norm1_w": gain(ks[2], (L, D_MODEL)),
        "w_in": nrm(ks[3], (L, D_MODEL, IN_COLS), D_MODEL ** -0.5),
        "conv_w": nrm(ks[4], (L, CONV_WIDTH, CONV_CH), CONV_WIDTH ** -0.5),
        "conv_b": nrm(ks[5], (L, CONV_CH), 0.02),
        "nsa_q_norm": gain(ks[6], (L, HEAD_DIM)),
        "nsa_k_norm": gain(ks[7], (L, 3, HEAD_DIM)),
        "cmp_pos": nrm(ks[8], (L, 2, CMP_LEN, HEAD_DIM), 0.1),
        "cmp_w1": nrm(ks[9], (L, 2, CMP_LEN * HEAD_DIM, CMP_HIDDEN), (CMP_LEN * HEAD_DIM) ** -0.5),
        "cmp_w2": nrm(ks[10], (L, 2, CMP_HIDDEN, HEAD_DIM), CMP_HIDDEN ** -0.5),
        "mla_q_a_norm": gain(ks[11], (L, Q_LORA)),
        "mla_kv_norm": gain(ks[12], (L, KV_LORA)),
        "mla_wq_b": nrm(ks[13], (L, Q_LORA, MLA_HEADS * qk_dim), Q_LORA ** -0.5),
        "mla_wkv_b": nrm(ks[14], (L, KV_LORA, MLA_HEADS * (NOPE_DIM + V_DIM)), KV_LORA ** -0.5),
        "mla_q_norm": gain(ks[15], (L, qk_dim)),
        "mla_k_norm": gain(ks[16], (L, qk_dim)),
        "out_norm_w": gain(ks[17], (L, D_MODEL)),
        "w_out": nrm(ks[18], (L, D_MODEL, D_MODEL), D_MODEL ** -0.5),
        "norm2_w": gain(ks[19], (L, D_MODEL)),
        "ffn_w1": nrm(ks[20], (L, D_MODEL, D_FF), D_MODEL ** -0.5),
        "ffn_w2": nrm(ks[21], (L, D_FF, D_MODEL), D_FF ** -0.5),
    }

def first_block(x, rel_bias, norm1_w, w_in, conv_w, conv_b, nsa_q_norm, nsa_k_norm, cmp_pos, cmp_w1, cmp_w2,
              mla_q_a_norm, mla_kv_norm, mla_wq_b, mla_wkv_b, mla_q_norm, mla_k_norm, out_norm_w, w_out,
              norm2_w, ffn_w1, ffn_w2):
    B, S, D = x.shape
    cos, sin = rope_tables(S)
    for l in range(DEPTH):
        h = rms_norm(x, norm1_w[l])
        cols = split_cols(h @ w_in[l], IN_SIZES)
        a_b, a_c, a_u = cols[0:3]
        n_q, n_kc, n_vc, n_ks, n_vs, n_kw, n_vw, n_g = cols[3:11]
        m_cq, m_ckv, m_kr = cols[11:14]
        s_q, s_k, s_v = cols[14:17]
        y_a = short_conv_mixer(a_b, a_c, a_u, conv_w[l], conv_b[l])
        y_b = nsa_mixer(n_q.reshape(B, S, NSA_HEADS, HEAD_DIM), n_kc, n_vc, n_ks, n_vs, n_kw, n_vw, n_g,
                        nsa_q_norm[l], nsa_k_norm[l], cmp_pos[l], cmp_w1[l], cmp_w2[l], rel_bias)
        y_c = mla_mixer(m_cq, m_ckv, m_kr, mla_q_a_norm[l], mla_kv_norm[l], mla_wq_b[l], mla_wkv_b[l],
                        mla_q_norm[l], mla_k_norm[l], cos, sin)
        y_d = stick_breaking_mixer(s_q.reshape(B, S, SB_HEADS, HEAD_DIM), s_k.reshape(B, S, SB_HEADS, HEAD_DIM),
                                   s_v.reshape(B, S, SB_HEADS, HEAD_DIM))
        y = jnp.concatenate([y_a, y_b, y_c, y_d], axis=-1).reshape(B, S, N_GROUPS, GROUP_WIDTH)
        y = rms_norm(y, out_norm_w[l].reshape(N_GROUPS, GROUP_WIDTH)).reshape(B, S, D)
        x = x + y @ w_out[l]
        h2 = rms_norm(x, norm2_w[l])
        x = x + jnp.square(jax.nn.relu(h2 @ ffn_w1[l])) @ ffn_w2[l]
    return x


MEM_LEN = 256
HG_HEADS = 4
HG_KEY_DIM = 128
HG_VAL_DIM = 128
HG_KW = HG_HEADS * HG_KEY_DIM
HG_VW = HG_HEADS * HG_VAL_DIM
HG_CHUNK = 64
ATT_Q_HEADS = 8
ATT_KV_HEADS = 2
ATT_GROUP = ATT_Q_HEADS // ATT_KV_HEADS
ATT_HEAD_DIM = 64
ATT_QW = ATT_Q_HEADS * ATT_HEAD_DIM
ATT_KVW = ATT_KV_HEADS * ATT_HEAD_DIM
WINDOW_2 = 128
ATT_BLOCK = 128
ROPE_THETA_2 = 500000.0
ROT_DIM = ATT_HEAD_DIM // 4
MEM_HEADS = 4
MEM_HEAD_DIM = D_MODEL // MEM_HEADS
D_FF_2 = 2816
NORM_EPS = 1e-6
IN_SPLITS = (HG_KW, HG_KW, HG_KW, HG_VW, HG_VW, ATT_QW, ATT_KVW, ATT_KVW, D_MODEL, D_MODEL)
IN_COLS_2 = sum(IN_SPLITS)
SPLIT_IDX = [int(c) for c in np.cumsum(IN_SPLITS)[:-1]]


def rms_norm_2(x, g):
    xf = x.astype(jnp.float32)
    y = xf * lax.rsqrt(jnp.mean(xf * xf, axis=-1, keepdims=True) + NORM_EPS) * g.astype(jnp.float32)
    return y.astype(x.dtype)

def partial_rotary(t, positions):
    half = ROT_DIM // 2
    inv_freq = 1.0 / (ROPE_THETA_2 ** (jnp.arange(0, ROT_DIM, 2, dtype=jnp.float32) / ROT_DIM))
    ang = positions.astype(jnp.float32)[..., None] * inv_freq
    cos, sin = jnp.cos(ang)[:, :, None, :], jnp.sin(ang)[:, :, None, :]
    tf = t.astype(jnp.float32)
    t1, t2 = tf[..., :half], tf[..., half:ROT_DIM]
    out = jnp.concatenate([t1 * cos - t2 * sin, t2 * cos + t1 * sin, tf[..., ROT_DIM:]], axis=-1)
    return out.astype(t.dtype)

def gla_chunkwise(q, k, log_f, v):
    B, S, H, K = q.shape
    V = v.shape[-1]
    n_chunks = S // HG_CHUNK

    def chunks(t):
        return t.reshape(B, n_chunks, HG_CHUNK, H, t.shape[-1]).transpose(1, 0, 3, 2, 4)

    incl = jnp.tril(jnp.ones((HG_CHUNK, HG_CHUNK), dtype=bool))[:, :, None]

    def step(state, inp):
        qc, kc, gc, vc = inp
        b = jnp.cumsum(gc, axis=2)
        o_inter = jnp.einsum('bhtk,bhkv->bhtv', qc * jnp.exp(b), state)
        decay = jnp.exp(jnp.where(incl, b[:, :, :, None, :] - b[:, :, None, :, :], -jnp.inf))
        scores = jnp.einsum('bhtk,bhtsk->bhts', qc, decay * kc[:, :, None, :, :])
        o_intra = jnp.einsum('bhts,bhsv->bhtv', scores, vc)
        b_end = b[:, :, -1, :]
        new_state = (jnp.exp(b_end)[..., None] * state
                     + jnp.einsum('bhsk,bhsv->bhkv', kc * jnp.exp(b_end[:, :, None, :] - b), vc))
        return new_state, o_inter + o_intra

    state0 = jnp.zeros((B, H, K, V), jnp.float32)
    _, o = lax.scan(step, state0, (chunks(q), chunks(k), chunks(log_f), chunks(v)))
    return o.transpose(1, 0, 3, 2, 4).reshape(B, S, H, V)

def window_gqa_sink(q, k, v, sink):
    B, S = q.shape[0], q.shape[1]
    nb = S // ATT_BLOCK
    qb = q.reshape(B, nb, ATT_BLOCK, ATT_KV_HEADS, ATT_GROUP, ATT_HEAD_DIM)

    def band(t):
        tp = jnp.pad(t.reshape(B, nb, ATT_BLOCK, ATT_KV_HEADS, ATT_HEAD_DIM),
                     ((0, 0), (1, 1), (0, 0), (0, 0), (0, 0)))
        return jnp.concatenate([tp[:, :-2], tp[:, 1:-1], tp[:, 2:]], axis=2)

    kb, vb = band(k), band(v)
    s = jnp.einsum('bnqhgd,bnkhd->bnhgqk', qb, kb).astype(jnp.float32) * (ATT_HEAD_DIM ** -0.5)
    blk = jnp.arange(nb)[:, None, None]
    qi = blk * ATT_BLOCK + jnp.arange(ATT_BLOCK)[None, :, None]
    kj = (blk - 1) * ATT_BLOCK + jnp.arange(3 * ATT_BLOCK)[None, None, :]
    valid = (jnp.abs(qi - kj) <= WINDOW_2) & (kj >= 0) & (kj < S)
    s = jnp.where(valid[None, :, None, None], s, -jnp.inf)
    sk = sink.astype(jnp.float32).reshape(ATT_KV_HEADS, ATT_GROUP)[None, None, :, :, None, None]
    m = jnp.maximum(jnp.max(s, axis=-1, keepdims=True), sk)
    p = jnp.exp(s - m)
    p = p / (jnp.sum(p, axis=-1, keepdims=True) + jnp.exp(sk - m))
    o = jnp.einsum('bnhgqk,bnkhd->bnqhgd', p.astype(v.dtype), vb)
    return o.reshape(B, S, ATT_QW)

def token_mixers(n, positions, w_in, lb_fwd, lb_bwd, hg_norm, sink, w_br_rec, w_br_att, w_out):
    B, S, _ = n.shape
    f32 = jnp.float32
    proj = n @ w_in
    q_r, fz_f, fz_b, i_r, g_r, q_a, k_a, v_a, gate_r, gate_a = jnp.split(proj, SPLIT_IDX, axis=-1)

    qh = jax.nn.silu(q_r.astype(f32)).reshape(B, S, HG_HEADS, HG_KEY_DIM) * (HG_KEY_DIM ** -0.5)
    vh = i_r.astype(f32).reshape(B, S, HG_HEADS, HG_VAL_DIM)

    def forget(z, lb):
        f = lb + (1.0 - lb) * jax.nn.sigmoid(z.astype(f32))
        return ((1.0 - f).reshape(B, S, HG_HEADS, HG_KEY_DIM),
                jnp.log(f).reshape(B, S, HG_HEADS, HG_KEY_DIM))

    k_f, lf_f = forget(fz_f, lb_fwd)
    k_b, lf_b = forget(fz_b, lb_bwd)
    o_f = gla_chunkwise(qh, k_f, lf_f, vh)
    o_b = gla_chunkwise(qh[:, ::-1], k_b[:, ::-1], lf_b[:, ::-1], vh[:, ::-1])[:, ::-1]
    o = o_f + o_b
    o = (o * lax.rsqrt(jnp.mean(o * o, axis=-1, keepdims=True) + NORM_EPS)
         * hg_norm.astype(f32).reshape(HG_HEADS, HG_VAL_DIM))
    o = o.reshape(B, S, HG_VW) * jax.nn.silu(g_r.astype(f32))
    y_rec = o.astype(n.dtype) @ w_br_rec

    qa = partial_rotary(q_a.reshape(B, S, ATT_Q_HEADS, ATT_HEAD_DIM), positions)
    ka = partial_rotary(k_a.reshape(B, S, ATT_KV_HEADS, ATT_HEAD_DIM), positions)
    va = v_a.reshape(B, S, ATT_KV_HEADS, ATT_HEAD_DIM)
    y_att = window_gqa_sink(qa, ka, va, sink) @ w_br_att

    merged = jax.nn.sigmoid(gate_r) * y_rec + jax.nn.sigmoid(gate_a) * y_att
    return merged @ w_out

def memory_cross_attention(n, mem_n, w_q, w_kv, w_o):
    B, S, _ = n.shape
    M = mem_n.shape[1]
    q = (n @ w_q).reshape(B, S, MEM_HEADS, MEM_HEAD_DIM)
    k, v = jnp.split(mem_n @ w_kv, 2, axis=-1)
    k = k.reshape(B, M, MEM_HEADS, MEM_HEAD_DIM)
    v = v.reshape(B, M, MEM_HEADS, MEM_HEAD_DIM)
    s = jnp.einsum('bshd,bmhd->bhsm', q, k).astype(jnp.float32) * (MEM_HEAD_DIM ** -0.5)
    p = jax.nn.softmax(s, axis=-1).astype(v.dtype)
    o = jnp.einsum('bhsm,bmhd->bshd', p, v).reshape(B, S, D_MODEL)
    return o @ w_o

def conv_ffn(n, w_up, conv_w, conv_b, w_down):
    S = n.shape[1]
    u, g = jnp.split(n @ w_up, 2, axis=-1)
    pad = CONV_WIDTH // 2
    gp = jnp.pad(g, ((0, 0), (pad, pad), (0, 0)))
    gc = sum(gp[:, j:j + S] * conv_w[j] for j in range(CONV_WIDTH)) + conv_b
    return (jax.nn.silu(gc) * u) @ w_down

def second_inputs(seed: int = 0) -> dict:
    key = jax.random.key(seed)
    ks = jax.random.split(key, 24)

    def nrm(k, shape, scale):
        return jax.random.normal(k, shape, jnp.float32) * scale

    def gain(k, shape):
        return 1.0 + 0.02 * jax.random.normal(k, shape, jnp.float32)

    L, D = DEPTH, D_MODEL
    return {
        'x': nrm(ks[0], (BATCH, SEQ, D), 1.0),
        'mem': nrm(ks[1], (BATCH, MEM_LEN, D), 1.0),
        'positions': jnp.broadcast_to(jnp.arange(SEQ, dtype=jnp.int32), (BATCH, SEQ)),
        'norm_mix': gain(ks[2], (L, D)),
        'w_in': nrm(ks[3], (L, D, IN_COLS_2), D ** -0.5),
        'lower_bounds': nrm(ks[4], (2, L + 1, HG_KW), 0.5),
        'hg_norm': gain(ks[5], (L, HG_VW)),
        'attn_sink': nrm(ks[6], (L, ATT_Q_HEADS), 0.5),
        'w_br_rec': nrm(ks[7], (L, HG_VW, D), HG_VW ** -0.5),
        'w_br_att': nrm(ks[8], (L, ATT_QW, D), ATT_QW ** -0.5),
        'w_mix_out': nrm(ks[9], (L, D, D), D ** -0.5),
        'norm_mem': gain(ks[10], (L, D)),
        'norm_mem_kv': gain(ks[11], (L, D)),
        'w_mem_q': nrm(ks[12], (L, D, D), D ** -0.5),
        'w_mem_kv': nrm(ks[13], (L, D, 2 * D), D ** -0.5),
        'w_mem_o': nrm(ks[14], (L, D, D), D ** -0.5),
        'norm_ffn': gain(ks[15], (L, D)),
        'w_up': nrm(ks[16], (L, D, 2 * D_FF_2), D ** -0.5),
        'conv_w': nrm(ks[17], (L, CONV_WIDTH, D_FF_2), CONV_WIDTH ** -0.5),
        'conv_b': nrm(ks[18], (L, D_FF_2), 0.01),
        'w_down': nrm(ks[19], (L, D_FF_2, D), D_FF_2 ** -0.5),
        'final_norm': gain(ks[20], (D,)),
    }

def second_block(x, mem, positions, norm_mix, w_in, lower_bounds, hg_norm, attn_sink, w_br_rec,
              w_br_att, w_mix_out, norm_mem, norm_mem_kv, w_mem_q, w_mem_kv, w_mem_o, norm_ffn,
              w_up, conv_w, conv_b, w_down, final_norm):
    lb_table = jnp.cumsum(jax.nn.softmax(lower_bounds.astype(jnp.float32), axis=1), axis=1)
    h = x
    for l in range(DEPTH):
        n = rms_norm_2(h, norm_mix[l])
        h = h + token_mixers(n, positions, w_in[l], lb_table[0, l], lb_table[1, l], hg_norm[l],
                             attn_sink[l], w_br_rec[l], w_br_att[l], w_mix_out[l])
        n = rms_norm_2(h, norm_mem[l])
        mem_n = rms_norm_2(mem, norm_mem_kv[l])
        h = h + memory_cross_attention(n, mem_n, w_mem_q[l], w_mem_kv[l], w_mem_o[l])
        n = rms_norm_2(h, norm_ffn[l])
        h = h + conv_ffn(n, w_up[l], conv_w[l], conv_b[l], w_down[l])
    return rms_norm_2(h, final_norm)


def setup_inputs(seed=0):
    out = dict(first_inputs(seed))
    for name, value in second_inputs(seed + 1).items():
        if name != "x":
            out[name + "_2"] = value
    return out


def reference(
    x, rel_bias, norm1_w, w_in, conv_w, conv_b, nsa_q_norm, nsa_k_norm, cmp_pos, cmp_w1, cmp_w2,
    mla_q_a_norm, mla_kv_norm, mla_wq_b, mla_wkv_b, mla_q_norm, mla_k_norm, out_norm_w, w_out,
    norm2_w, ffn_w1, ffn_w2, mem_2, positions_2, norm_mix_2, w_in_2, lower_bounds_2, hg_norm_2,
    attn_sink_2, w_br_rec_2, w_br_att_2, w_mix_out_2, norm_mem_2, norm_mem_kv_2, w_mem_q_2,
    w_mem_kv_2, w_mem_o_2, norm_ffn_2, w_up_2, conv_w_2, conv_b_2, w_down_2, final_norm_2,
):
    x = first_block(
        x, rel_bias, norm1_w, w_in, conv_w, conv_b, nsa_q_norm, nsa_k_norm, cmp_pos, cmp_w1,
        cmp_w2, mla_q_a_norm, mla_kv_norm, mla_wq_b, mla_wkv_b, mla_q_norm, mla_k_norm,
        out_norm_w, w_out, norm2_w, ffn_w1, ffn_w2,
    )
    return second_block(
        x, mem_2, positions_2, norm_mix_2, w_in_2, lower_bounds_2, hg_norm_2, attn_sink_2,
        w_br_rec_2, w_br_att_2, w_mix_out_2, norm_mem_2, norm_mem_kv_2, w_mem_q_2, w_mem_kv_2,
        w_mem_o_2, norm_ffn_2, w_up_2, conv_w_2, conv_b_2, w_down_2, final_norm_2,
    )


_drawn_inputs = setup_inputs


def setup_inputs(seed=0):
    import zlib

    import numpy as np

    out = dict(_drawn_inputs(seed))
    spreads = {}
    factors = {'conv_b': 6.658,
     'nsa_q_norm': 8.0,
     'nsa_k_norm': 8.0,
     'mla_q_a_norm': 7.111,
     'mla_kv_norm': 5.164,
     'mla_q_norm': 7.855,
     'mla_k_norm': 7.165,
     'out_norm_w': 3.592,
     'norm2_w': 3.543,
     'norm_mix_2': 8.0,
     'lower_bounds_2': 8.0,
     'hg_norm_2': 8.0,
     'attn_sink_2': 8.0,
     'norm_mem_2': 8.0,
     'norm_mem_kv_2': 8.0,
     'norm_ffn_2': 20.468,
     'conv_b_2': 56.433,
     'final_norm_2': 8.039}
    for name, (base, spread) in spreads.items():
        noise = np.random.default_rng([zlib.crc32(name.encode()), seed]).standard_normal(out[name].shape)
        drawn = base * np.exp(spread * noise) if base else spread * noise
        out[name] = __import__('jax').numpy.asarray(drawn.astype(out[name].dtype))
    for name, factor in factors.items():
        out[name] = (out[name] * factor).astype(out[name].dtype)
    return out
```

```python
import math
from contextlib import ExitStack

import numpy as np

import concourse.bass as bass
from concourse import mybir

ALU = mybir.AluOpType
ACT = mybir.ActivationFunctionType
AX_X = mybir.AxisListType.X
F32 = mybir.dt.float32
I32 = mybir.dt.int32
U32 = mybir.dt.uint32

P = 128
S = 512
D = 1024
TT = S // P
KT = D // P
EPS = 1e-6
MASKED = -1e30
NO_KEY = 1e28

SLOTS = 4
SLOT = 2048

N_CMP = 31
STRIP = 640
FWD = 992


def bucket(dist):
    d = max(dist, 0)
    if d < 16:
        return d
    return min(16 + int(math.log(d / 16) / math.log(128 / 16) * 16), 31)


def make_consts():
    parts = {}
    eye = np.eye(P, dtype=np.float32)
    parts["ident"] = eye
    parts["ones"] = np.ones((P, P), np.float32)
    parts["blk64"] = np.kron(np.eye(2), np.ones((64, 64))).astype(np.float32)
    row, col = np.arange(P)[:, None], np.arange(P)[None, :]
    parts["suffix"] = (row >= col).astype(np.float32)
    parts["strict"] = (row < col).astype(np.float32)
    parts["neg_strict"] = np.where(row < col, 0, MASKED).astype(np.float32)
    j = np.arange(S)[None, :]
    parts["causal"] = np.where(j <= row + (S - P), 0, MASKED).astype(np.float32)
    turn = np.zeros((P, P), np.float32)
    for i in range(16):
        turn[80 + i, 64 + i] = -1
        turn[64 + i, 80 + i] = 1
    parts["turn96"] = turn[:, :96]
    inv = 1.0 / (10000.0 ** (np.arange(0, 32, 2, dtype=np.float32) / np.float32(32)))
    ang = np.arange(S, dtype=np.float32)[:, None] * inv[None, :].astype(np.float32)
    cos96, sin96 = np.ones((P, S), np.float32), np.zeros((P, S), np.float32)
    cos96[64:96] = np.tile(np.cos(ang).T, (2, 1))
    sin96[64:96] = np.tile(np.sin(ang).T, (2, 1))
    parts["cos96"], parts["sin96"] = cos96, sin96
    j = np.arange(3 * P)[None, :] - P
    parts["band"] = np.where(np.abs(j - row) <= P, 0, MASKED).astype(np.float32)
    turn = np.zeros((P, P), np.float32)
    inv2 = (1.0 / (500000.0 ** (np.arange(0, 16, 2, dtype=np.float32) / np.float32(16)))).astype(np.float32)
    rate = np.zeros((P, 1), np.float32)
    for b in (0, 64):
        for i in range(8):
            turn[b + 8 + i, b + i] = -1
            turn[b + i, b + 8 + i] = 1
            rate[b + i] = rate[b + 8 + i] = inv2[i]
    parts["turn16"] = turn
    parts["rate"] = rate
    for n in range(7):
        w = 1 << n
        same = (row // (2 * w)) == (col // (2 * w))
        parts[f"lvf{n}"] = (same & (row % (2 * w) < w) & (col % (2 * w) >= w)).astype(np.float32)
        parts[f"lvb{n}"] = (same & (row % (2 * w) >= w) & (col % (2 * w) < w)).astype(np.float32)
    t = np.arange(S)[None, :] + 0 * row
    parts["carryf"] = (t % P != 0).astype(np.float32)
    parts["carryb"] = (t % P != P - 1).astype(np.float32)
    at, where = 0, {}
    for name, a in parts.items():
        where[name] = (at, a.shape[1])
        at += a.shape[1]
    hot = np.zeros((33, STRIP + FWD), np.float32)
    for y in range(STRIP):
        d = S - 1 - y
        hot[bucket(d) if d >= 0 else 32, y] = 1
    for y in range(FWD):
        d = y - (S - 1)
        hot[bucket(d) if d >= 0 else 32, STRIP + y] = 1
    return np.ascontiguousarray(np.concatenate(list(parts.values()), 1)), where, hot


COLUMNS = [
    ("norm1", 8), ("conv_w", 6), ("conv_b", 2), ("qn", 1), ("kn0", 1), ("kn12", 1), ("pos", 32), ("qa", 2),
    ("kvn", 1), ("mqn", 1), ("mkn", 1), ("onw", 8), ("norm2", 8),
    ("nmix", 8), ("lb", 16), ("hgn", 4), ("nmem", 8), ("nmkv", 8), ("nffn", 8), ("unused", 4),
    ("cw2", 66), ("cb2", 22), ("fin", 8),
]


def two_blocks(nc, A, out):
    consts, where, _ = make_consts()
    ctx = ExitStack()
    with ctx:
        def sb(name, cols, dt=F32):
            return ctx.enter_context(nc.sbuf_tensor(name, [P, cols], dt))

        def sem(name):
            return ctx.enter_context(nc.semaphore(name))

        SHARED = where["suffix"][0]
        b2_names = ("band", "turn16", "rate", *(f"lv{d}{n}" for n in range(7) for d in "fb"), "carryf", "carryb")
        b1_names = ("suffix", "strict", "neg_strict", "causal", "turn96", "cos96", "sin96")
        b1_cols = sum(where[n][1] for n in b1_names)
        b2_cols = sum(where[n][1] for n in b2_names)
        const_sb = sb("const_sb", SHARED + max(b1_cols, b2_cols))
        place = {n: where[n][0] for n in ("ident", "ones", "blk64")}
        for names in (b1_names, b2_names):
            at = SHARED
            for n in names:
                place[n] = at
                at += where[n][1]

        def const(name):
            return const_sb[:, place[name]:place[name] + where[name][1]]

        ncol = sum(w for _, w in COLUMNS)
        col_sb = sb("col_sb", ncol)
        rel_sb = sb("rel_sb", 4)
        cw2_sb = sb("cw2_sb", 256)
        sink_sb = sb("sink_sb", 8)
        col_at, at = {}, 0
        for n, w in COLUMNS:
            col_at[n] = at
            at += w

        def col(name, i=0, rows=slice(0, P)):
            return col_sb[rows, col_at[name] + i:col_at[name] + i + 1]

        ring = sb("ring", SLOTS * SLOT)
        res = sb("res", KT * S)
        act_in = sb("act_in", KT * S)
        mix = sb("mix", KT * S)
        arena = sb("arena", 32 * S)
        strips = sb("strips", 4 * S)
        cmp_bias = sb("cmp_bias", 4 * S)
        sq = sb("sq", 4 * S)
        rb = sb("rb", 2 * S)
        prob = sb("prob", 2 * S)
        prob_t = sb("prob_t", 2 * S)
        small = sb("small", 64)

        def tile(buf, i, w=S):
            return buf[:, i * w:(i + 1) * w]

        def xt(k):
            return tile(res, k)

        def nt(k):
            return tile(act_in, k)

        def yt(k):
            return tile(mix, k)

        def ar(i, n=1):
            return arena[:, i * S:(i + n) * S]

        bank = [ctx.enter_context(nc.psum_tensor(f"bank{i}", [P, S], F32)) for i in range(8)]
        ident, ones, blk64 = const("ident"), const("ones"), const("blk64")

        strip_dram = nc.dram_tensor("strip_dram", [4, P * STRIP], F32).ap()
        fwd_dram = nc.dram_tensor("fwd_dram", [4, N_CMP * FWD], F32).ap()

        const_in = sem("const_in")
        hot_in = sem("hot_in")
        cols_in = sem("cols_in")
        cols_zero = sem("cols_zero")
        cols_turned = sem("cols_turned")
        cols_out = sem("cols_out")
        x_in = sem("x_in")
        mem_in = sem("mem_in")
        pos_in = sem("pos_in")
        const2_in = sem("const2_in")
        slot_in = [sem(f"slot_in{i}") for i in range(SLOTS)]
        slot_mid = sem("slot_mid")
        tile_filled = sem("tile_filled")
        taken_act = sem("taken_act")
        taken_dve = sem("taken_dve")
        big_sq = sem("big_sq")
        big_add = sem("big_add")
        big_ss = sem("big_ss")
        big_rb = sem("big_rb")
        big_out = sem("big_out")
        nrm_sq = sem("nrm_sq")
        nrm_ss = sem("nrm_ss")
        nrm_rb = sem("nrm_rb")
        nrm_out = sem("nrm_out")
        bias_rep = sem("bias_rep")
        bias_mm = sem("bias_mm")
        bias_sb = sem("bias_sb")
        bias_out = sem("bias_out")
        bias_in = sem("bias_in")
        act_own = sem("act_own")
        dve_own = sem("dve_own")
        pool_own = sem("pool_own")
        turned = sem("turned")
        rope_out = sem("rope_out")
        conv_v = sem("conv_v")
        blocks_out = sem("blocks_out")
        hid_exp = sem("hid_exp")
        hid_out = sem("hid_out")
        score_mm = sem("score_mm")
        score_sh = sem("score_sh")
        exp_out = sem("exp_out")
        prob_out = sem("prob_out")
        trans_mm = sem("trans_mm")
        trans_act = sem("trans_act")
        trans_dve = sem("trans_dve")
        pv_mm = sem("pv_mm")
        head_out = sem("head_out")
        gates_out = sem("gates_out")
        sb_z = sem("sb_z")
        sb_zs = sem("sb_zs")
        sb_sp = sem("sb_sp")
        sb_c = sem("sb_c")
        sb_l = sem("sb_l")
        sb_t = sem("sb_t")
        sb_e = sem("sb_e")
        sb_a = sem("sb_a")
        sb_o = sem("sb_o")

        own = {"act": [0, act_own], "dve": [0, dve_own], "pool": [0, pool_own]}

        def link(eng, who, ins):
            own[who][0] += 1
            ins.then_inc(own[who][1], 1)
            eng.wait_ge(own[who][1], own[who][0])

        def cut(w, r0, rows, c0, cols):
            return w[r0:r0 + rows, c0:c0 + cols].rearrange("(k p) c -> p k c", p=P)

        w_in, w_out = A["w_in"][0], A["w_out"][0]
        w1, w2 = A["ffn_w1"][0], A["ffn_w2"][0]
        loads, load_at = [], {}

        def load(name, *parts):
            load_at[name] = len(loads)
            loads.append(parts)

        def wide(name, w, c0, r0=0, cols=256):
            load(name, (cols, 0, cut(w, r0, D, c0, cols)))

        for n, c0 in (("a_b", 0), ("a_c", 256), ("a_u", 512), ("n_q", 768)):
            wide(n, w_in, c0)
        load("n_k", (256, 0, cut(w_in, 0, D, 1024, 192)), (256, 192, cut(w_in, 0, D, 1280, 64)))
        load("m_q", (256, 0, cut(w_in, 0, D, 1420, 192)), (256, 192, cut(w_in, 0, D, 1740, 32)),
             (256, 224, cut(w_in, 0, D, 1408, 12)))
        load("m_kv", (256, 0, cut(w_in, 0, D, 1612, 128)), (256, 128, cut(w_in, 0, D, 1216, 64)),
             (256, 192, cut(w_in, 0, D, 1344, 64)))
        for n, c0 in (("s_q", 1772), ("s_k", 2028), ("s_v", 2284)):
            wide(n, w_in, c0)
        load("small", ("wq", None, None))
        for kv in range(2):
            for half in range(2):
                load(f"cmp{kv}{half}", (256, 0, cut(A["cmp_w1"][0, kv], half * D, D, 0, 256)))
        for i in range(4):
            wide(f"out{i}", w_out, 256 * i)
        FFN1_UP = len(loads)
        for i in range(16):
            wide(f"up{i}", w1, 256 * i)
        FFN1_DOWN = len(loads)
        for i in range(4):
            for q in range(4):
                wide(f"down{i}_{q}", w2, 256 * i, r0=q * D)
        w_in2 = A["w_in_2"][0]
        for i in range(10):
            wide(f"p{i}", w_in2, 256 * i)
        for i in range(3):
            wide(f"p{10 + i}", w_in2, 256 * (10 + i))
        for i in range(4):
            wide(f"gr{i}", w_in2, 3328 + 256 * i)
            wide(f"ga{i}", w_in2, 4352 + 256 * i)
            load(f"br{i}", (256, 0, cut(A["w_br_rec_2"][0], 0, 512, 256 * i, 256)),
                 (256, 0, cut(A["w_br_att_2"][0], 0, 512, 256 * i, 256), 1024))
        for i in range(4):
            wide(f"mix{i}", A["w_mix_out_2"][0], 256 * i)
        for i in range(8):
            wide(f"mkv{i}", A["w_mem_kv_2"][0], 256 * i)
        for n in ("q", "o"):
            for i in range(4):
                wide(f"mem_{n}{i}", A[f"w_mem_{n}_2"][0], 256 * i)
        for i in range(11):
            wide(f"g2_{i}", A["w_up_2"][0], 2816 + 256 * i)
            wide(f"u2_{i}", A["w_up_2"][0], 256 * i)
        for i in range(4):
            for q in range(3):
                load(f"d2_{i}_{q}", (256, 0, cut(A["w_down_2"][0], q * D, min(D, 2816 - q * D), 256 * i, 256)))

        def slot(name):
            s = load_at[name] % SLOTS
            return ring[:, s * SLOT:(s + 1) * SLOT]

        WKV_AT = 768

        def small_parts(dst):
            wq, wkv = A["mla_wq_b"][0], A["mla_wkv_b"][0]
            return [
                (dst[:, 0:384], wq[0:P, :]), (dst[0:64, 384:768], wq[P:192, :]), (dst[:, WKV_AT:WKV_AT + S], wkv),
            ]

        def part_list(i):
            s = i % SLOTS
            dst = ring[:, s * SLOT:(s + 1) * SLOT]
            if loads[i][0][0] == "wq":
                return small_parts(dst)
            found = []
            for cols, c0, src, *base in loads[i]:
                k, c = src.shape[1], src.shape[2]
                at = base[0] if base else 0
                found.append((dst[:, at:at + k * cols].rearrange("p (k c) -> p k c", c=cols)[:, :, c0:c0 + c], src))
            return found

        parts_of = [3 if x[0][0] == "wq" else len(x) for x in loads]

        def slot_ready(eng, name):
            i = load_at[name]
            eng.wait_ge(slot_in[i % SLOTS], 16 * sum(parts_of[j] for j in range(i % SLOTS, i + 1, SLOTS)))

        tiles, tile_at = [], {}

        def plan(name, who, load_name=None, ends=False):
            tile_at[name] = len(tiles)
            tiles.append((name, who))
            if ends:
                released[load_at[load_name]] = ("tile", len(tiles))

        released = {}
        mids = [0]

        def mid(load_name):
            mids[0] += 1
            released[load_at[load_name]] = ("mid", mids[0])

        for k in range(KT):
            plan(f"x{k}", "act")
        for t in ("a_b", "a_c", "a_u", "n_q"):
            plan(f"{t}0", "dve" if t == "a_u" else "act")
            plan(f"{t}1", "dve" if t == "a_u" else "act", t, True)
        plan("kcvc", "act")
        plan("kskw", "act", "n_k", True)
        plan("cq0", "act")
        plan("cq1", "act")
        plan("gates", "act", "m_q", True)
        plan("ckv", "act")
        plan("nv", "dve", "m_kv", True)
        for t in ("s_q", "s_k"):
            plan(f"{t}0", "act")
            plan(f"{t}1", "act", t, True)
        plan("s_v0", "dve")
        plan("s_v1", "dve", "s_v", True)
        for h in range(4):
            plan(f"mq{h}", "act")
        for h in range(4):
            plan(f"mk{h}", "act")
        plan("mv0", "dve")
        plan("mv1", "dve", "small", True)
        for kv in range(2):
            plan(f"hid{kv}", "dve")
            released[load_at[f"cmp{kv}0"]] = ("tile", len(tiles))
            released[load_at[f"cmp{kv}1"]] = ("tile", len(tiles))
        plan("kc", "act")
        plan("vc", "dve")
        for m in range(8):
            plan(f"wo{m}", "dve", f"out{m // 2}", m % 2 == 1)
        UP0 = len(tiles)
        for m in range(32):
            plan(f"up{m}", "act", f"up{m // 2}", m % 2 == 1)
        DOWN0 = len(tiles)
        for i in range(4):
            for q in range(3):
                mid(f"down{i}_{q}")
            plan(f"dn{2 * i}", "dve")
            plan(f"dn{2 * i + 1}", "dve", f"down{i}_3", True)
        for h in range(4):
            plan(f"qr{h}", "dve", f"p{h // 2}", h % 2 == 1)
        for g in range(8):
            plan(f"z{g}", "act", f"p{2 + g // 2}", g % 2 == 1)
        for i in range(4):
            plan(f"v{i}", "act", f"p{6 + i // 2}", i % 2 == 1)
        for h in range(4):
            plan(f"g{h}", "dve", f"p{8 + h // 2}", h % 2 == 1)
        for h in range(4):
            plan(f"qa{h}", "act", f"p{10 + h // 2}", h % 2 == 1)
        plan("ka", "act")
        plan("va", "dve", "p12", True)
        for i in range(4):
            plan(f"gr{2 * i}", "act")
            plan(f"gr{2 * i + 1}", "act", f"gr{i}", True)
            plan(f"ga{2 * i}", "act")
            plan(f"ga{2 * i + 1}", "act", f"ga{i}", True)
            for j in range(2):
                plan(f"rec{2 * i + j}", "dve")
                plan(f"att{2 * i + j}", "dve", f"br{i}", j == 1)
        for m in range(8):
            plan(f"mx{m}", "dve", f"mix{m // 2}", m % 2 == 1)
        for k in range(8):
            plan(f"m{k}", "act")
        for m in range(8):
            plan(f"memk{m}", "act", f"mkv{m // 2}", m % 2 == 1)
        for i in range(4):
            plan(f"memv{i}", "dve", f"mkv{4 + i}", True)
        for m in range(8):
            plan(f"memq{m}", "act", f"mem_q{m // 2}", m % 2 == 1)
        for m in range(8):
            plan(f"memo{m}", "dve", f"mem_o{m // 2}", m % 2 == 1)
        for i in range(11):
            plan(f"g2_{2 * i}", "act")
            plan(f"g2_{2 * i + 1}", "act", f"g2_{i}", True)
            plan(f"u2_{2 * i}", "dve")
            plan(f"u2_{2 * i + 1}", "dve", f"u2_{i}", True)
        for i in range(4):
            for q in range(2):
                mid(f"d2_{i}_{q}")
            plan(f"d2n{2 * i}", "dve")
            plan(f"d2n{2 * i + 1}", "dve", f"d2_{i}_2", True)
        for i in range(8):
            plan(f"o{i}", "act" if i % 2 else "dve")

        def count(who, n):
            return sum(w == who for _, w in tiles[:n])

        def taken(eng, name):
            n = tile_at[name]
            who = tiles[n][1]
            eng.wait_ge(taken_act if who == "act" else taken_dve, count(who, n + 1))

        def open_tile(eng, name):
            n = tile_at[name]
            if n >= 4:
                taken(eng, tiles[n - 4][0])
            return bank[n % 4]

        def filled(eng, name):
            eng.wait_ge(tile_filled, tile_at[name] + 1)
            return bank[tile_at[name] % 4]

        def wait_released(eng, i):
            kind, value = released[i]
            eng.wait_ge(tile_filled if kind == "tile" else slot_mid, value)

        AB, AV, AQ, KCVC, KSKW, KS2, KW2 = 0, 2, 4, 6, 7, 8, 9
        SZ = 10
        CQ, MQ, MK = 10, 12, 16
        SQT, SKT, CKV = 20, 22, 24
        NV, SV, MV = 25, 26, 28
        KCD, MISC = 30, 31
        nv = ar(NV)
        sv = ar(SV, 2).rearrange("p (t c) -> p t c", c=256)
        mv = ar(MV, 2).rearrange("p (t c) -> p t c", c=256)
        gates = small[:, 0:48]
        kcd = ar(KCD)
        vcd = ar(AV)
        blocks = ar(KCVC)
        misc = ar(MISC)
        hidden = misc[:, 0:128].rearrange("p (a n) -> p a n", n=32)
        hid_e = misc[:, 128:192].rearrange("p (a n) -> p a n", n=32)
        kc_raw = misc[:, 192:224]
        kc = misc[:, 224:256]
        vc = misc[:, 256:320]
        nmax = misc[:, 320:324]
        rsum = misc[:, 324:328]
        rinv = misc[:, 328:332]

        norms, norm_at = [], {}

        def add_norm(name, src, lhs, rows, width, n, outs):
            norm_at[name] = len(norms)
            norms.append((src, lhs, rows, width, n, outs))

        for i in range(2):
            add_norm(f"q{i}", [ar(AQ + i)], [blk64], P, S, 64, [(ar(AQ + i), ar(AQ + i), col("qn"), (0, P))])
        lo, hi = slice(0, 64), slice(64, P)
        add_norm("kskw", [ar(KSKW)], [blk64], P, S, 64, [
            (ar(KS2)[lo], ar(KSKW)[lo], col("kn12", 0, lo), (0, 64)),
            (ar(KS2)[hi], ar(KSKW)[lo], col("kn12", 0, lo), (0, 64)),
            (ar(KW2)[lo], ar(KSKW)[hi], col("kn12", 0, hi), (64, P)),
            (ar(KW2)[hi], ar(KSKW)[hi], col("kn12", 0, hi), (64, P))])
        add_norm("cq", [ar(CQ), ar(CQ + 1)[lo]], [ones, ones[lo]], P, S, 192, [
            (ar(CQ), ar(CQ), col("qa"), (0, P)), (ar(CQ + 1)[lo], ar(CQ + 1)[lo], col("qa", 1, lo), (0, 64))])
        add_norm("ckv", [ar(CKV)], [ones], P, S, P, [(ar(CKV), ar(CKV), col("kvn"), (0, P))])
        r96 = slice(0, 96)
        for t, base, gain in (("mq", MQ, "mqn"), ("mk", MK, "mkn")):
            for h in range(4):
                add_norm(f"{t}{h}", [ar(base + h)[r96]], [ones[r96, r96]], 96, S, 96,
                         [(ar(base + h)[r96], ar(base + h)[r96], col(gain, 0, r96), (0, 96))])
        add_norm("kc", [kc_raw[lo, 0:N_CMP]], [ones[lo, 0:64]], 64, N_CMP, 64, [
            (kc[lo, 0:N_CMP], kc_raw[lo, 0:N_CMP], col("kn0", 0, lo), (0, 64)),
            (kc[hi, 0:N_CMP], kc_raw[lo, 0:N_CMP], col("kn0", 0, lo), (0, 64))])
        for g in range(4):
            add_norm(f"y{g}", [yt(2 * g), yt(2 * g + 1)], [ones, ones], P, S, 256,
                     [(yt(2 * g + i), yt(2 * g + i), col("onw", 2 * g + i), (0, P)) for i in range(2)])
        for h in range(4):
            add_norm(f"r{h}", [yt(h)], [ones], P, S, P, [(yt(h), yt(h), col("hgn", h), (0, P))])
        NORM_BANK = (4, 5)

        def norm_squares(eng, name):
            u = norm_at[name]
            src, _, _, w, _, _ = norms[u]
            if u >= 2:
                eng.wait_ge(nrm_ss, u - 1)
            for i, a in enumerate(src):
                r0 = a.shape[0]
                last = nc.scalar.activation(sq[0:r0, (2 * (u % 2) + i) * S:(2 * (u % 2) + i) * S + w], a, ACT.Square)
            last.then_inc(nrm_sq, 1)

        def norm_sums(eng, name):
            u = norm_at[name]
            src, lhs, rows, w, _, _ = norms[u]
            eng.wait_ge(nrm_sq, u + 1)
            if u >= 2:
                eng.wait_ge(nrm_rb, u - 1)
            for i, a in enumerate(src):
                r0 = a.shape[0]
                at = (2 * (u % 2) + i) * S
                last = nc.tensor.matmul(bank[NORM_BANK[u % 2]][0:rows, 0:w], lhs[i], sq[0:r0, at:at + w],
                                        start=i == 0, stop=i == len(src) - 1)
            last.then_inc(nrm_ss, 1)

        def norm_factor(eng, name):
            u = norm_at[name]
            _, _, rows, w, n, _ = norms[u]
            eng.wait_ge(nrm_ss, u + 1)
            if u >= 2:
                eng.wait_ge(nrm_out, u - 1)
            r = rb[0:rows, (u % 2) * S:(u % 2) * S + w]
            link(eng, "act", nc.scalar.activation(r, bank[NORM_BANK[u % 2]][0:rows, 0:w], ACT.Ln,
                                                  bias=eps_col[0:rows], scale=1.0 / n))
            nc.scalar.activation(r, r, ACT.Exp, scale=-0.5).then_inc(nrm_rb, 1)

        def norm_apply(eng, name):
            u = norm_at[name]
            _, _, _, w, _, outs = norms[u]
            eng.wait_ge(nrm_rb, u + 1)
            for o, a, gain, (r0, r1) in outs:
                last = nc.vector.scalar_tensor_tensor(o, a, gain, rb[r0:r1, (u % 2) * S:(u % 2) * S + w],
                                                      ALU.mult, ALU.mult)
            last.then_inc(nrm_out, 1)

        def normed(eng, name):
            eng.wait_ge(nrm_out, norm_at[name] + 1)

        bigs, big_at = [], {}

        def add_big(name, src, dst, gain, w=S):
            big_at[name] = len(bigs)
            bigs.append((src, dst, gain, w))

        add_big("in1", xt, nt, "norm1")
        add_big("ffn1", xt, nt, "norm2")
        def mem_t(k):
            return ar(12, 4)[:, k * 256:(k + 1) * 256]

        add_big("mix", xt, nt, "nmix")
        add_big("memkv", mem_t, mem_t, "nmkv", 256)
        add_big("mem", xt, nt, "nmem")
        add_big("ffn2", xt, nt, "nffn")
        add_big("fin", xt, nt, "fin")
        acc = ctx.enter_context(nc.sbuf_tensor("acc", [P, S], F32))
        eps_t = sb("eps_t", 2)
        eps_col = eps_t[:, 0:1]
        one_col = eps_t[:, 1:2]
        BIG_BANK = 6

        def big_square(eng, name, k):
            b = big_at[name]
            src, _, _, w = bigs[b]
            n = 8 * b + k
            if n >= 2:
                eng.wait_ge(big_add, n - 1)
            nc.scalar.activation(sq[:, (n % 2) * S:(n % 2) * S + w], src(k), ACT.Square).then_inc(big_sq, 1)

        def big_sum(eng, name):
            b = big_at[name]
            w = bigs[b][3]
            for k in range(8):
                n = 8 * b + k
                eng.wait_ge(big_sq, n + 1)
                s_k = sq[:, (n % 2) * S:(n % 2) * S + w]
                if k == 0:
                    if b:
                        eng.wait_ge(big_ss, b)
                    nc.gpsimd.tensor_copy(acc[:, 0:w], s_k).then_inc(big_add, 1)
                else:
                    eng.wait_ge(big_add, n)
                    nc.gpsimd.tensor_tensor(acc[:, 0:w], acc[:, 0:w], s_k, ALU.add).then_inc(big_add, 1)

        def big_total(eng, name):
            b = big_at[name]
            w = bigs[b][3]
            eng.wait_ge(big_add, 8 * b + 8)
            nc.tensor.matmul(bank[BIG_BANK][:, 0:w], ones, acc[:, 0:w], start=True, stop=True).then_inc(big_ss, 1)

        def big_factor(eng, name):
            b = big_at[name]
            w = bigs[b][3]
            eng.wait_ge(big_ss, b + 1)
            link(eng, "act", nc.scalar.activation(rb[:, 0:w], bank[BIG_BANK][:, 0:w], ACT.Ln, bias=eps_col,
                                                  scale=1.0 / D))
            nc.scalar.activation(rb[:, 0:w], rb[:, 0:w], ACT.Exp, scale=-0.5).then_inc(big_rb, 1)

        def big_apply(eng, name):
            b = big_at[name]
            src, dst, gain, w = bigs[b]
            eng.wait_ge(big_rb, b + 1)
            for k in range(8):
                nc.vector.scalar_tensor_tensor(dst(k), src(k), col(gain, k), rb[:, 0:w], ALU.mult, ALU.mult)\
                    .then_inc(big_out, 1)

        def big_ready(eng, name, k):
            eng.wait_ge(big_out, 8 * big_at[name] + k + 1)

        units = []
        for hp in range(2):
            for h in (2 * hp, 2 * hp + 1):
                for qt in range(TT):
                    for kind in ("cmp", "slc", "win"):
                        units.append((kind, h, qt))
        N_NSA = len(units)
        for h in range(4):
            for qt in range(TT):
                units.append(("mla", h, qt))
        N_B1 = len(units)
        for h in range(8):
            for qt in range(TT):
                units.append(("gqa", h, qt))
        N_GQA = len(units)
        for h in range(4):
            for qt in range(TT):
                units.append(("mem", h, qt))
        N_ALL = len(units)
        SCORE_BANK = (0, 1, 2)
        TRANS_BANK = (3, 6)
        OUT_BANK = (5, 7)

        def key_tiles(u):
            kind, h, qt = units[u]
            if kind == "gqa":
                return list(range(max(0, qt - 1), min(TT - 1, qt + 1) + 1))
            if kind == "mem":
                return [0, 1]
            if kind == "cmp":
                return [0]
            return list(range(qt + 1))

        def width(u):
            return N_CMP if units[u][0] == "cmp" else P * len(key_tiles(u))

        def head_rows(h):
            return slice(64 * (h % 2), 64 * (h % 2) + 64)

        def pv_last(u):
            return units[u][0] not in ("cmp", "slc")

        def out_group(u):
            kind, h, qt = units[u]
            return {"cmp": 0, "slc": 0, "win": 0, "mla": 2, "gqa": 6, "mem": 10}[kind] + (
                2 * h if kind == "mem" else h // 2)

        def scores(eng, u):
            kind, h, qt = units[u]
            if u >= 3:
                eng.wait_ge(exp_out, u - 2)
            b = bank[SCORE_BANK[u % 3]]
            w, qs = width(u), slice(qt * P, (qt + 1) * P)
            if kind in ("cmp", "slc", "win"):
                r = head_rows(h)
                keys = {"cmp": kc, "slc": ar(KS2), "win": ar(KW2)}[kind][r, 0:w]
                last = nc.tensor.matmul(b[:, 0:w], ar(AQ + h // 2)[r, qs], keys, start=True, stop=kind != "cmp")
                if kind == "cmp":
                    last = nc.tensor.matmul(b[:, 0:w], cmp_bias[0:N_CMP, h * S + qt * P:h * S + (qt + 1) * P],
                                            ident[0:N_CMP, 0:N_CMP], start=False, stop=True)
            elif kind == "mla":
                last = nc.tensor.matmul(b[:, 0:w], ar(MQ + h)[0:96, qs], ar(MK + h)[0:96, 0:w], start=True, stop=True)
            elif kind == "gqa":
                r, k0 = head_rows(h), key_tiles(u)[0] * P
                last = nc.tensor.matmul(b[:, 0:w], ar(QA + h // 2)[r, qs], ar(KA + h // 4)[r, k0:k0 + w],
                                        start=True, stop=True)
            else:
                for i in range(2):
                    last = nc.tensor.matmul(b[:, 0:w], ar(MEMQ + 2 * h + i)[:, qs], mem_k[:, 2 * h + i, :],
                                            start=i == 0, stop=i == 1)
            last.then_inc(score_mm, 1)

        SCALE = {"cmp": 64 ** -0.5, "slc": 64 ** -0.5, "win": 64 ** -0.5, "mla": 96 ** -0.5, "gqa": 64 ** -0.5,
                 "mem": 256 ** -0.5}

        def prob_of(u):
            return prob[:, (u % 2) * S:(u % 2) * S + width(u)]

        def shift(eng, u):
            kind, h, qt = units[u]
            scale, w = SCALE[kind], width(u)
            b = bank[SCORE_BANK[u % 3]]
            nm = nmax[:, u % 4:u % 4 + 1]
            eng.wait_ge(score_mm, u + 1)
            if u >= 2:
                eng.wait_ge(trans_mm, u - 1)
            if kind in ("cmp", "mem"):
                link(eng, "dve", nc.vector.tensor_reduce(nm, b[:, 0:w], AX_X, ALU.max))
                nc.vector.tensor_scalar(nm, nm, -scale, NO_KEY, ALU.mult, ALU.min).then_inc(score_sh, 1)
                return
            if kind in ("slc", "win"):
                add = strips[:, h * S + (TT - 1 - qt) * P:(h + 1) * S]
            elif kind == "mla":
                add = const("causal")[:, (TT - 1 - qt) * P:S]
            else:
                k0 = (key_tiles(u)[0] - qt + 1) * P
                add = const("band")[:, k0:k0 + w]
            ins = nc.vector.tensor_tensor_reduce(prob_of(u), b[:, 0:w], add, -scale, NO_KEY, ALU.add, ALU.min, nm)
            if kind == "gqa":
                link(eng, "dve", ins)
                ins = nc.vector.tensor_tensor(nm, nm, nsink[:, h:h + 1], ALU.min)
            ins.then_inc(score_sh, 1)

        def exps(eng, u):
            kind, h, qt = units[u]
            b = bank[SCORE_BANK[u % 3]]
            nm, total = nmax[:, u % 4:u % 4 + 1], rsum[:, u % 4:u % 4 + 1]
            eng.wait_ge(score_sh, u + 1)
            if kind in ("cmp", "mem"):
                nc.scalar.activation(prob_of(u), b[:, 0:width(u)], ACT.Exp, bias=nm, scale=SCALE[kind],
                                     accum_out=total).then_inc(exp_out, 1)
                return
            if kind == "gqa":
                nc.scalar.activation(esink[:, u % 4:u % 4 + 1], sink_sb[:, h:h + 1], ACT.Exp, bias=nm)
            nc.scalar.activation(prob_of(u), prob_of(u), ACT.Exp, bias=nm, scale=-1.0,
                                 accum_out=total).then_inc(exp_out, 1)

        def normalise(eng, u):
            kind, h, qt = units[u]
            total, inv = rsum[:, u % 4:u % 4 + 1], rinv[:, u % 4:u % 4 + 1]
            eng.wait_ge(exp_out, u + 1)
            if kind == "cmp":
                link(eng, "dve", nc.vector.tensor_scalar(total, total, 1e-30, None, ALU.max))
            if kind == "gqa":
                link(eng, "dve", nc.vector.tensor_tensor(total, total, esink[:, u % 4:u % 4 + 1], ALU.add))
            link(eng, "dve", nc.vector.reciprocal(inv, total))
            if kind in ("cmp", "slc", "win"):
                g = 12 * qt + 3 * h + ("cmp", "slc", "win").index(kind)
                ins = nc.vector.tensor_scalar(prob_of(u), prob_of(u), inv, gates[:, g:g + 1], ALU.mult, ALU.mult)
            else:
                ins = nc.vector.tensor_scalar(prob_of(u), prob_of(u), inv, None, ALU.mult)
            ins.then_inc(prob_out, 1)

        def turn(eng, u):
            eng.wait_ge(prob_out, u + 1)
            if u >= 2:
                copied(eng, u - 2)
            b = bank[TRANS_BANK[u % 2]]
            p = prob_of(u)
            for i in range(len(key_tiles(u))):
                w = min(P, width(u))
                last = nc.tensor.transpose(b[0:w, i * P:(i + 1) * P], p[:, i * P:i * P + w], ident)
            last.then_inc(trans_mm, 1)

        def copied(eng, u):
            eng.wait_ge(trans_dve if u % 2 else trans_act, u // 2 + 1)

        def copy_turned(eng, u):
            eng.wait_ge(trans_mm, u + 1)
            if u >= 2:
                eng.wait_ge(pv_mm, u - 1)
            r = N_CMP if units[u][0] == "cmp" else P
            w = P * len(key_tiles(u))
            dst, src = prob_t[0:r, (u % 2) * S:(u % 2) * S + w], bank[TRANS_BANK[u % 2]][0:r, 0:w]
            if u % 2:
                nc.vector.tensor_copy(dst, src).then_inc(trans_dve, 1)
            else:
                nc.scalar.activation(dst, src, ACT.Copy).then_inc(trans_act, 1)

        def values(eng, u):
            kind, h, qt = units[u]
            copied(eng, u)
            g = out_group(u)
            if kind == "mem":
                if qt == 0:
                    eng.wait_ge(head_out, g)
                for m in range(2):
                    for i in range(2):
                        last = nc.tensor.matmul(
                            bank[OUT_BANK[m]][:, qt * P:(qt + 1) * P], mem_v[:, i, (2 * h + m) * P:(2 * h + m + 1) * P],
                            prob_t[:, (u % 2) * S + i * P:(u % 2) * S + (i + 1) * P], start=i == 0, stop=i == 1)
                last.then_inc(pv_mm, 1)
                return
            if qt == 0 and h % 2 == 0 and kind in ("cmp", "mla", "gqa") and g >= 2:
                eng.wait_ge(head_out, g - 1)
            o = bank[OUT_BANK[g % 2]][head_rows(h), qt * P:(qt + 1) * P]
            n = len(key_tiles(u))
            for i, kt in enumerate(key_tiles(u)):
                r = N_CMP if kind == "cmp" else P
                if kind == "cmp":
                    v = vc[0:N_CMP, 0:64]
                elif kind in ("slc", "win"):
                    v = nv[:, kt * P + (64 if kind == "win" else 0):kt * P + (64 if kind == "win" else 0) + 64]
                elif kind == "mla":
                    v = mv[:, kt, 64 * h:64 * h + 64]
                else:
                    v = va[:, kt * P + 64 * (h // 4):kt * P + 64 * (h // 4) + 64]
                last = nc.tensor.matmul(o, v, prob_t[0:r, (u % 2) * S + i * P:(u % 2) * S + (i + 1) * P],
                                        start=i == 0 and kind not in ("slc", "win"), stop=i == n - 1 and pv_last(u),
                                        )
            last.then_inc(pv_mm, 1)

        def take_heads(eng, u, dst):
            eng.wait_ge(pv_mm, u + 1)
            g = out_group(u)
            if units[u][0] == "mem":
                for m in range(2):
                    nc.scalar.activation(dst[m], bank[OUT_BANK[m]][:, :], ACT.Copy).then_inc(head_out, 1)
            else:
                nc.scalar.activation(dst, bank[OUT_BANK[g % 2]][:, :], ACT.Copy).then_inc(head_out, 1)

        AHEAD = 2

        def attend_pe(eng, u0, u1):
            for u in range(u0, min(u0 + AHEAD, u1)):
                scores(eng, u)
            for u in range(u0, u1):
                if u + AHEAD < u1:
                    scores(eng, u + AHEAD)
                turn(eng, u)
                if u > u0:
                    values(eng, u - 1)
            values(eng, u1 - 1)

        def attend_act(eng, u0, u1, pair_end):
            for u in range(u0, u1):
                exps(eng, u)
                if u > u0:
                    if (u - 1) % 2 == 0:
                        copy_turned(eng, u - 1)
                    if u - 2 >= u0:
                        pair_end(eng, u - 2)
            if (u1 - 1) % 2 == 0:
                copy_turned(eng, u1 - 1)
            for u in range(max(u0, u1 - 2), u1):
                pair_end(eng, u)

        def attend_dve(eng, u0, u1):
            shift(eng, u0)
            for u in range(u0, u1):
                if u + 1 < u1:
                    shift(eng, u + 1)
                normalise(eng, u)
                if u > u0 and (u - 1) % 2:
                    copy_turned(eng, u - 1)
            if (u1 - 1) % 2:
                copy_turned(eng, u1 - 1)

        def pair_end_b1(eng, u):
            kind, h, qt = units[u]
            if kind in ("win", "mla") and h % 2 == 1 and qt == TT - 1:
                take_heads(eng, u, yt(2 + h // 2 if kind == "win" else 4 + h // 2))

        ST_W = [S - kt * P for kt in range(TT)]
        ST_AT = [0, 512, 896, 1152]

        def stick(h, kt, which):
            at = (SZ * S) + (h % 2) * 2560 + which * 1280 + ST_AT[kt]
            return arena[:, at:at + ST_W[kt]]

        def stick_scores(eng, h):
            for kt in range(TT):
                n = 4 * h + kt
                if n >= 2:
                    eng.wait_ge(sb_zs, n - 1)
                r = head_rows(h)
                nc.tensor.matmul(bank[n % 2][:, 0:ST_W[kt]], ar(SKT + h // 2)[r, kt * P:(kt + 1) * P],
                                 ar(SQT + h // 2)[r, kt * P:S], start=True, stop=True).then_inc(sb_z, 1)

        def stick_sums(eng, h):
            eng.wait_ge(sb_sp, 4 * h + 4)
            for kt in range(TT):
                n = 4 * h + kt
                if n >= 2:
                    eng.wait_ge(sb_t, n - 1)
                b = bank[2 + n % 2]
                last = nc.tensor.matmul(b[:, 0:ST_W[kt]], const("suffix"), stick(h, kt, 1), start=True,
                                        stop=kt == TT - 1)
                for later in range(kt + 1, TT):
                    last = nc.tensor.matmul(b[:, (later - kt) * P:ST_W[kt]], ones, stick(h, later, 1), start=False,
                                            stop=later == TT - 1)
                last.then_inc(sb_c, 1)

        def stick_values(eng, h):
            for kt in range(TT):
                eng.wait_ge(sb_e, 4 * h + kt + 1)
                last = nc.tensor.matmul(bank[OUT_BANK[h // 2]][head_rows(h), kt * P:S],
                                        sv[:, kt, 64 * h:64 * h + 64], stick(h, kt, 0),
                                        start=kt == 0, stop=kt == TT - 1)
            last.then_inc(sb_o, 1)

        def stick_logs(eng, h):
            for kt in range(TT):
                n = 4 * h + kt
                eng.wait_ge(sb_z, n + 1)
                if h >= 2:
                    eng.wait_ge(sb_o, h - 1)
                z, s = stick(h, kt, 0), stick(h, kt, 1)
                nc.scalar.activation(z, bank[n % 2][:, 0:ST_W[kt]], ACT.Copy).then_inc(sb_zs, 1)
                eng.wait_ge(sb_zs, n + 1)
                link(eng, "act", nc.scalar.activation(s, z, ACT.Abs))
                link(eng, "act", nc.scalar.activation(s, s, ACT.Exp, scale=-1.0))
                nc.scalar.activation(s, s, ACT.Ln, bias=one_col).then_inc(sb_l, 1)

        def stick_softplus(eng, h):
            for kt in range(TT):
                n = 4 * h + kt
                eng.wait_ge(sb_l, n + 1)
                z, s = stick(h, kt, 0), stick(h, kt, 1)
                link(eng, "dve", nc.vector.scalar_tensor_tensor(s, z, 0.0, s, ALU.max, ALU.add))
                nc.vector.tensor_tensor(s[:, 0:P], s[:, 0:P], const("strict"), ALU.mult).then_inc(sb_sp, 1)

        def stick_shift(eng, h):
            for kt in range(TT):
                n = 4 * h + kt
                eng.wait_ge(sb_c, n + 1)
                z = stick(h, kt, 0)
                link(eng, "dve", nc.vector.tensor_tensor(z, z, bank[2 + n % 2][:, 0:ST_W[kt]], ALU.subtract))
                nc.vector.tensor_tensor(z[:, 0:P], z[:, 0:P], const("neg_strict"), ALU.add).then_inc(sb_t, 1)

        def stick_exps(eng, h):
            for kt in range(TT):
                n = 4 * h + kt
                eng.wait_ge(sb_t, n + 1)
                nc.scalar.activation(stick(h, kt, 0), stick(h, kt, 0), ACT.Exp).then_inc(sb_e, 1)

        def take_stick(eng, hp):
            eng.wait_ge(sb_o, 2 * hp + 2)
            nc.scalar.activation(yt(6 + hp), bank[OUT_BANK[hp]][:, :], ACT.Copy).then_inc(head_out, 1)

        QH, FG, VR, GR, QA, KA, VA = 0, 4, 12, 16, 20, 24, 26
        K_RAW = 27
        va = ar(VA)
        MEMQ = 0
        mem_tok = ar(8, 4).rearrange("p (t d) -> p t d", d=D)
        mem_k = ar(16, 4).rearrange("p (m s) -> p m s", s=256)
        mem_v = ar(20, 4).rearrange("p (t d) -> p t d", d=D)
        cols2 = sb("cols2", 64)
        low, one_low, low_e = cols2[:, 0:8], cols2[:, 8:16], cols2[:, 16:32]
        low_max, nsink, esink, decay = cols2[:, 32:40], cols2[:, 40:48], cols2[:, 48:52], cols2[:, 52:60]
        pos_i, angle, whole_i, fold = (tile(strips, i) for i in range(4))
        cos16, sin16 = tile(cmp_bias, 0), tile(cmp_bias, 1)
        padded = [ar(22, 3)[:, 520 * i:520 * i + S + 2] for i in range(2)]
        conv_c, conv_e = (ar(25), ar(26)), (ar(27), ar(28))
        trig_dve = sem("trig_dve")
        trig_act = sem("trig_act")
        low_dve = sem("low_dve")
        low_act = sem("low_act")
        qr_exp = sem("qr_exp")
        f_out = sem("f_out")
        g_exp = sem("g_exp")
        turned2 = sem("turned2")
        rope2 = sem("rope2")
        floor_out = sem("floor_out")
        log_out = sem("log_out")
        sum_out = sem("sum_out")
        end_diff = sem("end_diff")
        end_exp = sem("end_exp")
        ends_out = sem("ends_out")
        keys_turned = sem("keys_turned")
        keys_sb = sem("keys_sb")
        update_mm = sem("update_mm")
        states_out = sem("states_out")
        level_diff = sem("level_diff")
        level_exp = sem("level_exp")
        level_in = sem("level_in")
        level_mm = sem("level_mm")
        level_out = sem("level_out")
        rec_mm = sem("rec_mm")
        rec_out = sem("rec_out")
        rec_gated = sem("rec_gated")
        gate_sig = sem("gate_sig")
        merged = sem("merged")
        pads = sem("pads")
        conv2_out = sem("conv2_out")
        conv2_silu = sem("conv2_silu")
        out_done = sem("out_done")

        G_KEY = (ar(27), tile(cmp_bias, 3))
        G_SUM = (ar(28), acc[:, :])
        G_X = (ar(29), ar(30))
        G_END = ar(31)
        G_SCORE = (tile(strips, 0), tile(strips, 1))
        G_QUERY = (tile(strips, 2), tile(strips, 3))
        G_KEYT = tile(cmp_bias, 0)
        G_STATE = (tile(cmp_bias, 1), tile(cmp_bias, 2))
        LEVELS = 7

        def halves(a, n, d):
            w = 1 << n
            v = a.rearrange("p (b w) -> p b w", w=2 * w)
            left, right = v[:, :, 0:w], v[:, :, w:2 * w]
            return (right, left) if d == 0 else (left, right)

        def key_chunk(d, i):
            return i if d == 0 else TT - 1 - i

        def rec_floor(eng, g):
            if g >= 2:
                eng.wait_ge(level_mm, 8 * (g - 1))
            f = ar(FG + 4 * (g % 2) + g // 2)
            nc.vector.tensor_scalar(G_KEY[g % 2], f, -1.0, 1.0, ALU.mult, ALU.add)
            if g >= 2:
                eng.wait_ge(level_diff, 7 * (g - 1))
            nc.vector.tensor_scalar(G_SUM[g % 2], f, 1e-19, None, ALU.max).then_inc(floor_out, 1)

        def rec_log(eng, g):
            eng.wait_ge(floor_out, g + 1)
            nc.scalar.activation(G_SUM[g % 2], G_SUM[g % 2], ACT.Ln).then_inc(log_out, 1)

        def rec_scan(eng, g):
            eng.wait_ge(log_out, g + 1)
            s = G_SUM[g % 2]
            if g % 2 == 0:
                ins = nc.vector.tensor_tensor_scan(s, const("carryf"), s, 0.0, ALU.mult, ALU.add)
            else:
                ins = nc.vector.tensor_tensor_scan(s[:, ::-1], const("carryb")[:, ::-1], s[:, ::-1], 0.0,
                                                   ALU.mult, ALU.add)
            ins.then_inc(sum_out, 1)

        def rec_ends(g):
            return G_SUM[g % 2].rearrange("p (c t) -> p c t", t=P)[:, :, P - 1:P] if g % 2 == 0 else \
                G_SUM[g % 2].rearrange("p (c t) -> p c t", t=P)[:, :, 0:1]

        def rec_end_diff(eng, g):
            eng.wait_ge(sum_out, g + 1)
            if g:
                eng.wait_ge(keys_turned, g)
            nc.gpsimd.tensor_tensor(G_END.rearrange("p (c t) -> p c t", t=P), rec_ends(g).to_broadcast([P, TT, P]),
                                    G_SUM[g % 2].rearrange("p (c t) -> p c t", t=P), ALU.subtract)\
                .then_inc(end_diff, 1)

        def rec_end_exp(eng, g):
            eng.wait_ge(sum_out, g + 1)
            if g >= 2:
                eng.wait_ge(rec_mm, g // 2)
            nc.scalar.activation(G_QUERY[g % 2], G_SUM[g % 2], ACT.Exp)
            eng.wait_ge(end_diff, g + 1)
            nc.scalar.activation(G_END, G_END, ACT.Exp).then_inc(end_exp, 1)

        def rec_end_mul(eng, g):
            eng.wait_ge(end_exp, g + 1)
            q, h = G_QUERY[g % 2], g // 2
            at = P - 1 if g % 2 == 0 else 0
            link(eng, "dve", nc.vector.tensor_copy(
                decay[:, 4 * (g % 2):4 * (g % 2) + 4],
                q.rearrange("p (c t) -> p c t", t=P)[:, :, at:at + 1].rearrange("p c t -> p (c t)")))
            nc.vector.tensor_tensor(q, q, ar(QH + h), ALU.mult)
            nc.vector.tensor_tensor(G_END, G_END, G_KEY[g % 2], ALU.mult).then_inc(ends_out, 1)

        def rec_turn_keys(eng, g):
            eng.wait_ge(ends_out, g + 1)
            if g:
                eng.wait_ge(keys_sb, g)
            for i in range(TT - 1):
                c = key_chunk(g % 2, i)
                last = nc.tensor.transpose(bank[2][:, i * P:(i + 1) * P], G_END[:, c * P:(c + 1) * P], ident)
            last.then_inc(keys_turned, 1)

        def rec_copy_keys(eng, g):
            eng.wait_ge(keys_turned, g + 1)
            if g:
                eng.wait_ge(update_mm, g)
            nc.scalar.activation(G_KEYT[:, 0:3 * P], bank[2][:, 0:3 * P], ACT.Copy).then_inc(keys_sb, 1)

        def rec_updates(eng, g):
            eng.wait_ge(keys_sb, g + 1)
            if g:
                eng.wait_ge(states_out, g)
            h = g // 2
            for i in range(TT - 1):
                c = key_chunk(g % 2, i)
                last = nc.tensor.matmul(bank[3][:, i * P:(i + 1) * P], G_KEYT[:, i * P:(i + 1) * P],
                                        ar(VR + c)[:, h * P:(h + 1) * P], start=True, stop=True)
            last.then_inc(update_mm, 1)

        def rec_states(eng, g):
            eng.wait_ge(update_mm, g + 1)
            if g >= 2:
                eng.wait_ge(rec_mm, g // 2)
            st = G_STATE[g % 2]
            link(eng, "dve", nc.vector.tensor_copy(st[:, 0:P], bank[3][:, 0:P]))
            for i in (1, 2):
                d = 4 * (g % 2) + key_chunk(g % 2, i)
                ins = nc.vector.scalar_tensor_tensor(st[:, i * P:(i + 1) * P], st[:, (i - 1) * P:i * P],
                                                     decay[:, d:d + 1], bank[3][:, i * P:(i + 1) * P],
                                                     ALU.mult, ALU.add)
                if i == 1:
                    link(eng, "dve", ins)
            ins.then_inc(states_out, 1)

        def level_sub(eng, g, n):
            e = LEVELS * g + n
            if n == 0:
                eng.wait_ge(sum_out, g + 1)
            i = 8 * g + n + 1
            if e >= 2:
                eng.wait_ge(level_mm, i - 1 if n >= 2 else i - 2)
            w = 1 << n
            s = G_SUM[g % 2].rearrange("p (b w) -> p b w", w=2 * w)
            mid_at = w - 1 if g % 2 == 0 else w
            nc.gpsimd.tensor_tensor(G_X[e % 2].rearrange("p (b w) -> p b w", w=2 * w), s,
                                    s[:, :, mid_at:mid_at + 1].to_broadcast([P, S // (2 * w), 2 * w]),
                                    ALU.subtract).then_inc(level_diff, 1)

        def level_exps(eng, g, n):
            e = LEVELS * g + n
            eng.wait_ge(level_diff, e + 1)
            for half, sign in zip(halves(G_X[e % 2], n, g % 2), (1.0, -1.0)):
                ins = nc.scalar.activation(half, half, ACT.Exp, scale=sign)
            ins.then_inc(level_exp, 1)

        def level_mul(eng, g, n):
            e = LEVELS * g + n
            eng.wait_ge(level_exp, e + 1)
            for half, by in zip(halves(G_X[e % 2], n, g % 2), (ar(QH + g // 2), G_KEY[g % 2])):
                other = halves(by, n, g % 2)[0 if by is not G_KEY[g % 2] else 1]
                ins = nc.vector.tensor_tensor(half, half, other, ALU.mult)
            ins.then_inc(level_in, 1)

        def level_scores(eng, g, i):
            at = 8 * g + i
            if i:
                eng.wait_ge(level_in, LEVELS * g + i)
            else:
                eng.wait_ge(floor_out, g + 1)
            if at >= 2:
                eng.wait_ge(level_out, at - 1)
            for c in range(TT):
                cs = slice(c * P, (c + 1) * P)
                keys, qs = (G_X[(LEVELS * g + i - 1) % 2],) * 2 if i else (G_KEY[g % 2], ar(QH + g // 2))
                last = nc.tensor.matmul(bank[at % 2][:, cs], keys[:, cs], qs[:, cs], start=True, stop=True)
            last.then_inc(level_mm, 1)

        def level_keep(eng, g, i):
            at = 8 * g + i
            eng.wait_ge(level_mm, at + 1)
            dst = G_SCORE[g % 2].rearrange("p (c t) -> p c t", t=P)
            src = bank[at % 2][:, :].rearrange("p (c t) -> p c t", t=P)
            if i == 0:
                if g >= 2:
                    eng.wait_ge(rec_mm, g // 2)
                ins = nc.vector.tensor_tensor(dst, src, ident.unsqueeze(1).to_broadcast([P, TT, P]), ALU.mult)
            else:
                eng.wait_ge(level_out, at)
                mask = const(f"lv{'fb'[g % 2]}{i - 1}").bitcast(U32).unsqueeze(1).to_broadcast([P, TT, P])
                ins = nc.vector.copy_predicated(dst, mask, src)
            ins.then_inc(level_out, 1)

        def rec_values(eng, h):
            eng.wait_ge(level_out, 16 * h + 16)
            eng.wait_ge(states_out, 2 * h + 2)
            if h >= 2:
                eng.wait_ge(rec_out, h - 1)
            for c in range(TT):
                cs = slice(c * P, (c + 1) * P)
                terms = [(ar(VR + c)[:, h * P:(h + 1) * P], G_SCORE[d][:, cs]) for d in range(2)]
                for d in range(2):
                    i = c - 1 if d == 0 else TT - 2 - c
                    if i >= 0:
                        terms.append((G_STATE[d][:, i * P:(i + 1) * P], G_QUERY[d][:, cs]))
                for n, (a, b) in enumerate(terms):
                    last = nc.tensor.matmul(bank[6 + h % 2][:, cs], a, b, start=n == 0, stop=n == len(terms) - 1)
            last.then_inc(rec_mm, 1)

        x_tok = ar(16, 8).rearrange("p (t d) -> p t d", d=D)
        hot_sb = mix[0:33, 2 * S:2 * S + STRIP + FWD]
        rel_rep = mix[0:33, 6 * S:6 * S + 4 * P].rearrange("b (h p) -> b h p", p=P)
        stage_strip, stage_fwd = prob_t[:, 0:STRIP], prob[0:N_CMP, 0:FWD]

        row_stage = ar(24)[:, 0:2 * P].rearrange("r (g p) -> r g p", p=P)
        column_loads = []

        def rows_of(name, src, i=0, c0=0):
            r = col_at[name] + i
            n, w = src.shape
            column_loads.append((row_stage[r % P:r % P + n, r // P, c0:c0 + w], src))

        def vector(name, v, i=0, c0=0):
            rows_of(name, v.rearrange("(a p) -> a p", a=1), i, c0)

        def by_tile(name, v):
            rows_of(name, v.rearrange("(k p) -> k p", p=P))

        by_tile("norm1", A["norm1_w"][0])
        for j in range(3):
            rows_of("conv_w", A["conv_w"][0, j].rearrange("(k p) -> k p", p=P), 2 * j)
        by_tile("conv_b", A["conv_b"][0])
        for c0 in (0, 64):
            vector("qn", A["nsa_q_norm"][0], 0, c0)
            vector("kn0", A["nsa_k_norm"][0, 0], 0, c0)
            vector("kn12", A["nsa_k_norm"][0, 1 + c0 // 64], 0, c0)
        for kv in range(2):
            rows_of("pos", A["cmp_pos"][0, kv].rearrange("(j a) d -> j (a d)", a=2), 16 * kv)
        vector("qa", A["mla_q_a_norm"][0, 0:P])
        vector("qa", A["mla_q_a_norm"][0, P:192], 1)
        vector("kvn", A["mla_kv_norm"][0])
        vector("mqn", A["mla_q_norm"][0])
        vector("mkn", A["mla_k_norm"][0])
        by_tile("onw", A["out_norm_w"][0])
        by_tile("norm2", A["norm2_w"][0])
        by_tile("nmix", A["norm_mix_2"][0])
        for d in range(2):
            for e in range(2):
                rows_of("lb", A["lower_bounds_2"][d, e].rearrange("(k p) -> k p", p=P), 8 * d + 4 * e)
        by_tile("hgn", A["hg_norm_2"][0])
        by_tile("nmem", A["norm_mem_2"][0])
        by_tile("nmkv", A["norm_mem_kv_2"][0])
        by_tile("nffn", A["norm_ffn_2"][0])
        for j in range(3):
            rows_of("cw2", A["conv_w_2"][0, j].rearrange("(k p) -> k p", p=P), 22 * j)
        by_tile("cb2", A["conv_b_2"][0])
        by_tile("fin", A["final_norm_2"])
        column_loads.append((rel_sb[0:32, :], A["rel_bias"]))
        cw2 = cw2_sb[:, :].rearrange("p (a c) -> p a c", c=64)
        column_loads.append((cw2, A["cmp_w2"][0].rearrange("v (m p) c -> p (v m) c", p=P)))
        column_loads.append((sink_sb[:, :], A["attn_sink_2"].to_broadcast([P, 8])))
        assert all(r.shape[0] + 0 <= P for r, _ in column_loads) and ncol <= 2 * P

        block = ctx.enter_context(nc.Block())

        @block.sync
        def _(eng):
            eng.dma_start(x_tok, A["x"][0].rearrange("(t p) d -> p t d", p=P)).then_inc(x_in, 16)

            def fetch(i):
                if i >= SLOTS:
                    wait_released(eng, i - SLOTS)
                for dst, src in part_list(i):
                    eng.dma_start(dst, src).then_inc(slot_in[i % SLOTS], 16)

            for i in range(len(loads)):
                fetch(i)
            eng.wait_ge(out_done, 16 * 4)

        @block.gpsimd
        def _(eng):
            eng.dma_start(const_sb[:, 0:SHARED + b1_cols], A["consts"][:, 0:SHARED + b1_cols]).then_inc(const_in, 16)
            eng.dma_start(hot_sb, A["hot"]).then_inc(hot_in, 16)
            nc.gpsimd.memset(small[:, 60:62], 0.0)
            big_sum(eng, "in1")
            for h in range(4):
                eng.wait_ge(bias_sb, 2 * h + 2)
                if h:
                    eng.wait_ge(bias_out, 32 * h)
                eng.dma_start(strip_dram[h].rearrange("(p y) -> p y", y=STRIP), stage_strip).then_inc(bias_out, 16)
                eng.dma_start(fwd_dram[h].rearrange("(p y) -> p y", y=FWD), stage_fwd).then_inc(bias_out, 16)
            eng.wait_ge(bias_out, 128)
            for h in range(4):
                eng.dma_start(
                    strips[:, h * S:(h + 1) * S],
                    strip_dram[h, P - 1:P - 1 + P * (STRIP - 1)].rearrange("(p y) -> p y", y=STRIP - 1)[:, 0:S],
                ).then_inc(bias_in, 16)
                eng.dma_start(
                    cmp_bias[0:N_CMP, h * S:(h + 1) * S],
                    fwd_dram[h, 480:480 + N_CMP * (FWD - 16)].rearrange("(p y) -> p y", y=FWD - 16)[:, 0:S],
                ).then_inc(bias_in, 16)
            big_sum(eng, "ffn1")
            eng.wait_ge(tile_filled, tile_at["wo0"] + 1)
            eng.wait_ge(big_out, 16)
            eng.dma_start(const_sb[:, SHARED:SHARED + b2_cols],
                          A["consts"][:, SHARED + b1_cols:SHARED + b1_cols + b2_cols]).then_inc(const2_in, 16)
            eng.dma_start(pos_i.bitcast(I32), A["positions_2"].to_broadcast([P, S])).then_inc(pos_in, 16)
            big_sum(eng, "mix")
            for g in range(8):
                rec_end_diff(eng, g)
                for n in range(LEVELS):
                    level_sub(eng, g, n)
            eng.wait_ge(merged, 8)
            eng.wait_ge(taken_dve, count("dve", tile_at["mx7"] + 1))
            eng.dma_start(mem_tok, A["mem_2"][0].rearrange("(t p) d -> p t d", p=P)).then_inc(mem_in, 16)
            big_sum(eng, "memkv")
            for name in ("mem", "ffn2", "fin"):
                big_sum(eng, name)

        @block.tensor
        def _(eng):
            eng.wait_ge(const_in, 16)
            eng.wait_ge(cols_in, 16 * len(column_loads))
            for g in range(2):
                last = nc.tensor.transpose(bank[7][0:P, g * P:(g + 1) * P], row_stage[:, g, :], ident)
            last.then_inc(cols_turned, 1)
            eng.wait_ge(x_in, 16)
            for k in range(KT):
                b = open_tile(eng, f"x{k}")
                for t in range(TT):
                    last = nc.tensor.transpose(b[:, t * P:(t + 1) * P], x_tok[:, t, k * P:(k + 1) * P], ident)
                last.then_inc(tile_filled, 1)
            big_total(eng, "in1")

            def features(name, load_name, c0, rows=P, big=None, w=S, ks=8, src=nt):
                b = open_tile(eng, name)
                slot_ready(eng, load_name)
                sl = slot(load_name)
                for k in range(ks):
                    if big:
                        big_ready(eng, big, k)
                    last = nc.tensor.matmul(b[0:rows, 0:w], sl[:, k * 256 + c0:k * 256 + c0 + rows], src(k),
                                            start=k == 0, stop=k == ks - 1)
                last.then_inc(tile_filled, 1)

            def tokens(name, load_name, c0, cols, ts, src=nt):
                b = open_tile(eng, name)
                slot_ready(eng, load_name)
                sl = slot(load_name)
                for i, t in enumerate(ts):
                    for k in range(KT):
                        last = nc.tensor.matmul(b[:, i * cols:(i + 1) * cols], src(k)[:, t * P:(t + 1) * P],
                                                sl[:, k * 256 + c0:k * 256 + c0 + cols],
                                                start=k == 0, stop=k == KT - 1)
                last.then_inc(tile_filled, 1)

            def bias_tables(h):
                if h == 0:
                    eng.wait_ge(bias_rep, 1)
                    eng.wait_ge(hot_in, 16)
                for n, (y0, w, rows) in enumerate(((0, 320, P), (320, 320, P), (640, 496, N_CMP), (1136, 496, N_CMP))):
                    if h and n % 2 == 0:
                        eng.wait_ge(bias_sb, 2 * h - 1 + n // 2)
                    if h == 0 and n == 2:
                        eng.wait_ge(big_rb, 1)
                    last = nc.tensor.matmul(bank[4 + n][0:rows, 0:w], rel_rep[:, h, 0:rows], hot_sb[:, y0:y0 + w],
                                            start=True, stop=True)
                    if n % 2:
                        last.then_inc(bias_mm, 1)

            for t in ("a_b", "a_c", "a_u", "n_q"):
                for i in range(2):
                    features(f"{t}{i}", t, P * i, big="in1" if (t, i) == ("a_b", 0) else None)
                bias_tables(("a_b", "a_c", "a_u", "n_q").index(t))
            features("kcvc", "n_k", 0)
            features("kskw", "n_k", P)
            features("cq0", "m_q", 0)
            features("cq1", "m_q", P, 96)
            tokens("gates", "m_q", 224, 12, range(TT))
            eng.wait_ge(bias_sb, 8)
            norm_sums(eng, "q0")
            norm_sums(eng, "q1")
            features("ckv", "m_kv", 0)
            tokens("nv", "m_kv", P, P, range(TT))
            norm_sums(eng, "kskw")
            norm_sums(eng, "cq")
            features("s_q0", "s_q", 0)
            features("s_q1", "s_q", P)
            norm_sums(eng, "ckv")
            features("s_k0", "s_k", 0)
            features("s_k1", "s_k", P)
            tokens("s_v0", "s_v", 0, 256, (0, 1))
            tokens("s_v1", "s_v", 0, 256, (2, 3))

            sl = slot("small")
            slot_ready(eng, "small")
            normed(eng, "ckv")
            for h in range(4):
                b = open_tile(eng, f"mq{h}")
                nc.tensor.matmul(b[0:96, :], sl[:, 96 * h:96 * h + 96], ar(CQ), start=True, stop=False)
                nc.tensor.matmul(b[0:96, :], sl[0:64, 384 + 96 * h:480 + 96 * h], ar(CQ + 1)[0:64], start=False,
                                 stop=True).then_inc(tile_filled, 1)
            for h in range(4):
                b = open_tile(eng, f"mk{h}")
                nc.tensor.matmul(b[0:64, :], sl[:, WKV_AT + P * h:WKV_AT + P * h + 64], ar(CKV), start=True,
                                 stop=True).then_inc(tile_filled, 1)
            taken(eng, "cq1")
            nc.tensor.matmul(bank[7][0:96, :], const("turn96")[64:96, :], ar(CQ + 1)[64:96], start=True,
                             stop=True).then_inc(turned, 1)
            wkv = sl[:, WKV_AT:WKV_AT + S].rearrange("p (h c) -> p h c", c=P)
            for i in range(2):
                b = open_tile(eng, f"mv{i}")
                for j in range(2):
                    t = 2 * i + j
                    last = nc.tensor.matmul(b[:, 256 * j:256 * j + 256], ar(CKV)[:, t * P:(t + 1) * P],
                                            wkv[:, :, 64:P], start=True, stop=True)
                last.then_inc(tile_filled, 1)
            for h in range(4):
                taken(eng, f"mq{h}")
                eng.wait_ge(rope_out, h + 1)
                nc.tensor.matmul(bank[7][0:96, :], const("turn96")[0:96, :], ar(MQ + h)[0:96], start=True,
                                 stop=True).then_inc(turned, 1)
            for kv in range(2):
                b = open_tile(eng, f"hid{kv}")
                eng.wait_ge(blocks_out, kv + 1)
                blk = (blocks, ar(AV + 1))[kv][:, 0:16 * N_CMP].rearrange("p (j n) -> p j n", n=N_CMP)
                slot_ready(eng, f"cmp{kv}0")
                slot_ready(eng, f"cmp{kv}1")
                for m in range(2):
                    for j in range(16):
                        w = slot(f"cmp{kv}{j // 8}")
                        last = nc.tensor.matmul(b[:, 32 * m:32 * m + N_CMP],
                                                w[:, (j % 8) * 256 + m * P:(j % 8) * 256 + (m + 1) * P],
                                                blk[:, j, :], start=j == 0, stop=j == 15)
                last.then_inc(tile_filled, 1)
            for h in range(4):
                norm_sums(eng, f"mq{h}")
            b = open_tile(eng, "kc")
            eng.wait_ge(hid_out, 1)
            for m in range(2):
                last = nc.tensor.matmul(b[0:64, 0:N_CMP], cw2[:, m, :], hidden[:, m, 0:N_CMP], start=m == 0,
                                        stop=m == 1)
            last.then_inc(tile_filled, 1)
            b = open_tile(eng, "vc")
            eng.wait_ge(hid_out, 2)
            for m in range(2):
                last = nc.tensor.matmul(b[0:N_CMP, 0:64], hidden[:, 2 + m, 0:N_CMP], cw2[:, 2 + m, :], start=m == 0,
                                        stop=m == 1)
            last.then_inc(tile_filled, 1)
            for h in range(4):
                norm_sums(eng, f"mk{h}")
            norm_sums(eng, "kc")

            taken(eng, "kc")
            taken(eng, "vc")
            taken(eng, "s_v1")
            eng.wait_ge(gates_out, 1)
            eng.wait_ge(bias_in, 128)
            normed(eng, "kc")
            attend_pe(eng, 0, N_B1)
            eng.wait_ge(head_out, 4)
            stick_scores(eng, 0)
            for h in range(4):
                if h + 1 < 4:
                    stick_scores(eng, h + 1)
                stick_sums(eng, h)
                stick_values(eng, h)
            for g in range(4):
                norm_sums(eng, f"y{g}")
            for m in range(8):
                b = open_tile(eng, f"wo{m}")
                slot_ready(eng, f"out{m // 2}")
                sl = slot(f"out{m // 2}")
                for k in range(KT):
                    normed(eng, f"y{k // 2}")
                    last = nc.tensor.matmul(b[:, :], sl[:, k * 256 + (m % 2) * P:k * 256 + (m % 2) * P + P], yt(k),
                                            start=k == 0, stop=k == KT - 1)
                last.then_inc(tile_filled, 1)
            big_total(eng, "ffn1")
            for m in range(32):
                features(f"up{m}", f"up{m // 2}", (m % 2) * P, big="ffn1" if m == 0 else None)
            for i in range(4):
                bs = [open_tile(eng, f"dn{2 * i + j}") for j in range(2)]
                for q in range(4):
                    slot_ready(eng, f"down{i}_{q}")
                    sl = slot(f"down{i}_{q}")
                    for j in range(2):
                        for k in range(8):
                            if i == 0:
                                taken(eng, f"up{8 * q + k}")
                            last = nc.tensor.matmul(bs[j][:, :], sl[:, k * 256 + j * P:k * 256 + j * P + P],
                                                    ar(8 * q + k), start=q == 0 and k == 0, stop=q == 3 and k == 7)
                        if q == 3:
                            last.then_inc(tile_filled, 1)
                        elif j == 1:
                            last.then_inc(slot_mid, 1)
            big_total(eng, "mix")
            for h in range(4):
                features(f"qr{h}", f"p{h // 2}", (h % 2) * P, big="mix" if h == 0 else None)
            for g in range(8):
                features(f"z{g}", f"p{2 + g // 2}", (g % 2) * P)
            for i in range(4):
                tokens(f"v{i}", f"p{6 + i // 2}", 0, 256, (2 * (i % 2), 2 * (i % 2) + 1))
            for h in range(4):
                features(f"g{h}", f"p{8 + h // 2}", (h % 2) * P)
            eng.wait_ge(const2_in, 16)
            for h in range(4):
                features(f"qa{h}", f"p{10 + h // 2}", (h % 2) * P)
            features("ka", "p12", 0)
            tokens("va", "p12", P, P, range(TT))
            for i in range(5):
                taken(eng, f"qa{i}" if i < 4 else "ka")
                if i:
                    eng.wait_ge(rope2, i)
                nc.tensor.matmul(bank[7][:, :], const("turn16"), ar(QA + i) if i < 4 else ar(K_RAW), start=True,
                                 stop=True).then_inc(turned2, 1)
            taken(eng, "va")
            eng.wait_ge(rope2, 5)
            attend_pe(eng, N_B1, N_GQA)
            eng.wait_ge(head_out, 10)
            for g in range(8):
                for i in range(8):
                    level_scores(eng, g, i)
                    if i == 1:
                        rec_turn_keys(eng, g)
                    if i == 3:
                        rec_updates(eng, g)
                if g % 2:
                    rec_values(eng, g // 2)
            for h in range(4):
                norm_sums(eng, f"r{h}")
            for i in range(4):
                for n in ("gr", "ga"):
                    for j in range(2):
                        features(f"{n}{2 * i + j}", f"{n}{i}", j * P)
                slot_ready(eng, f"br{i}")
                sl = slot(f"br{i}")
                if i == 0:
                    eng.wait_ge(rec_gated, 4)
                for j in range(2):
                    for a, n in enumerate(("rec", "att")):
                        b = open_tile(eng, f"{n}{2 * i + j}")
                        for k in range(4):
                            at = 1024 * a + 256 * k + j * P
                            last = nc.tensor.matmul(b[:, :], sl[:, at:at + P], yt(4 * a + k), start=k == 0,
                                                    stop=k == 3)
                        last.then_inc(tile_filled, 1)
            eng.wait_ge(merged, 8)
            for m in range(8):
                features(f"mx{m}", f"mix{m // 2}", (m % 2) * P, src=lambda k: ar(8 + k))
            eng.wait_ge(mem_in, 16)
            for k in range(8):
                b = open_tile(eng, f"m{k}")
                for t in range(2):
                    last = nc.tensor.transpose(b[:, t * P:(t + 1) * P], mem_tok[:, t, k * P:(k + 1) * P], ident)
                last.then_inc(tile_filled, 1)
            big_total(eng, "memkv")
            for m in range(8):
                features(f"memk{m}", f"mkv{m // 2}", (m % 2) * P, big="memkv" if m == 0 else None, w=256, src=mem_t)
            for i in range(4):
                tokens(f"memv{i}", f"mkv{4 + i}", 0, 256, (0, 1), src=mem_t)
            big_total(eng, "mem")
            for m in range(8):
                features(f"memq{m}", f"mem_q{m // 2}", (m % 2) * P, big="mem" if m == 0 else None)
            taken(eng, "memq7")
            taken(eng, "memv3")
            attend_pe(eng, N_GQA, N_ALL)
            eng.wait_ge(head_out, 18)
            for m in range(8):
                features(f"memo{m}", f"mem_o{m // 2}", (m % 2) * P, src=yt)
            big_total(eng, "ffn2")
            for i in range(11):
                for n in ("g2_", "u2_"):
                    for j in range(2):
                        features(f"{n}{2 * i + j}", f"{n}{i}", j * P, big="ffn2" if (i, n, j) == (0, "g2_", 0) else None)
            for i in range(4):
                bs = [open_tile(eng, f"d2n{2 * i + j}") for j in range(2)]
                for q in range(3):
                    slot_ready(eng, f"d2_{i}_{q}")
                    sl = slot(f"d2_{i}_{q}")
                    n = 8 if q < 2 else 6
                    for j in range(2):
                        for k in range(n):
                            if i == 0:
                                taken(eng, f"u2_{8 * q + k}")
                            last = nc.tensor.matmul(bs[j][:, :], sl[:, k * 256 + j * P:k * 256 + j * P + P],
                                                    ar(8 * q + k), start=q == 0 and k == 0, stop=q == 2 and k == n - 1)
                        if q == 2:
                            last.then_inc(tile_filled, 1)
                        elif j == 1:
                            last.then_inc(slot_mid, 1)
            big_total(eng, "fin")
            for i in range(8):
                b = open_tile(eng, f"o{i}")
                t, half = i // 2, i % 2
                for k in range(4):
                    big_ready(eng, "fin", 4 * half + k)
                    last = nc.tensor.transpose(b[:, k * P:(k + 1) * P], nt(4 * half + k)[:, t * P:(t + 1) * P], ident)
                last.then_inc(tile_filled, 1)

        @block.scalar
        def _(eng):
            nc.scalar.preload_act_table_set("natural_log_exp_and_others")
            eng.wait_ge(cols_zero, 1)
            for dst, src in column_loads:
                eng.dma_start(dst, src).then_inc(cols_in, 16)

            def take(name, dst, rows=P, w=S, func=ACT.Copy, scale=1.0):
                b = filled(eng, name)
                nc.scalar.activation(dst, b[0:rows, 0:w], func, scale=scale).then_inc(taken_act, 1)

            for k in range(KT):
                take(f"x{k}", xt(k))
                taken(eng, f"x{k}")
                big_square(eng, "in1", k)
            eng.wait_ge(bias_rep, 1)
            big_factor(eng, "in1")
            for i in range(2):
                take(f"a_b{i}", ar(AB + i))
            for i in range(2):
                take(f"a_c{i}", ar(AV + i))
            for i in range(2):
                take(f"n_q{i}", ar(AQ + i))
            b = filled(eng, "kcvc")
            eng.wait_ge(conv_v, 2)
            nc.scalar.activation(kcd[0:64, :], b[0:64, :], ACT.Copy)
            nc.scalar.activation(kcd[64:P, 0:S - 1], b[0:64, 1:S], ACT.Copy)
            nc.scalar.activation(vcd[0:64, :], b[64:P, :], ACT.Copy)
            nc.scalar.activation(vcd[64:P, 0:S - 1], b[64:P, 1:S], ACT.Copy).then_inc(taken_act, 1)
            take("kskw", ar(KSKW))
            taken(eng, "kskw")
            norm_squares(eng, "q0")
            norm_squares(eng, "q1")
            take("cq0", ar(CQ))
            take("cq1", ar(CQ + 1)[0:96], 96)
            take("gates", gates, P, 48, ACT.Exp, -1.0)
            norm_factor(eng, "q0")
            norm_squares(eng, "kskw")
            norm_factor(eng, "q1")
            take("ckv", ar(CKV))
            taken(eng, "ckv")
            norm_squares(eng, "cq")
            norm_factor(eng, "kskw")
            take("s_q0", ar(SQT), scale=0.125)
            take("s_q1", ar(SQT + 1), scale=0.125)
            norm_squares(eng, "ckv")
            norm_factor(eng, "cq")
            take("s_k0", ar(SKT))
            norm_factor(eng, "ckv")
            take("s_k1", ar(SKT + 1))
            for h in range(4):
                take(f"mq{h}", ar(MQ + h)[0:96], 96)
            for h in range(4):
                take(f"mk{h}", ar(MK + h)[0:64], 64)
            for kv in range(2):
                b = filled(eng, f"hid{kv}")
                if kv:
                    eng.wait_ge(hid_out, 1)
                nc.scalar.activation(hid_e[:, :, 0:N_CMP], b[:, 0:64].rearrange("p (a n) -> p a n", n=32)[:, :, 0:N_CMP],
                                     ACT.Exp, scale=-1.0).then_inc(hid_exp, 1)
            for h in range(4):
                eng.wait_ge(rope_out, h + 2)
                norm_squares(eng, f"mq{h}")
                if h:
                    norm_factor(eng, f"mq{h - 1}")
            take("kc", kc_raw[0:64, 0:N_CMP], 64, N_CMP)
            taken(eng, "kc")
            for h in range(4):
                norm_squares(eng, f"mk{h}")
                norm_factor(eng, f"mk{h - 1}" if h else "mq3")
            norm_squares(eng, "kc")
            norm_factor(eng, "mk3")
            norm_factor(eng, "kc")
            attend_act(eng, 0, N_B1, pair_end_b1)
            stick_logs(eng, 0)
            for h in range(4):
                if h + 1 < 4:
                    stick_logs(eng, h + 1)
                stick_exps(eng, h)
                if h % 2:
                    take_stick(eng, h // 2)
            eng.wait_ge(head_out, 6)
            eng.wait_ge(conv_v, 4)
            for g in range(4):
                norm_squares(eng, f"y{g}")
                if g:
                    norm_factor(eng, f"y{g - 1}")
            norm_factor(eng, "y3")
            for k in range(KT):
                taken(eng, f"wo{k}")
                big_square(eng, "ffn1", k)
            big_factor(eng, "ffn1")

            for m in range(32):
                b = filled(eng, f"up{m}")
                link(eng, "act", nc.scalar.activation(ar(m), b[:, :], ACT.Relu))
                nc.scalar.activation(ar(m), ar(m), ACT.Square).then_inc(taken_act, 1)
            nc.scalar.preload_act_table_set("silu_and_others")
            for i in range(2):
                t = (sin16, cos16)[i]
                eng.wait_ge(trig_dve, i + 1)
                nc.scalar.activation(t, t, ACT.Sin).then_inc(trig_act, 1)
            nc.scalar.preload_act_table_set("natural_log_exp_and_others")
            eng.wait_ge(low_dve, 1)
            nc.scalar.activation(low_e, low_e, ACT.Exp).then_inc(low_act, 1)

            def big_norm(name, tile_name):
                for k in range(KT):
                    taken(eng, f"{tile_name}{k}")
                    big_square(eng, name, k)
                big_factor(eng, name)

            big_norm("mix", "dn")
            for h in range(4):
                b = filled(eng, f"qr{h}")
                nc.scalar.activation(ar(QH + h), b[:, :], ACT.Exp, scale=-1.0).then_inc(qr_exp, 1)
            for g in range(8):
                take(f"z{g}", ar(FG + g), func=ACT.Exp, scale=-1.0)
            for i in range(4):
                b = filled(eng, f"v{i}")
                dst = ar(VR, 4).rearrange("p (t d) -> p t d", d=S)[:, 2 * (i % 2):2 * (i % 2) + 2,
                                                                  256 * (i // 2):256 * (i // 2) + 256]
                nc.scalar.activation(dst, b[:, :].rearrange("p (t d) -> p t d", d=256), ACT.Copy)\
                    .then_inc(taken_act, 1)
            for h in range(4):
                b = filled(eng, f"g{h}")
                nc.scalar.activation(ar(GR + h), b[:, :], ACT.Exp, scale=-1.0).then_inc(g_exp, 1)
            for h in range(4):
                take(f"qa{h}", ar(QA + h))
            take("ka", ar(K_RAW))

            def pair_end_gqa(eng, u):
                _, h, qt = units[u]
                if h % 2 == 1 and qt == TT - 1:
                    take_heads(eng, u, yt(4 + h // 2))

            attend_act(eng, N_B1, N_GQA, pair_end_gqa)
            rec_log(eng, 0)
            for g in range(8):
                rec_end_exp(eng, g)
                for n in range(LEVELS):
                    level_exps(eng, g, n)
                    if n == 1:
                        rec_copy_keys(eng, g)
                    if n == 3 and g + 1 < 8:
                        rec_log(eng, g + 1)
                if g % 2:
                    eng.wait_ge(rec_mm, g // 2 + 1)
                    nc.scalar.activation(yt(g // 2), bank[6 + (g // 2) % 2][:, :], ACT.Copy).then_inc(rec_out, 1)
            for h in range(4):
                eng.wait_ge(rec_out, h + 1)
                norm_squares(eng, f"r{h}")
                if h:
                    norm_factor(eng, f"r{h - 1}")
            norm_factor(eng, "r3")
            for i in range(4):
                for j in range(4):
                    n = f"{('gr', 'ga')[j // 2]}{2 * i + j % 2}"
                    if i:
                        eng.wait_ge(merged, 2 * i)
                    take(n, ar(4 + j), func=ACT.Exp, scale=-1.0)
            for k in range(8):
                take(f"m{k}", mem_t(k), w=256)
                taken(eng, f"m{k}")
                big_square(eng, "memkv", k)
            big_factor(eng, "memkv")
            for m in range(8):
                take(f"memk{m}", mem_k[:, m, :], w=256)
            big_norm("mem", "mx")
            for m in range(8):
                take(f"memq{m}", ar(MEMQ + m))

            def pair_end_mem(eng, u):
                _, h, qt = units[u]
                if qt == TT - 1:
                    take_heads(eng, u, [yt(2 * h), yt(2 * h + 1)])

            attend_act(eng, N_GQA, N_ALL, pair_end_mem)
            big_norm("ffn2", "memo")
            nc.scalar.preload_act_table_set("silu_and_others")
            eng.wait_ge(pads, 1)
            for m in range(22):
                b = filled(eng, f"g2_{m}")
                if m >= 2:
                    eng.wait_ge(conv2_out, m - 1)
                nc.scalar.activation(padded[m % 2][:, 1:S + 1], b[:, :], ACT.Copy).then_inc(taken_act, 1)
                if m % 2:
                    for i in (m - 1, m):
                        eng.wait_ge(conv2_out, i + 1)
                        if i >= 2:
                            taken(eng, f"u2_{i - 2}")
                        nc.scalar.activation(conv_e[i % 2], conv_c[i % 2], ACT.Silu).then_inc(conv2_silu, 1)
            nc.scalar.preload_act_table_set("natural_log_exp_and_others")
            big_norm("fin", "d2n")
            for i in range(1, 8, 2):
                take(f"o{i}", ar(i))
            for t in range(4):
                taken(eng, f"o{2 * t}")
                taken(eng, f"o{2 * t + 1}")
                eng.dma_start(out[0, t * P:(t + 1) * P, :], ar(2 * t, 2)).then_inc(out_done, 16)

        @block.vector
        def _(eng):
            nc.vector.memset(eps_col, EPS)
            nc.vector.memset(rel_rep[32:33], MASKED)
            nc.vector.memset(one_col, 1.0)
            nc.vector.memset(ar(24)[:, 0:2 * P], 0.0).then_inc(cols_zero, 1)
            eng.wait_ge(cols_turned, 1)
            nc.vector.tensor_copy(col_sb[:, :], bank[7][:, 0:ncol]).then_inc(cols_out, 1)
            eng.wait_ge(const_in, 16)
            for h in range(4):
                last = nc.vector.tensor_scalar(rel_rep[0:32, h, :], ones[0:32], rel_sb[0:32, h:h + 1], 8.0,
                                               ALU.mult, ALU.mult)
            last.then_inc(bias_rep, 1)
            eng.wait_ge(cols_out, 1)
            big_apply(eng, "in1")

            def take(name, dst, rows=P, w=S):
                b = filled(eng, name)
                nc.vector.tensor_copy(dst, b[0:rows, 0:w]).then_inc(taken_dve, 1)

            def take_bias(h):
                eng.wait_ge(bias_mm, 2 * h + 1)
                if h:
                    eng.wait_ge(bias_out, 32 * h)
                nc.vector.tensor_copy(stage_strip[:, 0:320], bank[4][:, 0:320])
                nc.vector.tensor_copy(stage_strip[:, 320:640], bank[5][:, 0:320]).then_inc(bias_sb, 1)
                eng.wait_ge(bias_mm, 2 * h + 2)
                nc.vector.tensor_copy(stage_fwd[:, 0:496], bank[6][0:N_CMP, 0:496])
                nc.vector.tensor_copy(stage_fwd[:, 496:992], bank[7][0:N_CMP, 0:496]).then_inc(bias_sb, 1)

            take_bias(0)
            take_bias(1)
            for i in range(2):
                b = filled(eng, f"a_u{i}")
                taken(eng, f"a_c{i}")
                v, y = ar(AV + i), yt(i)
                nc.vector.tensor_tensor(v, v, b[:, :], ALU.mult).then_inc(taken_dve, 1)
                taken(eng, f"a_u{i}")
                link(eng, "dve", nc.vector.tensor_scalar(y, v, col("conv_w", 4 + i), col("conv_b", i),
                                                         ALU.mult, ALU.add))
                link(eng, "dve", nc.vector.scalar_tensor_tensor(y[:, 1:S], v[:, 0:S - 1], col("conv_w", 2 + i),
                                                                y[:, 1:S], ALU.mult, ALU.add))
                nc.vector.scalar_tensor_tensor(y[:, 2:S], v[:, 0:S - 2], col("conv_w", i),
                                               y[:, 2:S], ALU.mult, ALU.add).then_inc(conv_v, 1)
            eng.wait_ge(conv_v, 2)
            for i in range(2):
                nc.vector.tensor_tensor(yt(i), yt(i), ar(AB + i), ALU.mult).then_inc(conv_v, 1)
            take_bias(2)
            take_bias(3)
            norm_apply(eng, "q0")
            taken(eng, "gates")
            link(eng, "dve", nc.vector.tensor_scalar(gates, gates, 1.0, None, ALU.add))
            nc.vector.reciprocal(gates, gates).then_inc(gates_out, 1)
            norm_apply(eng, "q1")
            take("nv", nv)
            norm_apply(eng, "kskw")
            norm_apply(eng, "cq")
            norm_apply(eng, "ckv")
            for i in range(2):
                take(f"s_v{i}", ar(SV + i))

            taken(eng, "kcvc")
            for kv in range(2):
                src = (kcd, vcd)[kv].rearrange("p (n l) -> p l n", l=16)
                dst = (blocks, ar(AV + 1))[kv][:, 0:16 * N_CMP].rearrange("p (j n) -> p j n", n=N_CMP)
                pos = col_sb[:, col_at["pos"] + 16 * kv:col_at["pos"] + 16 * kv + 16].unsqueeze(2)
                for half in range(2):
                    js = slice(8 * half, 8 * half + 8)
                    last = nc.vector.tensor_tensor(dst[:, js, :], src[:, 0:16:2, half:half + N_CMP],
                                                   pos[:, js, :].to_broadcast([P, 8, N_CMP]), ALU.add)
                last.then_inc(blocks_out, 1)

            def rope(r, src, dsts, rows, t):
                eng.wait_ge(turned, r + 1)
                t1, t2 = prob[rows, 0:S], prob[rows, S:2 * S]
                nc.vector.tensor_tensor(t1, src[rows], const("cos96")[rows], ALU.mult)
                link(eng, "dve", nc.vector.tensor_tensor(t2, bank[7][rows, :], const("sin96")[rows], ALU.mult))
                for d in dsts:
                    last = nc.vector.tensor_tensor(d[rows], t1, t2, ALU.add)
                last.then_inc(rope_out, 1)

            eng.wait_ge(bias_out, 128)
            taken(eng, "cq1")
            rope(0, ar(CQ + 1), [ar(MK + h) for h in range(4)], slice(64, 96), None)
            for i in range(2):
                take(f"mv{i}", ar(MV + i))
            for h in range(4):
                rope(h + 1, ar(MQ + h), [ar(MQ + h)], slice(0, 96), None)
            for kv in range(2):
                b = filled(eng, f"hid{kv}")
                eng.wait_ge(hid_exp, kv + 1)
                e = hid_e[:, :, 0:N_CMP]
                link(eng, "dve", nc.vector.tensor_scalar(e, e, 1.0, None, ALU.add))
                link(eng, "dve", nc.vector.reciprocal(e, e))
                nc.vector.tensor_tensor(hidden[:, 2 * kv:2 * kv + 2, 0:N_CMP],
                                        b[:, 0:64].rearrange("p (a n) -> p a n", n=32)[:, :, 0:N_CMP], e,
                                        ALU.mult).then_inc(taken_dve, 1)
                taken(eng, f"hid{kv}")
                nc.vector.tensor_copy(small[:, 60:61], e[:, 0, 0:1]).then_inc(hid_out, 1)
            for h in range(4):
                norm_apply(eng, f"mq{h}")
            take("vc", vc[0:N_CMP], N_CMP, 64)
            for h in range(4):
                norm_apply(eng, f"mk{h}")
            norm_apply(eng, "kc")
            attend_dve(eng, 0, N_B1)
            stick_softplus(eng, 0)
            for h in range(4):
                if h + 1 < 4:
                    stick_softplus(eng, h + 1)
                stick_shift(eng, h)
            for g in range(4):
                norm_apply(eng, f"y{g}")

            def add_to_residual(name, k):
                b = filled(eng, name)
                nc.vector.tensor_tensor(xt(k), xt(k), b[:, :], ALU.add).then_inc(taken_dve, 1)

            for k in range(KT):
                add_to_residual(f"wo{k}", k)
            big_apply(eng, "ffn1")
            for k in range(KT):
                add_to_residual(f"dn{k}", k)
            TURN = 2 * math.pi
            C1 = 6.28125
            C2 = float(np.float32(0.0019350051879882812))
            C3 = TURN - C1 - C2
            eng.wait_ge(pos_in, 16)
            eng.wait_ge(const2_in, 16)
            dve = nc.vector
            link(eng, "dve", dve.tensor_copy(angle, pos_i.bitcast(I32)))
            link(eng, "dve", dve.tensor_scalar(angle, angle, const("rate"), None, ALU.mult))
            link(eng, "dve", dve.tensor_scalar(whole_i.bitcast(I32), angle, 1 / TURN, None, ALU.mult))
            link(eng, "dve", dve.tensor_copy(fold, whole_i.bitcast(I32)))
            for c in (C1, C2, C3):
                link(eng, "dve", dve.scalar_tensor_tensor(angle, fold, -c, angle, ALU.mult, ALU.add))
            for i, t in enumerate((sin16, cos16)):
                link(eng, "dve", dve.tensor_scalar(t, angle, math.pi / 2 * i, None, ALU.add))
                for _ in range(2):
                    link(eng, "dve", dve.tensor_scalar(fold, t, math.pi, -TURN, ALU.is_gt, ALU.mult))
                    link(eng, "dve", dve.tensor_tensor(t, t, fold, ALU.add))
                    link(eng, "dve", dve.tensor_scalar(fold, t, -math.pi, TURN, ALU.is_lt, ALU.mult))
                    link(eng, "dve", dve.tensor_tensor(t, t, fold, ALU.add))
                pi = float(np.nextafter(np.float32(math.pi), np.float32(0)))
                dve.tensor_scalar(t, t, pi, -pi, ALU.min, ALU.max).then_inc(trig_dve, 1)
            lb = col_sb[:, col_at["lb"]:col_at["lb"] + 16].rearrange("p (d e h) -> p d e h", e=2, h=4)
            e = low_e.rearrange("p (d e h) -> p d e h", e=2, h=4)
            mx = low_max.rearrange("p (d h) -> p d h", h=4)
            link(eng, "dve", dve.tensor_tensor(mx, lb[:, :, 0, :], lb[:, :, 1, :], ALU.max))
            dve.tensor_tensor(e[:, :, 0, :], lb[:, :, 0, :], mx, ALU.subtract)
            dve.tensor_tensor(e[:, :, 1, :], lb[:, :, 1, :], mx, ALU.subtract).then_inc(low_dve, 1)
            eng.wait_ge(low_act, 1)
            link(eng, "dve", dve.tensor_tensor(mx, e[:, :, 0, :], e[:, :, 1, :], ALU.add))
            link(eng, "dve", dve.reciprocal(low_max, low_max))
            link(eng, "dve", dve.tensor_tensor(low.rearrange("p (d h) -> p d h", h=4), mx, e[:, :, 0, :], ALU.mult))
            link(eng, "dve", dve.tensor_scalar(one_low, low, -1.0, 1.0, ALU.mult, ALU.add))
            link(eng, "dve", dve.tensor_scalar(nsink, sink_sb[:, :], -1.0, None, ALU.mult))

            big_apply(eng, "mix")
            for h in range(4):
                b = filled(eng, f"qr{h}")
                eng.wait_ge(qr_exp, h + 1)
                q = ar(QH + h)
                link(eng, "dve", dve.tensor_scalar(q, q, 1.0, None, ALU.add))
                link(eng, "dve", dve.reciprocal(q, q))
                dve.scalar_tensor_tensor(q, b[:, :], P ** -0.5, q, ALU.mult, ALU.mult).then_inc(taken_dve, 1)
            for g in range(8):
                taken(eng, f"z{g}")
                f = ar(FG + g)
                link(eng, "dve", dve.tensor_scalar(f, f, 1.0, None, ALU.add))
                link(eng, "dve", dve.reciprocal(f, f))
                dve.tensor_scalar(f, f, one_low[:, g:g + 1], low[:, g:g + 1], ALU.mult, ALU.add).then_inc(f_out, 1)
            for h in range(4):
                b = filled(eng, f"g{h}")
                eng.wait_ge(g_exp, h + 1)
                q = ar(GR + h)
                link(eng, "dve", dve.tensor_scalar(q, q, 1.0, None, ALU.add))
                link(eng, "dve", dve.reciprocal(q, q))
                dve.tensor_tensor(q, b[:, :], q, ALU.mult).then_inc(taken_dve, 1)
            take("va", ar(VA))
            eng.wait_ge(trig_act, 2)
            for i in range(5):
                taken(eng, f"qa{i}" if i < 4 else "ka")
                eng.wait_ge(turned2, i + 1)
                if i:
                    eng.wait_ge(rope2, i)
                src = ar(QA + i) if i < 4 else ar(K_RAW)
                t1, t2 = prob[:, 0:S], prob[:, S:2 * S]
                dve.tensor_tensor(t1, src, cos16, ALU.mult)
                link(eng, "dve", dve.tensor_tensor(t2, bank[7][:, :], sin16, ALU.mult))
                lo, hi = slice(0, 64), slice(64, P)
                outs = [(src, slice(0, P))] if i < 4 else [
                    (ar(KA)[lo], lo), (ar(KA)[hi], lo), (ar(KA + 1)[lo], hi), (ar(KA + 1)[hi], hi)]
                for o, r in outs:
                    last = dve.tensor_tensor(o, t1[r], t2[r], ALU.add)
                last.then_inc(rope2, 1)
            eng.wait_ge(f_out, 8)
            attend_dve(eng, N_B1, N_GQA)
            rec_floor(eng, 0)
            rec_scan(eng, 0)
            for g in range(8):
                rec_end_mul(eng, g)
                level_keep(eng, g, 0)
                for n in range(LEVELS):
                    level_mul(eng, g, n)
                    if n:
                        level_keep(eng, g, n)
                    if n == 3:
                        rec_states(eng, g)
                        if g + 1 < 8:
                            rec_floor(eng, g + 1)
                    if n == 5 and g + 1 < 8:
                        rec_scan(eng, g + 1)
                level_keep(eng, g, LEVELS)
            for h in range(4):
                norm_apply(eng, f"r{h}")
                normed(eng, f"r{h}")
                dve.tensor_tensor(yt(h), yt(h), ar(GR + h), ALU.mult).then_inc(rec_gated, 1)
            for i in range(4):
                for j in range(4):
                    taken(eng, f"{('gr', 'ga')[j // 2]}{2 * i + j % 2}")
                    s = ar(4 + j)
                    link(eng, "dve", dve.tensor_scalar(s, s, 1.0, None, ALU.add))
                    link(eng, "dve", dve.reciprocal(s, s))
                for j in range(2):
                    m = 2 * i + j
                    b = filled(eng, f"rec{m}")
                    dve.tensor_tensor(ar(8 + m), b[:, :], ar(4 + j), ALU.mult).then_inc(taken_dve, 1)
                    b = filled(eng, f"att{m}")
                    dve.tensor_tensor(ar(6 + j), b[:, :], ar(6 + j), ALU.mult).then_inc(taken_dve, 1)
                    taken(eng, f"att{m}")
                    dve.tensor_tensor(ar(8 + m), ar(8 + m), ar(6 + j), ALU.add).then_inc(merged, 1)
            for k in range(8):
                add_to_residual(f"mx{k}", k)
            big_apply(eng, "memkv")
            for i in range(4):
                b = filled(eng, f"memv{i}")
                dve.tensor_copy(mem_v[:, :, 256 * i:256 * i + 256], b[:, :].rearrange("p (t d) -> p t d", d=256))\
                    .then_inc(taken_dve, 1)
            big_apply(eng, "mem")
            attend_dve(eng, N_GQA, N_ALL)
            for k in range(8):
                add_to_residual(f"memo{k}", k)
            for p in padded:
                dve.memset(p[:, 0:1], 0.0)
                last = dve.memset(p[:, S + 1:S + 2], 0.0)
            last.then_inc(pads, 1)
            big_apply(eng, "ffn2")

            def conv2(m):
                taken(eng, f"g2_{m}")
                g, c = padded[m % 2], conv_c[m % 2]
                w = [col("cw2", 22 * j + m) for j in range(3)]
                link(eng, "dve", dve.tensor_scalar(c, g[:, 0:S], w[0], col("cb2", m), ALU.mult, ALU.add))
                link(eng, "dve", dve.scalar_tensor_tensor(c, g[:, 1:S + 1], w[1], c, ALU.mult, ALU.add))
                dve.scalar_tensor_tensor(c, g[:, 2:S + 2], w[2], c, ALU.mult, ALU.add).then_inc(conv2_out, 1)

            for i in range(11):
                for m in (2 * i, 2 * i + 1):
                    conv2(m)
                for m in (2 * i, 2 * i + 1):
                    x = conv_e[m % 2]
                    eng.wait_ge(conv2_silu, m + 1)
                    b = filled(eng, f"u2_{m}")
                    dve.tensor_tensor(ar(m), x, b[:, :], ALU.mult).then_inc(taken_dve, 1)
            for k in range(8):
                add_to_residual(f"d2n{k}", k)
            big_apply(eng, "fin")
            for i in range(0, 8, 2):
                take(f"o{i}", ar(i))


_NAMES = [
    "x", "rel_bias", "norm1_w", "w_in", "conv_w", "conv_b", "nsa_q_norm", "nsa_k_norm", "cmp_pos", "cmp_w1", "cmp_w2",
    "mla_q_a_norm", "mla_kv_norm", "mla_wq_b", "mla_wkv_b", "mla_q_norm", "mla_k_norm", "out_norm_w", "w_out",
    "norm2_w", "ffn_w1", "ffn_w2", "mem_2", "positions_2", "norm_mix_2", "w_in_2", "lower_bounds_2", "hg_norm_2",
    "attn_sink_2", "w_br_rec_2", "w_br_att_2", "w_mix_out_2", "norm_mem_2", "norm_mem_kv_2", "w_mem_q_2",
    "w_mem_kv_2", "w_mem_o_2", "norm_ffn_2", "w_up_2", "conv_w_2", "conv_b_2", "w_down_2", "final_norm_2",
]


def kernel(**inputs):
    import concourse.bacc as bacc
    from concourse.bass_utils import run_bass_kernel_spmd

    nc = bacc.Bacc("TRN2", target_bir_lowering=False, num_devices=1)
    table, _, hot = make_consts()
    arrays = {f"in_{n}": np.ascontiguousarray(inputs[n]) for n in _NAMES}
    arrays["in_consts"], arrays["in_hot"] = table, hot
    aps = {n[3:]: nc.dram_tensor(n, a.shape, mybir.dt.from_np(a.dtype), kind="ExternalInput").ap()
           for n, a in arrays.items()}
    out = nc.dram_tensor("out", (1, S, D), F32, kind="ExternalOutput").ap()
    two_blocks(nc, aps, out)
    r = run_bass_kernel_spmd(nc, [arrays], core_ids=[0])
    return r.results[0]["out"]
```

```python
import math
from contextlib import ExitStack

import numpy as np

import concourse.bass as bass
from concourse import mybir

ALU = mybir.AluOpType
ACT = mybir.ActivationFunctionType
AX_X = mybir.AxisListType.X
F32 = mybir.dt.float32
F32R = mybir.dt.float32r
I32 = mybir.dt.int32
U32 = mybir.dt.uint32

P = 128
S = 512
D = 1024
TT = S // P
KT = D // P
EPS = 1e-6
MASKED = -1e30
NO_KEY = 1e28

SLOTS = 3
SLOT = 2048
PAIRS = 2
PART = 1024

N_CMP = 31
STRIP = 640
FWD = 992


def bucket(dist):
    d = max(dist, 0)
    if d < 16:
        return d
    return min(16 + int(math.log(d / 16) / math.log(128 / 16) * 16), 31)


def make_consts():
    parts = {}
    eye = np.eye(P, dtype=np.float32)
    parts["ident"] = eye
    parts["ones"] = np.ones((P, P), np.float32)
    parts["blk64"] = np.kron(np.eye(2), np.ones((64, 64))).astype(np.float32)
    row, col = np.arange(P)[:, None], np.arange(P)[None, :]
    parts["suffix"] = (row >= col).astype(np.float32)
    parts["strict"] = (row < col).astype(np.float32)
    parts["neg_strict"] = np.where(row < col, 0, MASKED).astype(np.float32)
    j = np.arange(S)[None, :]
    parts["causal"] = np.where(j <= row + (S - P), 0, MASKED).astype(np.float32)
    turn = np.zeros((P, P), np.float32)
    for i in range(16):
        turn[80 + i, 64 + i] = -1
        turn[64 + i, 80 + i] = 1
    parts["turn96"] = turn[:, :96]
    inv = 1.0 / (10000.0 ** (np.arange(0, 32, 2, dtype=np.float32) / np.float32(32)))
    ang = np.arange(S, dtype=np.float32)[:, None] * inv[None, :].astype(np.float32)
    cos96, sin96 = np.ones((P, S), np.float32), np.zeros((P, S), np.float32)
    cos96[64:96] = np.tile(np.cos(ang).T, (2, 1))
    sin96[64:96] = np.tile(np.sin(ang).T, (2, 1))
    parts["cos96"], parts["sin96"] = cos96, sin96
    j = np.arange(3 * P)[None, :] - P
    parts["band"] = np.where(np.abs(j - row) <= P, 0, MASKED).astype(np.float32)
    turn = np.zeros((P, P), np.float32)
    inv2 = (1.0 / (500000.0 ** (np.arange(0, 16, 2, dtype=np.float32) / np.float32(16)))).astype(np.float32)
    rate = np.zeros((P, 1), np.float32)
    for b in (0, 64):
        for i in range(8):
            turn[b + 8 + i, b + i] = -1
            turn[b + i, b + 8 + i] = 1
            rate[b + i] = rate[b + 8 + i] = inv2[i]
    parts["turn16"] = turn
    parts["rate"] = rate
    for n in range(7):
        w = 1 << n
        same = (row // (2 * w)) == (col // (2 * w))
        parts[f"lvf{n}"] = (same & (row % (2 * w) < w) & (col % (2 * w) >= w)).astype(np.float32)
        parts[f"lvb{n}"] = (same & (row % (2 * w) >= w) & (col % (2 * w) < w)).astype(np.float32)
    t = np.arange(S)[None, :] + 0 * row
    parts["carryf"] = (t % P != 0).astype(np.float32)
    parts["carryb"] = (t % P != P - 1).astype(np.float32)
    at, where = 0, {}
    for name, a in parts.items():
        where[name] = (at, a.shape[1])
        at += a.shape[1]
    hot = np.zeros((33, STRIP + FWD), np.float32)
    for y in range(STRIP):
        d = S - 1 - y
        hot[bucket(d) if d >= 0 else 32, y] = 1
    for y in range(FWD):
        d = y - (S - 1)
        hot[bucket(d) if d >= 0 else 32, STRIP + y] = 1
    return np.ascontiguousarray(np.concatenate(list(parts.values()), 1)), where, hot


COLUMNS = [
    ("norm1", 8), ("conv_w", 6), ("conv_b", 2), ("qn", 1), ("kn0", 1), ("kn12", 1), ("pos", 32), ("qa", 2),
    ("kvn", 1), ("mqn", 1), ("mkn", 1), ("onw", 8), ("norm2", 8),
    ("nmix", 8), ("lb", 16), ("hgn", 4), ("nmem", 8), ("nmkv", 8), ("nffn", 8), ("unused", 4),
    ("cw2", 66), ("cb2", 22), ("fin", 8),
]


def two_blocks(nc, A, out):
    consts, where, _ = make_consts()
    ctx = ExitStack()
    with ctx:
        def sb(name, cols, dt=F32):
            return ctx.enter_context(nc.sbuf_tensor(name, [P, cols], dt))

        def sem(name):
            return ctx.enter_context(nc.semaphore(name))

        SHARED = where["suffix"][0]
        b2_names = ("band", "turn16", "rate", *(f"lv{d}{n}" for n in range(7) for d in "fb"))
        b1_names = ("suffix", "strict", "neg_strict", "causal", "turn96", "cos96", "sin96")
        b1_cols = sum(where[n][1] for n in b1_names)
        b2_cols = sum(where[n][1] for n in b2_names)
        const_sb = sb("const_sb", SHARED + max(b1_cols, b2_cols))
        place = {n: where[n][0] for n in ("ident", "ones", "blk64")}
        for names in (b1_names, b2_names):
            at = SHARED
            for n in names:
                place[n] = at
                at += where[n][1]

        def const(name):
            return const_sb[:, place[name]:place[name] + where[name][1]]

        ncol = sum(w for _, w in COLUMNS)
        col_sb = sb("col_sb", ncol)
        rel_sb = sb("rel_sb", 4)
        cw2_sb = sb("cw2_sb", 256)
        sink_sb = sb("sink_sb", 8)
        col_at, at = {}, 0
        for n, w in COLUMNS:
            col_at[n] = at
            at += w

        def col(name, i=0, rows=slice(0, P)):
            return col_sb[rows, col_at[name] + i:col_at[name] + i + 1]

        ring = sb("ring", SLOTS * SLOT)
        res = sb("res", KT * S)
        w_high = sb("w_high", PAIRS * PART, F32R)
        w_low = sb("w_low", PAIRS * PART, F32R)
        act_high = sb("act_high", KT * S, F32R)
        act_low = sb("act_low", KT * S, F32R)
        arena = sb("arena", 32 * S)
        strips = sb("strips", 4 * S)
        cmp_bias = sb("cmp_bias", 4 * S)
        sq = sb("sq", 4 * S)
        rb = sb("rb", 2 * S)
        prob = sb("prob", 2 * S)
        prob_t = sb("prob_t", 2 * S)
        small = sb("small", 64)

        def tile(buf, i, w=S):
            return buf[:, i * w:(i + 1) * w]

        def xt(k):
            return tile(res, k)

        def nt(k):
            return tile(act_high, k), tile(act_low, k)

        def ar(i, n=1):
            return arena[:, i * S:(i + n) * S]

        bank = [ctx.enter_context(nc.psum_tensor(f"bank{i}", [P, S], F32)) for i in range(8)]
        ident, ones, blk64 = const("ident"), const("ones"), const("blk64")

        strip_dram = nc.dram_tensor("strip_dram", [4, P * STRIP], F32).ap()
        fwd_dram = nc.dram_tensor("fwd_dram", [4, N_CMP * FWD], F32).ap()

        const_in = sem("const_in")
        const1_in = sem("const1_in")
        hot_in = sem("hot_in")
        cols_in = sem("cols_in")
        cols_zero = sem("cols_zero")
        cols_turned = sem("cols_turned")
        cols_out = sem("cols_out")
        x_in = [sem(f"x_in{half}") for half in range(2)]
        mem_in = sem("mem_in")
        pos_in = sem("pos_in")
        const2_in = sem("const2_in")
        slot_in = [sem(f"slot_in{i}") for i in range(SLOTS)]
        hidden_used = sem("hidden_used")
        part_high = sem("part_high")
        part_out = sem("part_out")
        w_rounded = sem("w_rounded")
        w_split = sem("w_split")
        big_tmp = sem("big_tmp")
        big_high = sem("big_high")
        tile_filled = sem("tile_filled")
        taken_act = sem("taken_act")
        taken_dve = sem("taken_dve")
        big_sq = sem("big_sq")
        big_add = sem("big_add")
        big_ss = sem("big_ss")
        big_rb = sem("big_rb")
        big_out = sem("big_out")
        nrm_sq = sem("nrm_sq")
        nrm_ss = sem("nrm_ss")
        nrm_rb = sem("nrm_rb")
        nrm_out = sem("nrm_out")
        bias_rep = sem("bias_rep")
        bias_mm = sem("bias_mm")
        bias_sb = sem("bias_sb")
        bias_out = sem("bias_out")
        bias_in = sem("bias_in")
        act_own = sem("act_own")
        dve_own = sem("dve_own")
        pool_own = sem("pool_own")
        turned = sem("turned")
        rope_out = sem("rope_out")
        conv_v = sem("conv_v")
        blocks_out = sem("blocks_out")
        hid_exp = sem("hid_exp")
        hid_out = sem("hid_out")
        score_mm = sem("score_mm")
        score_sh = sem("score_sh")
        exp_out = sem("exp_out")
        prob_out = sem("prob_out")
        trans_mm = sem("trans_mm")
        trans_act = sem("trans_act")
        trans_dve = sem("trans_dve")
        pv_mm = sem("pv_mm")
        head_out = sem("head_out")
        gates_out = sem("gates_out")
        sb_z = sem("sb_z")
        sb_zs = sem("sb_zs")
        sb_sp = sem("sb_sp")
        sb_c = sem("sb_c")
        sb_l = sem("sb_l")
        sb_t = sem("sb_t")
        sb_e = sem("sb_e")
        sb_a = sem("sb_a")
        sb_o = sem("sb_o")

        own = {"act": [0, act_own], "dve": [0, dve_own], "pool": [0, pool_own]}

        def link(eng, who, ins):
            own[who][0] += 1
            ins.then_inc(own[who][1], 1)
            eng.wait_ge(own[who][1], own[who][0])

        def cut(w, r0, rows, c0, cols):
            return w[r0:r0 + rows, c0:c0 + cols].rearrange("(k p) c -> p k c", p=P)

        w_in, w_out = A["w_in"][0], A["w_out"][0]
        w1, w2 = A["ffn_w1"][0], A["ffn_w2"][0]
        loads, load_at = [], {}

        def load(name, *parts):
            load_at[name] = len(loads)
            loads.append(parts)

        def wide(name, w, c0, r0=0, cols=256):
            load(name, (cols, 0, cut(w, r0, D, c0, cols)))

        for n, c0 in (("a_b", 0), ("a_c", 256), ("a_u", 512), ("n_q", 768)):
            wide(n, w_in, c0)
        load("n_k", (256, 0, cut(w_in, 0, D, 1024, 192)), (256, 192, cut(w_in, 0, D, 1280, 64)))
        load("m_q", (256, 0, cut(w_in, 0, D, 1420, 192)), (256, 192, cut(w_in, 0, D, 1740, 32)),
             (256, 224, cut(w_in, 0, D, 1408, 12)))
        load("m_kv", (256, 0, cut(w_in, 0, D, 1612, 128)), (256, 128, cut(w_in, 0, D, 1216, 64)),
             (256, 192, cut(w_in, 0, D, 1344, 64)))
        for n, c0 in (("s_q", 1772), ("s_k", 2028), ("s_v", 2284)):
            wide(n, w_in, c0)
        load("small", ("wq", None, None))
        for kv in range(2):
            for half in range(2):
                load(f"cmp{kv}{half}", (256, 0, cut(A["cmp_w1"][0, kv], half * D, D, 0, 256)))
        for i in range(4):
            wide(f"out{i}", w_out, 256 * i)
        FFN1_UP = len(loads)
        for i in range(16):
            wide(f"up{i}", w1, 256 * i)
        FFN1_DOWN = len(loads)
        for j in range(16):
            load(f"down{j}", (D, 0, cut(w2, 256 * j, 256, 0, D)))
        w_in2 = A["w_in_2"][0]
        for i in range(10):
            wide(f"p{i}", w_in2, 256 * i)
        for i in range(3):
            wide(f"p{10 + i}", w_in2, 256 * (10 + i))
        for i in range(4):
            wide(f"gr{i}", w_in2, 3328 + 256 * i)
            wide(f"ga{i}", w_in2, 4352 + 256 * i)
            load(f"br{i}", (256, 0, cut(A["w_br_rec_2"][0], 0, 512, 256 * i, 256)),
                 (256, 0, cut(A["w_br_att_2"][0], 0, 512, 256 * i, 256), 1024))
        for i in range(4):
            wide(f"mix{i}", A["w_mix_out_2"][0], 256 * i)
        for i in range(8):
            wide(f"mkv{i}", A["w_mem_kv_2"][0], 256 * i)
        for n in ("q", "o"):
            for i in range(4):
                wide(f"mem_{n}{i}", A[f"w_mem_{n}_2"][0], 256 * i)
        for i in range(11):
            wide(f"g2_{i}", A["w_up_2"][0], 2816 + 256 * i)
            wide(f"u2_{i}", A["w_up_2"][0], 256 * i)
        for j in range(11):
            load(f"d2_{j}", (D, 0, cut(A["w_down_2"][0], 256 * j, 256, 0, D)))

        def slot(name):
            s = load_at[name] % SLOTS
            return ring[:, s * SLOT:(s + 1) * SLOT]

        WKV_AT = 768

        def small_parts(dst):
            wq, wkv = A["mla_wq_b"][0], A["mla_wkv_b"][0]
            return [
                (dst[:, 0:384], wq[0:P, :]), (dst[0:64, 384:768], wq[P:192, :]), (dst[:, WKV_AT:WKV_AT + S], wkv),
            ]

        def part_list(i):
            s = i % SLOTS
            dst = ring[:, s * SLOT:(s + 1) * SLOT]
            if loads[i][0][0] == "wq":
                return small_parts(dst)
            found = []
            for cols, c0, src, *base in loads[i]:
                k, c = src.shape[1], src.shape[2]
                at = base[0] if base else 0
                found.append((dst[:, at:at + k * cols].rearrange("p (k c) -> p k c", c=cols)[:, :, c0:c0 + c], src))
            return found

        parts_of = [3 if x[0][0] == "wq" else len(x) for x in loads]

        def slot_ready(eng, name):
            i = load_at[name]
            eng.wait_ge(slot_in[i % SLOTS], 16 * sum(parts_of[j] for j in range(i % SLOTS, i + 1, SLOTS)))

        tiles, tile_at, bank_at = [], {}, {}

        def plan(name, who, load_name=None, ends=False, in_bank=None):
            bank_at[name] = len(tiles) % 4 if in_bank is None else in_bank
            tile_at[name] = len(tiles)
            tiles.append((name, who))
            if ends:
                released[load_at[load_name]] = ("tile", len(tiles))

        released = {}
        w_parts, w_part_at = [], {}

        def split(name, load_name, c0, cols=P, last=None):
            w_part_at[name] = len(w_parts)
            w_parts.append((load_name, c0, cols, last or name))
            released[load_at[load_name]] = ("split", len(w_parts))

        for k in range(KT):
            plan(f"x{k}", "act")
        for t in ("a_b", "a_c", "a_u", "n_q"):
            plan(f"{t}0", "dve" if t == "a_u" else "act")
            plan(f"{t}1", "dve" if t == "a_u" else "act", t, True)
        plan("kcvc", "act")
        plan("kskw", "act", "n_k", True)
        plan("cq0", "act")
        plan("cq1", "act")
        plan("gates", "act", "m_q", True)
        plan("ckv", "act")
        plan("nv", "dve", "m_kv", True)
        for t in ("s_q", "s_k"):
            plan(f"{t}0", "act")
            plan(f"{t}1", "act", t, True)
        plan("s_v0", "dve")
        plan("s_v1", "dve", "s_v", True)
        for h in range(4):
            plan(f"mq{h}", "act")
        for h in range(4):
            plan(f"mk{h}", "act")
        plan("mv0", "dve")
        plan("mv1", "dve", "small", True)
        for kv in range(2):
            plan(f"hid{kv}", "dve")
            released[load_at[f"cmp{kv}0"]] = ("tile", len(tiles))
            released[load_at[f"cmp{kv}1"]] = ("tile", len(tiles))
        plan("kc", "act")
        plan("vc", "dve")
        for m in range(8):
            plan(f"wo{m}", "dve")
        UP0 = len(tiles)
        for m in range(32):
            plan(f"up{m}", "act", f"up{m // 2}", m % 2 == 1)
        DOWN0 = len(tiles)
        def plan_down(name):
            for m in range(KT):
                plan(f"{name}{m}", "dve", in_bank=m if m >= 4 else None)

        used = [0]

        def split_rows(name, load_name, n, tile_name):
            for k in range(n):
                if k < n - 2:
                    used[0] += 1
                split(f"{name}{k}", f"{load_name}{k // 2}", (k % 2) * D, D, used[0] if k < n - 2 else f"{tile_name}7")

        plan_down("dn")
        for t in ("a_b", "a_c", "a_u", "n_q"):
            for i in range(2):
                split(f"{t}{i}", t, P * i)
        split("kcvc", "n_k", 0)
        split("kskw", "n_k", P)
        split("cq0", "m_q", 0)
        split("cq1", "m_q", P, 108, "gates")
        split("ckv", "m_kv", 0)
        split("nv", "m_kv", P)
        for t in ("s_q", "s_k", "s_v"):
            for i in range(2):
                split(f"{t}{i}", t, P * i, last="s_v1" if t == "s_v" else None)
        for m in range(8):
            split(f"wo{m}", f"out{m // 2}", (m % 2) * P)
        for m in range(32):
            split(f"up{m}", f"up{m // 2}", (m % 2) * P)
        split_rows("wd", "down", 32, "dn")
        for h in range(4):
            plan(f"qr{h}", "dve", f"p{h // 2}", h % 2 == 1)
        for g in range(8):
            plan(f"z{g}", "act", f"p{2 + g // 2}", g % 2 == 1)
        for i in range(4):
            plan(f"v{i}", "act", f"p{6 + i // 2}", i % 2 == 1)
        for h in range(4):
            plan(f"g{h}", "dve", f"p{8 + h // 2}", h % 2 == 1)
        for h in range(4):
            plan(f"qa{h}", "act", f"p{10 + h // 2}", h % 2 == 1)
        plan("ka", "act")
        plan("va", "dve", "p12", True)
        for i in range(4):
            plan(f"gr{2 * i}", "act")
            plan(f"gr{2 * i + 1}", "act", f"gr{i}", True)
            plan(f"ga{2 * i}", "act")
            plan(f"ga{2 * i + 1}", "act", f"ga{i}", True)
            for j in range(2):
                plan(f"rec{2 * i + j}", "dve")
                plan(f"att{2 * i + j}", "dve", f"br{i}", j == 1)
        for m in range(8):
            plan(f"mx{m}", "dve")
        for k in range(8):
            plan(f"m{k}", "act")
        for m in range(8):
            plan(f"memk{m}", "act", f"mkv{m // 2}", m % 2 == 1)
        for i in range(4):
            plan(f"memv{i}", "dve", f"mkv{4 + i}", True)
        for m in range(8):
            plan(f"memq{m}", "act", f"mem_q{m // 2}", m % 2 == 1)
        for m in range(8):
            plan(f"memo{m}", "dve")
        for i in range(11):
            plan(f"g2_{2 * i}", "act")
            plan(f"g2_{2 * i + 1}", "act", f"g2_{i}", True)
            plan(f"u2_{2 * i}", "dve")
            plan(f"u2_{2 * i + 1}", "dve", f"u2_{i}", True)
        plan_down("d2n")
        for i in range(8):
            plan(f"o{i}", "act" if i % 2 else "dve")
        for n, first in (("qr", 0), ("z", 2), ("v", 6), ("g", 8), ("qa", 10)):
            for h in range(8 if n == "z" else 4):
                split(f"{n}{h}", f"p{first + h // 2}", (h % 2) * P, last=f"v{h // 2 * 2 + 1}" if n == "v" else None)
        split("ka", "p12", 0)
        split("va", "p12", P)
        for i in range(4):
            for n in ("gr", "ga"):
                for j in range(2):
                    split(f"{n}{2 * i + j}", f"{n}{i}", j * P)
        for n, load_name in (("mx", "mix"), ("memq", "mem_q"), ("memo", "mem_o")):
            for m in range(8):
                split(f"{n}{m}", f"{load_name}{m // 2}", (m % 2) * P)
        for i in range(11):
            for n in ("g2_", "u2_"):
                for j in range(2):
                    split(f"{n}{2 * i + j}", f"{n}{i}", j * P)
        split_rows("we", "d2_", 22, "d2n")

        def count(who, n):
            return sum(w == who for _, w in tiles[:n])

        def taken(eng, name):
            n = tile_at[name]
            who = tiles[n][1]
            eng.wait_ge(taken_act if who == "act" else taken_dve, count(who, n + 1))

        def open_tile(eng, name):
            n = tile_at[name]
            if n >= 4:
                taken(eng, tiles[n - 4][0])
            return bank[bank_at[name]]

        def filled(eng, name):
            eng.wait_ge(tile_filled, tile_at[name] + 1)
            return bank[bank_at[name]]

        def wait_released(eng, i):
            kind, value = released[i]
            eng.wait_ge({"tile": tile_filled, "split": w_split}[kind], value)

        def raw_part(name):
            load_name, c0, cols, _ = w_parts[w_part_at[name]]
            if cols == D:
                return slot(load_name)[:, c0:c0 + D].rearrange("p (k c) -> p k c", c=P)
            return slot(load_name).rearrange("p (k c) -> p k c", c=256)[:, :, c0:c0 + cols]

        def part(buf, name):
            i, cols = w_part_at[name], w_parts[w_part_at[name]][2]
            cols = min(cols, P)
            at = (i % PAIRS) * PART
            return buf[:, at:at + KT * cols].rearrange("p (k c) -> p k c", c=cols)

        def part_pair(buf, name):
            assert w_part_at[name] % PAIRS == 0
            return buf[:, :].rearrange("p (b k c) -> p k b c", b=PAIRS, c=P)

        part_names = list(w_part_at)
        next_part = {"act": 0, "pool": 0}

        def round_weights(eng, upto):
            while next_part["act"] <= w_part_at[upto]:
                i = next_part["act"]
                name = part_names[i]
                slot_ready(eng, w_parts[i][0])
                if i >= PAIRS:
                    last = w_parts[i - PAIRS][3]
                    if isinstance(last, int):
                        eng.wait_ge(hidden_used, last)
                    else:
                        filled(eng, last)
                nc.scalar.activation(part(w_high, name), raw_part(name), ACT.Copy).then_inc(w_rounded, 1)
                next_part["act"] += 1

        PHASE_ENDS = ("s_v1", "wd31", "mx7", "we21")

        def ahead(eng, name):
            i = min(w_part_at[name] + PAIRS, *(w_part_at[e] for e in PHASE_ENDS if w_part_at[e] >= w_part_at[name]))\
                if name not in PHASE_ENDS else w_part_at[name]
            round_weights(eng, part_names[i])

        def split_weights(eng, upto):
            while next_part["pool"] <= w_part_at[upto]:
                i = next_part["pool"]
                name = part_names[i]
                eng.wait_ge(w_rounded, i + 1)
                nc.gpsimd.tensor_tensor(part(w_low, name), raw_part(name), part(w_high, name).bitcast(F32),
                                        ALU.subtract).then_inc(w_split, 1)
                next_part["pool"] += 1

        AB, AV, AQ, KCVC, KSKW, KS2, KW2 = 0, 2, 4, 6, 7, 8, 9
        SZ = 10
        CQ, MQ, MK = 10, 12, 16
        SQT, SKT, CKV = 20, 22, 24
        NV, SV, MV = 25, 26, 28
        KCD, MISC = 30, 31
        nv = ar(NV)
        sv = ar(SV, 2).rearrange("p (t c) -> p t c", c=256)
        mv = ar(MV, 2).rearrange("p (t c) -> p t c", c=256)
        gates = small[:, 0:48]
        kcd = ar(KCD)
        vcd = ar(AV)
        blocks = ar(KCVC)
        misc = ar(MISC)
        hidden = misc[:, 0:128].rearrange("p (a n) -> p a n", n=32)
        hid_e = misc[:, 128:192].rearrange("p (a n) -> p a n", n=32)
        kc_raw = misc[:, 192:224]
        kc = misc[:, 224:256]
        vc = misc[:, 256:320]
        yt = (ar(AB), ar(AB + 1), ar(AQ), ar(AQ + 1), ar(KS2), ar(KW2), ar(SQT), ar(SQT + 1)).__getitem__
        nmax = misc[:, 320:324]
        rsum = misc[:, 324:328]
        rinv = misc[:, 328:332]

        norms, norm_at = [], {}

        def add_norm(name, src, lhs, rows, width, n, outs):
            norm_at[name] = len(norms)
            norms.append((src, lhs, rows, width, n, outs))

        for i in range(2):
            add_norm(f"q{i}", [ar(AQ + i)], [blk64], P, S, 64, [(ar(AQ + i), ar(AQ + i), col("qn"), (0, P))])
        lo, hi = slice(0, 64), slice(64, P)
        add_norm("kskw", [ar(KSKW)], [blk64], P, S, 64, [
            (ar(KS2)[lo], ar(KSKW)[lo], col("kn12", 0, lo), (0, 64)),
            (ar(KS2)[hi], ar(KSKW)[lo], col("kn12", 0, lo), (0, 64)),
            (ar(KW2)[lo], ar(KSKW)[hi], col("kn12", 0, hi), (64, P)),
            (ar(KW2)[hi], ar(KSKW)[hi], col("kn12", 0, hi), (64, P))])
        add_norm("cq", [ar(CQ), ar(CQ + 1)[lo]], [ones, ones[lo]], P, S, 192, [
            (ar(CQ), ar(CQ), col("qa"), (0, P)), (ar(CQ + 1)[lo], ar(CQ + 1)[lo], col("qa", 1, lo), (0, 64))])
        add_norm("ckv", [ar(CKV)], [ones], P, S, P, [(ar(CKV), ar(CKV), col("kvn"), (0, P))])
        r96 = slice(0, 96)
        for t, base, gain in (("mq", MQ, "mqn"), ("mk", MK, "mkn")):
            for h in range(4):
                add_norm(f"{t}{h}", [ar(base + h)[r96]], [ones[r96, r96]], 96, S, 96,
                         [(ar(base + h)[r96], ar(base + h)[r96], col(gain, 0, r96), (0, 96))])
        add_norm("kc", [kc_raw[lo, 0:N_CMP]], [ones[lo, 0:64]], 64, N_CMP, 64, [
            (kc[lo, 0:N_CMP], kc_raw[lo, 0:N_CMP], col("kn0", 0, lo), (0, 64)),
            (kc[hi, 0:N_CMP], kc_raw[lo, 0:N_CMP], col("kn0", 0, lo), (0, 64))])
        for g in range(4):
            add_norm(f"y{g}", [yt(2 * g), yt(2 * g + 1)], [ones, ones], P, S, 256,
                     [(yt(2 * g + i), yt(2 * g + i), col("onw", 2 * g + i), (0, P)) for i in range(2)])
        for h in range(4):
            add_norm(f"r{h}", [ar(h)], [ones], P, S, P, [(ar(h), ar(h), col("hgn", h), (0, P))])
        NORM_BANK = (4, 5)

        def norm_squares(eng, name):
            u = norm_at[name]
            src, _, _, w, _, _ = norms[u]
            if u >= 2:
                eng.wait_ge(nrm_ss, u - 1)
            for i, a in enumerate(src):
                r0 = a.shape[0]
                last = nc.scalar.activation(sq[0:r0, (2 * (u % 2) + i) * S:(2 * (u % 2) + i) * S + w], a, ACT.Square)
            last.then_inc(nrm_sq, 1)

        def norm_sums(eng, name):
            u = norm_at[name]
            src, lhs, rows, w, _, _ = norms[u]
            eng.wait_ge(nrm_sq, u + 1)
            if u >= 2:
                eng.wait_ge(nrm_rb, u - 1)
            for i, a in enumerate(src):
                r0 = a.shape[0]
                at = (2 * (u % 2) + i) * S
                last = nc.tensor.matmul(bank[NORM_BANK[u % 2]][0:rows, 0:w], lhs[i], sq[0:r0, at:at + w],
                                        start=i == 0, stop=i == len(src) - 1)
            last.then_inc(nrm_ss, 1)

        def norm_factor(eng, name):
            u = norm_at[name]
            _, _, rows, w, n, _ = norms[u]
            eng.wait_ge(nrm_ss, u + 1)
            if u >= 2:
                eng.wait_ge(nrm_out, u - 1)
            r = rb[0:rows, (u % 2) * S:(u % 2) * S + w]
            link(eng, "act", nc.scalar.activation(r, bank[NORM_BANK[u % 2]][0:rows, 0:w], ACT.Ln,
                                                  bias=eps_col[0:rows], scale=1.0 / n))
            nc.scalar.activation(r, r, ACT.Exp, scale=-0.5).then_inc(nrm_rb, 1)

        def norm_apply(eng, name):
            u = norm_at[name]
            _, _, _, w, _, outs = norms[u]
            eng.wait_ge(nrm_rb, u + 1)
            for o, a, gain, (r0, r1) in outs:
                last = nc.vector.scalar_tensor_tensor(o, a, gain, rb[r0:r1, (u % 2) * S:(u % 2) * S + w],
                                                      ALU.mult, ALU.mult)
            last.then_inc(nrm_out, 1)

        def normed(eng, name):
            eng.wait_ge(nrm_out, norm_at[name] + 1)

        bigs, big_at, split_big_at = [], {}, {}

        def add_big(name, src, dst, gain, w=S):
            if dst is nt:
                split_big_at[name] = len(split_big_at)
            big_at[name] = len(bigs)
            bigs.append((src, dst, gain, w))

        add_big("in1", xt, nt, "norm1")
        add_big("ffn1", xt, nt, "norm2")
        def mem_t(k):
            return ar(12, 4)[:, k * 256:(k + 1) * 256]

        add_big("mix", xt, nt, "nmix")
        add_big("memkv", mem_t, mem_t, "nmkv", 256)
        add_big("mem", xt, nt, "nmem")
        add_big("ffn2", xt, nt, "nffn")
        add_big("fin", xt, lambda k: ar(8 + k), "fin")
        acc = ctx.enter_context(nc.sbuf_tensor("acc", [P, S], F32))
        eps_t = sb("eps_t", 2)
        eps_col = eps_t[:, 0:1]
        one_col = eps_t[:, 1:2]
        BIG_BANK = 6

        def big_square(eng, name, k):
            b = big_at[name]
            src, _, _, w = bigs[b]
            n = 8 * b + k
            if n >= 2:
                eng.wait_ge(big_add, n - 1)
            nc.scalar.activation(sq[:, (n % 2) * S:(n % 2) * S + w], src(k), ACT.Square).then_inc(big_sq, 1)

        def big_sum(eng, name, parts=None, tile_name=None):
            b = big_at[name]
            w = bigs[b][3]
            for k in range(8):
                n = 8 * b + k
                if k == 6 and parts:
                    split_weights(eng, parts)
                if tile_name:
                    split_weights(eng, part_names[w_part_at[f"{tile_name}{k}"] + PAIRS])
                eng.wait_ge(big_sq, n + 1)
                s_k = sq[:, (n % 2) * S:(n % 2) * S + w]
                if k == 0:
                    if b:
                        eng.wait_ge(big_ss, b)
                    nc.gpsimd.tensor_copy(acc[:, 0:w], s_k).then_inc(big_add, 1)
                else:
                    eng.wait_ge(big_add, n)
                    nc.gpsimd.tensor_tensor(acc[:, 0:w], acc[:, 0:w], s_k, ALU.add).then_inc(big_add, 1)

        def big_total(eng, name):
            b = big_at[name]
            w = bigs[b][3]
            eng.wait_ge(big_add, 8 * b + 8)
            nc.tensor.matmul(bank[BIG_BANK][:, 0:w], ones, acc[:, 0:w], start=True, stop=True).then_inc(big_ss, 1)

        def big_factor(eng, name):
            b = big_at[name]
            w = bigs[b][3]
            eng.wait_ge(big_ss, b + 1)
            link(eng, "act", nc.scalar.activation(rb[:, 0:w], bank[BIG_BANK][:, 0:w], ACT.Ln, bias=eps_col,
                                                  scale=1.0 / D))
            nc.scalar.activation(rb[:, 0:w], rb[:, 0:w], ACT.Exp, scale=-0.5).then_inc(big_rb, 1)

        def big_before(k):
            return tile((prob, prob_t)[k // 2 % 2], k % 2)

        def big_apply(eng, name):
            b = big_at[name]
            src, dst, gain, w = bigs[b]
            eng.wait_ge(big_rb, b + 1)
            if dst is not nt:
                for k in range(8):
                    nc.vector.scalar_tensor_tensor(dst(k), src(k), col(gain, k), rb[:, 0:w], ALU.mult, ALU.mult)\
                        .then_inc(big_out, 1)
                return

            def rest(k):
                high, low = nt(k)
                eng.wait_ge(big_high, 8 * split_big_at[name] + k + 1)
                nc.vector.tensor_tensor(low, big_before(k), high.bitcast(F32), ALU.subtract).then_inc(big_out, 1)

            for k in range(8):
                nc.vector.scalar_tensor_tensor(big_before(k), src(k), col(gain, k), rb[:, 0:w], ALU.mult,
                                               ALU.mult).then_inc(big_tmp, 1)
                if k:
                    rest(k - 1)
            rest(7)

        def big_round(eng, name):
            for k in range(8):
                eng.wait_ge(big_tmp, 8 * split_big_at[name] + k + 1)
                nc.scalar.activation(nt(k)[0], big_before(k), ACT.Copy).then_inc(big_high, 1)

        def big_ready(eng, name, k):
            eng.wait_ge(big_out, 8 * big_at[name] + k + 1)

        splits, split_src_at = [], {}

        def add_split(name, src, dst):
            split_src_at[name] = len(splits)
            splits.append((src, dst))

        for k in range(8):
            add_split(f"y{k}", yt(k), nt(k))
        for k in range(32):
            add_split(f"h{k}", ar(k), nt(k % 8))
        for k in range(8):
            add_split(f"g{k}", ar(8 + k), nt(k))
        for k in range(8):
            add_split(f"o{k}", ar(k), nt(k))
        for k in range(22):
            add_split(f"e{k}", ar(k), nt(k % 8))

        def part_round(eng, name):
            src, (high, _) = splits[split_src_at[name]]
            nc.scalar.activation(high, src, ACT.Copy).then_inc(part_high, 1)

        def part_rest(eng, name):
            src, (high, low) = splits[split_src_at[name]]
            eng.wait_ge(part_high, split_src_at[name] + 1)
            nc.vector.tensor_tensor(low, src, high.bitcast(F32), ALU.subtract).then_inc(part_out, 1)

        def in_parts(eng, name):
            eng.wait_ge(part_out, split_src_at[name] + 1)

        def round_hidden(eng, name, parts, n, before, up):
            filled(eng, f"{up}{n - 1}")
            for k in range(n):
                if k >= 8:
                    eng.wait_ge(hidden_used, before + k - 7)
                taken(eng, f"{up}{k}")
                part_round(eng, f"{name}{k}")
                if k >= 3:
                    round_weights(eng, f"{parts}{k - 1}")
            round_weights(eng, f"{parts}{n - 1}")

        units = []
        for hp in range(2):
            for h in (2 * hp, 2 * hp + 1):
                for qt in range(TT):
                    for kind in ("cmp", "slc", "win"):
                        units.append((kind, h, qt))
        N_NSA = len(units)
        for h in range(4):
            for qt in range(TT):
                units.append(("mla", h, qt))
        N_B1 = len(units)
        for h in range(8):
            for qt in range(TT):
                units.append(("gqa", h, qt))
        N_GQA = len(units)
        for h in range(4):
            for qt in range(TT):
                units.append(("mem", h, qt))
        N_ALL = len(units)
        SCORE_BANK = (0, 1, 2, 4)
        TRANS_BANK = (3, 6)
        OUT_BANK = (5, 7)

        def key_tiles(u):
            kind, h, qt = units[u]
            if kind == "gqa":
                return list(range(max(0, qt - 1), min(TT - 1, qt + 1) + 1))
            if kind == "mem":
                return [0, 1]
            if kind == "cmp":
                return [0]
            return list(range(qt + 1))

        def width(u):
            return N_CMP if units[u][0] == "cmp" else P * len(key_tiles(u))

        def head_rows(h):
            return slice(64 * (h % 2), 64 * (h % 2) + 64)

        def pv_last(u):
            return units[u][0] not in ("cmp", "slc")

        def out_group(u):
            kind, h, qt = units[u]
            return {"cmp": 0, "slc": 0, "win": 0, "mla": 2, "gqa": 6, "mem": 10}[kind] + (
                2 * h if kind == "mem" else h // 2)

        def scores(eng, u):
            kind, h, qt = units[u]
            if u >= 4:
                eng.wait_ge(exp_out, u - 3)
            b = bank[SCORE_BANK[u % 4]]
            w, qs = width(u), slice(qt * P, (qt + 1) * P)
            if kind in ("cmp", "slc", "win"):
                r = head_rows(h)
                keys = {"cmp": kc, "slc": ar(KS2), "win": ar(KW2)}[kind][r, 0:w]
                last = nc.tensor.matmul(b[:, 0:w], ar(AQ + h // 2)[r, qs], keys, start=True, stop=kind != "cmp")
                if kind == "cmp":
                    last = nc.tensor.matmul(b[:, 0:w], cmp_bias[0:N_CMP, h * S + qt * P:h * S + (qt + 1) * P],
                                            ident[0:N_CMP, 0:N_CMP], start=False, stop=True)
            elif kind == "mla":
                last = nc.tensor.matmul(b[:, 0:w], ar(MQ + h)[0:96, qs], ar(MK + h)[0:96, 0:w], start=True, stop=True)
            elif kind == "gqa":
                r, k0 = head_rows(h), key_tiles(u)[0] * P
                last = nc.tensor.matmul(b[:, 0:w], ar(QA + h // 2)[r, qs], ar(KA + h // 4)[r, k0:k0 + w],
                                        start=True, stop=True)
            else:
                for i in range(2):
                    last = nc.tensor.matmul(b[:, 0:w], ar(MEMQ + 2 * h + i)[:, qs], mem_k[:, 2 * h + i, :],
                                            start=i == 0, stop=i == 1)
            last.then_inc(score_mm, 1)

        SCALE = {"cmp": 64 ** -0.5, "slc": 64 ** -0.5, "win": 64 ** -0.5, "mla": 96 ** -0.5, "gqa": 64 ** -0.5,
                 "mem": 256 ** -0.5}

        def prob_of(u):
            return (tile(prob, 0), tile(prob, 1), tile(sq, 2), tile(sq, 3))[u % 4][:, 0:width(u)]

        def shift(eng, u):
            kind, h, qt = units[u]
            scale, w = SCALE[kind], width(u)
            b = bank[SCORE_BANK[u % 4]]
            nm = nmax[:, u % 4:u % 4 + 1]
            eng.wait_ge(score_mm, u + 1)
            if u >= 4:
                eng.wait_ge(trans_mm, u - 3)
            if kind in ("cmp", "mem"):
                link(eng, "dve", nc.vector.tensor_reduce(nm, b[:, 0:w], AX_X, ALU.max))
                nc.vector.tensor_scalar(nm, nm, -scale, NO_KEY, ALU.mult, ALU.min).then_inc(score_sh, 1)
                return
            if kind in ("slc", "win"):
                add = strips[:, h * S + (TT - 1 - qt) * P:(h + 1) * S]
            elif kind == "mla":
                add = const("causal")[:, (TT - 1 - qt) * P:S]
            else:
                k0 = (key_tiles(u)[0] - qt + 1) * P
                add = const("band")[:, k0:k0 + w]
            ins = nc.vector.tensor_tensor_reduce(prob_of(u), b[:, 0:w], add, -scale, NO_KEY, ALU.add, ALU.min, nm)
            if kind == "gqa":
                link(eng, "dve", ins)
                ins = nc.vector.tensor_tensor(nm, nm, nsink[:, h:h + 1], ALU.min)
            ins.then_inc(score_sh, 1)

        def exps(eng, u):
            kind, h, qt = units[u]
            b = bank[SCORE_BANK[u % 4]]
            nm, total = nmax[:, u % 4:u % 4 + 1], rsum[:, u % 4:u % 4 + 1]
            eng.wait_ge(score_sh, u + 1)
            if kind in ("cmp", "mem"):
                nc.scalar.activation(prob_of(u), b[:, 0:width(u)], ACT.Exp, bias=nm, scale=SCALE[kind],
                                     accum_out=total).then_inc(exp_out, 1)
                return
            if kind == "gqa":
                nc.scalar.activation(esink[:, u % 4:u % 4 + 1], sink_sb[:, h:h + 1], ACT.Exp, bias=nm)
            nc.scalar.activation(prob_of(u), prob_of(u), ACT.Exp, bias=nm, scale=-1.0,
                                 accum_out=total).then_inc(exp_out, 1)

        def normalise(eng, u):
            kind, h, qt = units[u]
            total, inv = rsum[:, u % 4:u % 4 + 1], rinv[:, u % 4:u % 4 + 1]
            eng.wait_ge(exp_out, u + 1)
            if kind == "cmp":
                link(eng, "dve", nc.vector.tensor_scalar(total, total, 1e-30, None, ALU.max))
            if kind == "gqa":
                link(eng, "dve", nc.vector.tensor_tensor(total, total, esink[:, u % 4:u % 4 + 1], ALU.add))
            link(eng, "dve", nc.vector.reciprocal(inv, total))
            if kind in ("cmp", "slc", "win"):
                g = 12 * qt + 3 * h + ("cmp", "slc", "win").index(kind)
                ins = nc.vector.tensor_scalar(prob_of(u), prob_of(u), inv, gates[:, g:g + 1], ALU.mult, ALU.mult)
            else:
                ins = nc.vector.tensor_scalar(prob_of(u), prob_of(u), inv, None, ALU.mult)
            ins.then_inc(prob_out, 1)

        def turn(eng, u):
            eng.wait_ge(prob_out, u + 1)
            if u >= 2:
                copied(eng, u - 2)
            b = bank[TRANS_BANK[u % 2]]
            p = prob_of(u)
            for i in range(len(key_tiles(u))):
                w = min(P, width(u))
                last = nc.tensor.transpose(b[0:w, i * P:(i + 1) * P], p[:, i * P:i * P + w], ident)
            last.then_inc(trans_mm, 1)

        def copied(eng, u):
            eng.wait_ge(trans_dve if u % 2 else trans_act, u // 2 + 1)

        def copy_turned(eng, u):
            eng.wait_ge(trans_mm, u + 1)
            if u >= 2:
                eng.wait_ge(pv_mm, u - 1)
            r = N_CMP if units[u][0] == "cmp" else P
            w = P * len(key_tiles(u))
            dst, src = prob_t[0:r, (u % 2) * S:(u % 2) * S + w], bank[TRANS_BANK[u % 2]][0:r, 0:w]
            if u % 2:
                nc.vector.tensor_copy(dst, src).then_inc(trans_dve, 1)
            else:
                nc.scalar.activation(dst, src, ACT.Copy).then_inc(trans_act, 1)

        def values(eng, u):
            kind, h, qt = units[u]
            copied(eng, u)
            g = out_group(u)
            if kind == "mem":
                if qt == 0:
                    eng.wait_ge(head_out, g)
                for m in range(2):
                    for i in range(2):
                        last = nc.tensor.matmul(
                            bank[OUT_BANK[m]][:, qt * P:(qt + 1) * P], mem_v[:, i, (2 * h + m) * P:(2 * h + m + 1) * P],
                            prob_t[:, (u % 2) * S + i * P:(u % 2) * S + (i + 1) * P], start=i == 0, stop=i == 1)
                last.then_inc(pv_mm, 1)
                return
            if qt == 0 and h % 2 == 0 and kind in ("cmp", "mla", "gqa") and g >= 2:
                eng.wait_ge(head_out, g - 1)
            o = bank[OUT_BANK[g % 2]][head_rows(h), qt * P:(qt + 1) * P]
            n = len(key_tiles(u))
            for i, kt in enumerate(key_tiles(u)):
                r = N_CMP if kind == "cmp" else P
                if kind == "cmp":
                    v = vc[0:N_CMP, 0:64]
                elif kind in ("slc", "win"):
                    v = nv[:, kt * P + (64 if kind == "win" else 0):kt * P + (64 if kind == "win" else 0) + 64]
                elif kind == "mla":
                    v = mv[:, kt, 64 * h:64 * h + 64]
                else:
                    v = va[:, kt * P + 64 * (h // 4):kt * P + 64 * (h // 4) + 64]
                last = nc.tensor.matmul(o, v, prob_t[0:r, (u % 2) * S + i * P:(u % 2) * S + (i + 1) * P],
                                        start=i == 0 and kind not in ("slc", "win"), stop=i == n - 1 and pv_last(u),
                                        )
            last.then_inc(pv_mm, 1)

        def take_heads(eng, u, dst):
            eng.wait_ge(pv_mm, u + 1)
            g = out_group(u)
            if units[u][0] == "mem":
                for m in range(2):
                    nc.scalar.activation(dst[m], bank[OUT_BANK[m]][:, :], ACT.Copy).then_inc(head_out, 1)
            else:
                nc.scalar.activation(dst, bank[OUT_BANK[g % 2]][:, :], ACT.Copy).then_inc(head_out, 1)

        AHEAD = 3

        def attend_pe(eng, u0, u1):
            for u in range(u0, min(u0 + AHEAD, u1)):
                scores(eng, u)
            for u in range(u0, u1):
                if u + AHEAD < u1:
                    scores(eng, u + AHEAD)
                turn(eng, u)
                if u > u0:
                    values(eng, u - 1)
            values(eng, u1 - 1)

        def attend_act(eng, u0, u1, pair_end):
            for u in range(u0, u1):
                exps(eng, u)
                if u > u0:
                    if (u - 1) % 2 == 0:
                        copy_turned(eng, u - 1)
                    if u - 2 >= u0:
                        pair_end(eng, u - 2)
            if (u1 - 1) % 2 == 0:
                copy_turned(eng, u1 - 1)
            for u in range(max(u0, u1 - 2), u1):
                pair_end(eng, u)

        def attend_dve(eng, u0, u1, between=None):
            shift(eng, u0)
            shift(eng, u0 + 1)
            for u in range(u0, u1):
                if u + 2 < u1:
                    shift(eng, u + 2)
                normalise(eng, u)
                if u > u0 and (u - 1) % 2:
                    copy_turned(eng, u - 1)
                if between:
                    between(eng, u)
            if (u1 - 1) % 2:
                copy_turned(eng, u1 - 1)

        def pair_end_b1(eng, u):
            kind, h, qt = units[u]
            if kind in ("win", "mla") and h % 2 == 1 and qt == TT - 1:
                take_heads(eng, u, yt(2 + h // 2 if kind == "win" else 4 + h // 2))

        ST_W = [S - kt * P for kt in range(TT)]
        ST_AT = [0, 512, 896, 1152]

        def stick(h, kt, which):
            at = (SZ * S) + (h % 2) * 2560 + which * 1280 + ST_AT[kt]
            return arena[:, at:at + ST_W[kt]]

        def stick_scores(eng, h):
            for kt in range(TT):
                n = 4 * h + kt
                if n >= 2:
                    eng.wait_ge(sb_zs, n - 1)
                r = head_rows(h)
                nc.tensor.matmul(bank[n % 2][:, 0:ST_W[kt]], ar(SKT + h // 2)[r, kt * P:(kt + 1) * P],
                                 ar(SQT + h // 2)[r, kt * P:S], start=True, stop=True).then_inc(sb_z, 1)

        def stick_sums(eng, h):
            eng.wait_ge(sb_sp, 4 * h + 4)
            for kt in range(TT):
                n = 4 * h + kt
                if n >= 2:
                    eng.wait_ge(sb_t, n - 1)
                b = bank[2 + n % 2]
                last = nc.tensor.matmul(b[:, 0:ST_W[kt]], const("suffix"), stick(h, kt, 1), start=True,
                                        stop=kt == TT - 1)
                for later in range(kt + 1, TT):
                    last = nc.tensor.matmul(b[:, (later - kt) * P:ST_W[kt]], ones, stick(h, later, 1), start=False,
                                            stop=later == TT - 1)
                last.then_inc(sb_c, 1)

        def stick_values(eng, h):
            for kt in range(TT):
                eng.wait_ge(sb_e, 4 * h + kt + 1)
                last = nc.tensor.matmul(bank[OUT_BANK[h // 2]][head_rows(h), kt * P:S],
                                        sv[:, kt, 64 * h:64 * h + 64], stick(h, kt, 0),
                                        start=kt == 0, stop=kt == TT - 1)
            last.then_inc(sb_o, 1)

        def stick_logs(eng, h):
            for kt in range(TT):
                n = 4 * h + kt
                eng.wait_ge(sb_z, n + 1)
                if h >= 2:
                    eng.wait_ge(sb_o, h - 1)
                z, s = stick(h, kt, 0), stick(h, kt, 1)
                nc.scalar.activation(z, bank[n % 2][:, 0:ST_W[kt]], ACT.Copy).then_inc(sb_zs, 1)
                eng.wait_ge(sb_zs, n + 1)
                link(eng, "act", nc.scalar.activation(s, z, ACT.Abs))
                link(eng, "act", nc.scalar.activation(s, s, ACT.Exp, scale=-1.0))
                nc.scalar.activation(s, s, ACT.Ln, bias=one_col).then_inc(sb_l, 1)

        def stick_softplus(eng, h):
            for kt in range(TT):
                n = 4 * h + kt
                eng.wait_ge(sb_l, n + 1)
                z, s = stick(h, kt, 0), stick(h, kt, 1)
                link(eng, "dve", nc.vector.scalar_tensor_tensor(s, z, 0.0, s, ALU.max, ALU.add))
                nc.vector.tensor_tensor(s[:, 0:P], s[:, 0:P], const("strict"), ALU.mult).then_inc(sb_sp, 1)

        def stick_shift(eng, h):
            for kt in range(TT):
                n = 4 * h + kt
                eng.wait_ge(sb_c, n + 1)
                z = stick(h, kt, 0)
                link(eng, "dve", nc.vector.tensor_tensor(z, z, bank[2 + n % 2][:, 0:ST_W[kt]], ALU.subtract))
                nc.vector.tensor_tensor(z[:, 0:P], z[:, 0:P], const("neg_strict"), ALU.add).then_inc(sb_t, 1)

        def stick_exps(eng, h):
            for kt in range(TT):
                n = 4 * h + kt
                eng.wait_ge(sb_t, n + 1)
                nc.scalar.activation(stick(h, kt, 0), stick(h, kt, 0), ACT.Exp).then_inc(sb_e, 1)

        def take_stick(eng, hp):
            eng.wait_ge(sb_o, 2 * hp + 2)
            nc.scalar.activation(yt(6 + hp), bank[OUT_BANK[hp]][:, :], ACT.Copy).then_inc(head_out, 1)

        QH, FG, VR, GR, QA, KA, VA = 0, 4, 12, 16, 20, 24, 26
        K_RAW = 27
        va = ar(VA)
        MEMQ = 0
        mem_tok = ar(8, 4).rearrange("p (t d) -> p t d", d=D)
        mem_k = ar(16, 4).rearrange("p (m s) -> p m s", s=256)
        mem_v = ar(20, 4).rearrange("p (t d) -> p t d", d=D)
        cols2 = sb("cols2", 64)
        low, one_low, low_e = cols2[:, 0:8], cols2[:, 8:16], cols2[:, 16:32]
        low_max, nsink, esink, decay = cols2[:, 32:40], cols2[:, 40:48], cols2[:, 48:52], cols2[:, 52:60]
        pos_i, angle, whole_i, fold = (tile(strips, i) for i in range(4))
        cos16, sin16 = tile(cmp_bias, 0), tile(cmp_bias, 1)
        padded = [ar(22, 3)[:, 520 * i:520 * i + S + 2] for i in range(2)]
        conv_c, conv_e = (ar(25), ar(26)), (ar(27), ar(28))
        carry = {0: tile(rb, 0), 1: tile(rb, 1)}
        carry_in = sem("carry_in")
        trig_dve = sem("trig_dve")
        trig_act = sem("trig_act")
        low_dve = sem("low_dve")
        low_act = sem("low_act")
        qr_exp = sem("qr_exp")
        f_out = sem("f_out")
        g_exp = sem("g_exp")
        turned2 = sem("turned2")
        rope2 = sem("rope2")
        floor_out = sem("floor_out")
        log_out = sem("log_out")
        sum_out = sem("sum_out")
        end_diff = sem("end_diff")
        end_exp = sem("end_exp")
        ends_out = sem("ends_out")
        keys_turned = sem("keys_turned")
        keys_sb = sem("keys_sb")
        update_mm = sem("update_mm")
        states_out = sem("states_out")
        level_diff = sem("level_diff")
        level_exp = sem("level_exp")
        level_in = sem("level_in")
        level_mm = sem("level_mm")
        level_out = sem("level_out")
        rec_mm = sem("rec_mm")
        rec_out = sem("rec_out")
        rec_gated = sem("rec_gated")
        gate_sig = sem("gate_sig")
        merged = sem("merged")
        pads = sem("pads")
        conv2_out = sem("conv2_out")
        conv2_silu = sem("conv2_silu")
        out_done = sem("out_done")

        G_KEY = (ar(27), tile(cmp_bias, 3))
        G_SUM = (ar(28), acc[:, :])
        G_X = (ar(29), ar(30))
        G_END = ar(31)
        G_SCORE = (tile(strips, 0), tile(strips, 1))
        G_QUERY = (tile(strips, 2), tile(strips, 3))
        G_KEYT = tile(cmp_bias, 0)
        G_STATE = (tile(cmp_bias, 1), tile(cmp_bias, 2))
        LEVELS = 7

        def halves(a, n, d):
            w = 1 << n
            v = a.rearrange("p (b w) -> p b w", w=2 * w)
            left, right = v[:, :, 0:w], v[:, :, w:2 * w]
            return (right, left) if d == 0 else (left, right)

        def key_chunk(d, i):
            return i if d == 0 else TT - 1 - i

        def rec_floor(eng, g):
            if g >= 2:
                eng.wait_ge(level_mm, 8 * (g - 1))
            f = ar(FG + 4 * (g % 2) + g // 2)
            nc.vector.tensor_scalar(G_KEY[g % 2], f, -1.0, 1.0, ALU.mult, ALU.add)
            if g >= 2:
                eng.wait_ge(level_diff, 7 * (g - 1))
            nc.vector.tensor_scalar(G_SUM[g % 2], f, 1e-19, None, ALU.max).then_inc(floor_out, 1)

        def rec_log(eng, g):
            eng.wait_ge(floor_out, g + 1)
            nc.scalar.activation(G_SUM[g % 2], G_SUM[g % 2], ACT.Ln).then_inc(log_out, 1)

        def rec_scan(eng, g):
            eng.wait_ge(log_out, g + 1)
            if g == 0:
                eng.wait_ge(carry_in, 16)
            s = G_SUM[g % 2]
            if g % 2 == 0:
                ins = nc.vector.tensor_tensor_scan(s, carry[0], s, 0.0, ALU.mult, ALU.add)
            else:
                ins = nc.vector.tensor_tensor_scan(s[:, ::-1], carry[1][:, ::-1], s[:, ::-1], 0.0,
                                                   ALU.mult, ALU.add)
            ins.then_inc(sum_out, 1)

        def rec_ends(g):
            return G_SUM[g % 2].rearrange("p (c t) -> p c t", t=P)[:, :, P - 1:P] if g % 2 == 0 else \
                G_SUM[g % 2].rearrange("p (c t) -> p c t", t=P)[:, :, 0:1]

        def rec_end_diff(eng, g):
            eng.wait_ge(sum_out, g + 1)
            if g:
                eng.wait_ge(keys_turned, g)
            nc.gpsimd.tensor_tensor(G_END.rearrange("p (c t) -> p c t", t=P), rec_ends(g).to_broadcast([P, TT, P]),
                                    G_SUM[g % 2].rearrange("p (c t) -> p c t", t=P), ALU.subtract)\
                .then_inc(end_diff, 1)

        def rec_end_exp(eng, g):
            eng.wait_ge(sum_out, g + 1)
            if g >= 2:
                eng.wait_ge(rec_mm, g // 2)
            nc.scalar.activation(G_QUERY[g % 2], G_SUM[g % 2], ACT.Exp)
            eng.wait_ge(end_diff, g + 1)
            nc.scalar.activation(G_END, G_END, ACT.Exp).then_inc(end_exp, 1)

        def rec_end_mul(eng, g):
            eng.wait_ge(end_exp, g + 1)
            q, h = G_QUERY[g % 2], g // 2
            at = P - 1 if g % 2 == 0 else 0
            link(eng, "dve", nc.vector.tensor_copy(
                decay[:, 4 * (g % 2):4 * (g % 2) + 4],
                q.rearrange("p (c t) -> p c t", t=P)[:, :, at:at + 1].rearrange("p c t -> p (c t)")))
            nc.vector.tensor_tensor(q, q, ar(QH + h), ALU.mult)
            nc.vector.tensor_tensor(G_END, G_END, G_KEY[g % 2], ALU.mult).then_inc(ends_out, 1)

        def rec_turn_keys(eng, g):
            eng.wait_ge(ends_out, g + 1)
            if g:
                eng.wait_ge(keys_sb, g)
            for i in range(TT - 1):
                c = key_chunk(g % 2, i)
                last = nc.tensor.transpose(bank[2][:, i * P:(i + 1) * P], G_END[:, c * P:(c + 1) * P], ident)
            last.then_inc(keys_turned, 1)

        def rec_copy_keys(eng, g):
            eng.wait_ge(keys_turned, g + 1)
            if g:
                eng.wait_ge(update_mm, g)
            nc.scalar.activation(G_KEYT[:, 0:3 * P], bank[2][:, 0:3 * P], ACT.Copy).then_inc(keys_sb, 1)

        def rec_updates(eng, g):
            eng.wait_ge(keys_sb, g + 1)
            if g:
                eng.wait_ge(states_out, g)
            h = g // 2
            for i in range(TT - 1):
                c = key_chunk(g % 2, i)
                last = nc.tensor.matmul(bank[3][:, i * P:(i + 1) * P], G_KEYT[:, i * P:(i + 1) * P],
                                        ar(VR + c)[:, h * P:(h + 1) * P], start=True, stop=True)
            last.then_inc(update_mm, 1)

        def rec_states(eng, g):
            eng.wait_ge(update_mm, g + 1)
            if g >= 2:
                eng.wait_ge(rec_mm, g // 2)
            st = G_STATE[g % 2]
            link(eng, "dve", nc.vector.tensor_copy(st[:, 0:P], bank[3][:, 0:P]))
            for i in (1, 2):
                d = 4 * (g % 2) + key_chunk(g % 2, i)
                ins = nc.vector.scalar_tensor_tensor(st[:, i * P:(i + 1) * P], st[:, (i - 1) * P:i * P],
                                                     decay[:, d:d + 1], bank[3][:, i * P:(i + 1) * P],
                                                     ALU.mult, ALU.add)
                if i == 1:
                    link(eng, "dve", ins)
            ins.then_inc(states_out, 1)

        def level_sub(eng, g, n):
            e = LEVELS * g + n
            if n == 0:
                eng.wait_ge(sum_out, g + 1)
            i = 8 * g + n + 1
            if e >= 2:
                eng.wait_ge(level_mm, i - 1 if n >= 2 else i - 2)
            w = 1 << n
            s = G_SUM[g % 2].rearrange("p (b w) -> p b w", w=2 * w)
            mid_at = w - 1 if g % 2 == 0 else w
            nc.gpsimd.tensor_tensor(G_X[e % 2].rearrange("p (b w) -> p b w", w=2 * w), s,
                                    s[:, :, mid_at:mid_at + 1].to_broadcast([P, S // (2 * w), 2 * w]),
                                    ALU.subtract).then_inc(level_diff, 1)

        def level_exps(eng, g, n):
            e = LEVELS * g + n
            eng.wait_ge(level_diff, e + 1)
            for half, sign in zip(halves(G_X[e % 2], n, g % 2), (1.0, -1.0)):
                ins = nc.scalar.activation(half, half, ACT.Exp, scale=sign)
            ins.then_inc(level_exp, 1)

        def level_mul(eng, g, n):
            e = LEVELS * g + n
            eng.wait_ge(level_exp, e + 1)
            for half, by in zip(halves(G_X[e % 2], n, g % 2), (ar(QH + g // 2), G_KEY[g % 2])):
                other = halves(by, n, g % 2)[0 if by is not G_KEY[g % 2] else 1]
                ins = nc.vector.tensor_tensor(half, half, other, ALU.mult)
            ins.then_inc(level_in, 1)

        def level_scores(eng, g, i):
            at = 8 * g + i
            if i:
                eng.wait_ge(level_in, LEVELS * g + i)
            else:
                eng.wait_ge(floor_out, g + 1)
            if at >= 2:
                eng.wait_ge(level_out, at - 1)
            for c in range(TT):
                cs = slice(c * P, (c + 1) * P)
                keys, qs = (G_X[(LEVELS * g + i - 1) % 2],) * 2 if i else (G_KEY[g % 2], ar(QH + g // 2))
                last = nc.tensor.matmul(bank[at % 2][:, cs], keys[:, cs], qs[:, cs], start=True, stop=True)
            last.then_inc(level_mm, 1)

        def level_keep(eng, g, i):
            at = 8 * g + i
            eng.wait_ge(level_mm, at + 1)
            dst = G_SCORE[g % 2].rearrange("p (c t) -> p c t", t=P)
            src = bank[at % 2][:, :].rearrange("p (c t) -> p c t", t=P)
            if i == 0:
                if g >= 2:
                    eng.wait_ge(rec_mm, g // 2)
                ins = nc.vector.tensor_tensor(dst, src, ident.unsqueeze(1).to_broadcast([P, TT, P]), ALU.mult)
            else:
                eng.wait_ge(level_out, at)
                mask = const(f"lv{'fb'[g % 2]}{i - 1}").bitcast(U32).unsqueeze(1).to_broadcast([P, TT, P])
                ins = nc.vector.copy_predicated(dst, mask, src)
            ins.then_inc(level_out, 1)

        def rec_values(eng, h):
            eng.wait_ge(level_out, 16 * h + 16)
            eng.wait_ge(states_out, 2 * h + 2)
            if h >= 2:
                eng.wait_ge(rec_out, h - 1)
            for c in range(TT):
                cs = slice(c * P, (c + 1) * P)
                terms = [(ar(VR + c)[:, h * P:(h + 1) * P], G_SCORE[d][:, cs]) for d in range(2)]
                for d in range(2):
                    i = c - 1 if d == 0 else TT - 2 - c
                    if i >= 0:
                        terms.append((G_STATE[d][:, i * P:(i + 1) * P], G_QUERY[d][:, cs]))
                for n, (a, b) in enumerate(terms):
                    last = nc.tensor.matmul(bank[6 + h % 2][:, cs], a, b, start=n == 0, stop=n == len(terms) - 1)
            last.then_inc(rec_mm, 1)

        x_tok = ar(16, 8).rearrange("p (t d) -> p t d", d=D)
        hot_sb = ar(26, 4)[0:33, 0:STRIP + FWD]
        rel_rep = ar(31)[0:33].rearrange("b (h p) -> b h p", p=P)
        stage_strip, stage_fwd = prob_t[:, 0:STRIP], prob[0:N_CMP, 0:FWD]

        row_stage = ar(24)[:, 0:2 * P].rearrange("r (g p) -> r g p", p=P)
        column_loads = []

        def rows_of(name, src, i=0, c0=0):
            r = col_at[name] + i
            n, w = src.shape
            column_loads.append((row_stage[r % P:r % P + n, r // P, c0:c0 + w], src))

        def vector(name, v, i=0, c0=0):
            rows_of(name, v.rearrange("(a p) -> a p", a=1), i, c0)

        def by_tile(name, v):
            rows_of(name, v.rearrange("(k p) -> k p", p=P))

        by_tile("norm1", A["norm1_w"][0])
        for j in range(3):
            rows_of("conv_w", A["conv_w"][0, j].rearrange("(k p) -> k p", p=P), 2 * j)
        by_tile("conv_b", A["conv_b"][0])
        for c0 in (0, 64):
            vector("qn", A["nsa_q_norm"][0], 0, c0)
            vector("kn0", A["nsa_k_norm"][0, 0], 0, c0)
            vector("kn12", A["nsa_k_norm"][0, 1 + c0 // 64], 0, c0)
        for kv in range(2):
            rows_of("pos", A["cmp_pos"][0, kv].rearrange("(j a) d -> j (a d)", a=2), 16 * kv)
        vector("qa", A["mla_q_a_norm"][0, 0:P])
        vector("qa", A["mla_q_a_norm"][0, P:192], 1)
        vector("kvn", A["mla_kv_norm"][0])
        vector("mqn", A["mla_q_norm"][0])
        vector("mkn", A["mla_k_norm"][0])
        by_tile("onw", A["out_norm_w"][0])
        by_tile("norm2", A["norm2_w"][0])
        by_tile("nmix", A["norm_mix_2"][0])
        for d in range(2):
            for e in range(2):
                rows_of("lb", A["lower_bounds_2"][d, e].rearrange("(k p) -> k p", p=P), 8 * d + 4 * e)
        by_tile("hgn", A["hg_norm_2"][0])
        by_tile("nmem", A["norm_mem_2"][0])
        by_tile("nmkv", A["norm_mem_kv_2"][0])
        by_tile("nffn", A["norm_ffn_2"][0])
        for j in range(3):
            rows_of("cw2", A["conv_w_2"][0, j].rearrange("(k p) -> k p", p=P), 22 * j)
        by_tile("cb2", A["conv_b_2"][0])
        by_tile("fin", A["final_norm_2"])
        column_loads.append((rel_sb[0:32, :], A["rel_bias"]))
        cw2 = cw2_sb[:, :].rearrange("p (a c) -> p a c", c=64)
        column_loads.append((cw2, A["cmp_w2"][0].rearrange("v (m p) c -> p (v m) c", p=P)))
        column_loads.append((sink_sb[:, :], A["attn_sink_2"].to_broadcast([P, 8])))
        assert all(r.shape[0] + 0 <= P for r, _ in column_loads) and ncol <= 2 * P

        block = ctx.enter_context(nc.Block())

        @block.sync
        def _(eng):
            for half in range(2):
                ds = slice(half * S, (half + 1) * S)
                eng.dma_start(x_tok[:, :, ds], A["x"][0].rearrange("(t p) d -> p t d", p=P)[:, :, ds]).then_inc(x_in[half], 16)

            def fetch(i):
                if i >= SLOTS:
                    wait_released(eng, i - SLOTS)
                for dst, src in part_list(i):
                    eng.dma_start(dst, src).then_inc(slot_in[i % SLOTS], 16)

            for i in range(len(loads)):
                fetch(i)
            eng.wait_ge(out_done, 16 * 4)

        @block.gpsimd
        def _(eng):
            eng.dma_start(const_sb[:, 0:SHARED], A["consts"][:, 0:SHARED]).then_inc(const_in, 16)
            eng.dma_start(hot_sb, A["hot"]).then_inc(hot_in, 16)
            eng.dma_start(const_sb[:, SHARED:SHARED + b1_cols],
                          A["consts"][:, SHARED:SHARED + b1_cols]).then_inc(const1_in, 16)
            nc.gpsimd.memset(small[:, 60:62], 0.0)
            big_sum(eng, "in1")
            split_weights(eng, "a_c1")
            for h in range(4):
                eng.wait_ge(bias_sb, 2 * h + 2)
                if h:
                    eng.wait_ge(bias_out, 32 * h)
                eng.dma_start(strip_dram[h].rearrange("(p y) -> p y", y=STRIP), stage_strip).then_inc(bias_out, 16)
                eng.dma_start(fwd_dram[h].rearrange("(p y) -> p y", y=FWD), stage_fwd).then_inc(bias_out, 16)
                split_weights(eng, ("a_u1", "kcvc", "cq0", "cq1")[h])
            eng.wait_ge(bias_out, 128)
            for h in range(4):
                eng.dma_start(
                    strips[:, h * S:(h + 1) * S],
                    strip_dram[h, P - 1:P - 1 + P * (STRIP - 1)].rearrange("(p y) -> p y", y=STRIP - 1)[:, 0:S],
                ).then_inc(bias_in, 16)
                eng.dma_start(
                    cmp_bias[0:N_CMP, h * S:(h + 1) * S],
                    fwd_dram[h, 480:480 + N_CMP * (FWD - 16)].rearrange("(p y) -> p y", y=FWD - 16)[:, 0:S],
                ).then_inc(bias_in, 16)
            split_weights(eng, "wo1")
            big_sum(eng, "ffn1", tile_name="wo")
            split_weights(eng, "up3")
            eng.wait_ge(tile_filled, tile_at["wo0"] + 1)
            eng.wait_ge(big_out, 16)
            eng.dma_start(const_sb[:, SHARED:SHARED + b2_cols],
                          A["consts"][:, SHARED + b1_cols:SHARED + b1_cols + b2_cols]).then_inc(const2_in, 16)
            eng.dma_start(pos_i.bitcast(I32), A["positions_2"].to_broadcast([P, S])).then_inc(pos_in, 16)
            split_weights(eng, "wd31")
            big_sum(eng, "mix")
            split_weights(eng, "qr1")
            eng.wait_ge(big_out, 8 * big_at["mix"] + 8)
            c0 = where["carryf"][0]
            eng.dma_start(rb[:, :], A["consts"][:, c0:c0 + 2 * S]).then_inc(carry_in, 16)
            split_weights(eng, "gr1")
            for g in range(8):
                rec_end_diff(eng, g)
                for n in range(LEVELS):
                    level_sub(eng, g, n)
            split_weights(eng, "mx1")
            in_parts(eng, "g7")
            eng.dma_start(mem_tok, A["mem_2"][0].rearrange("(t p) d -> p t d", p=P)).then_inc(mem_in, 16)
            split_weights(eng, "mx7")
            big_sum(eng, "memkv")
            big_sum(eng, "mem", "memq1")
            split_weights(eng, "memo1")
            big_sum(eng, "ffn2", tile_name="memo")
            split_weights(eng, "we21")
            big_sum(eng, "fin")

        @block.tensor
        def _(eng):
            eng.wait_ge(const_in, 16)
            for k in range(KT):
                if k % 4 == 0:
                    eng.wait_ge(x_in[k // 4], 16)
                if k == 6:
                    eng.wait_ge(cols_in, 16 * len(column_loads))
                    for g in range(2):
                        last = nc.tensor.transpose(bank[7][0:P, g * P:(g + 1) * P], row_stage[:, g, :], ident)
                    last.then_inc(cols_turned, 1)
                b = open_tile(eng, f"x{k}")
                for t in range(TT):
                    last = nc.tensor.transpose(b[:, t * P:(t + 1) * P], x_tok[:, t, k * P:(k + 1) * P], ident)
                last.then_inc(tile_filled, 1)
            big_total(eng, "in1")

            def features(name, rows=P, big=None, parts=None):
                b = open_tile(eng, name)
                eng.wait_ge(w_split, w_part_at[name] + 1)
                high, low = part(w_high, name), part(w_low, name)
                for k in range(KT):
                    if big:
                        big_ready(eng, big, k)
                    if parts:
                        in_parts(eng, f"{parts}{k}")
                    a_high, a_low = nt(k)
                    passes = ((high, a_high), (high, a_low), (low, a_high))
                    for n, (w, a) in enumerate(passes):
                        last = nc.tensor.matmul(b[0:rows, :], w[:, k, 0:rows], a, start=k == 0 and n == 0,
                                                stop=k == KT - 1 and n == 2)
                last.then_inc(tile_filled, 1)

            def tokens(name, part_name=None, c0=0, cols=P):
                b = open_tile(eng, name)
                part_name = part_name or name
                eng.wait_ge(w_split, w_part_at[part_name] + 1)
                high, low = part(w_high, part_name), part(w_low, part_name)
                for t in range(TT):
                    for k in range(KT):
                        a_high, a_low = nt(k)
                        for n, (w, a) in enumerate(((high, a_high), (low, a_high), (high, a_low))):
                            last = nc.tensor.matmul(b[:, t * cols:(t + 1) * cols], a[:, t * P:(t + 1) * P],
                                                    w[:, k, c0:c0 + cols], start=k == 0 and n == 0,
                                                    stop=k == KT - 1 and n == 2)
                last.then_inc(tile_filled, 1)

            def tokens_wide(name, first, ts):
                b = open_tile(eng, name)
                eng.wait_ge(w_split, w_part_at[first] + 2)
                high, low = part_pair(w_high, first), part_pair(w_low, first)
                for i, t in enumerate(ts):
                    for k in range(KT):
                        a_high, a_low = nt(k)
                        for n, (w, a) in enumerate(((high, a_high), (low, a_high), (high, a_low))):
                            last = nc.tensor.matmul(b[:, i * 256:(i + 1) * 256].rearrange("p (b c) -> p b c", c=P),
                                                    a[:, t * P:(t + 1) * P], w[:, k], start=k == 0 and n == 0,
                                                    stop=k == KT - 1 and n == 2)
                last.then_inc(tile_filled, 1)

            def features_whole(name, load_name, c0, w=S, src=None, big=None):
                b = open_tile(eng, name)
                slot_ready(eng, load_name)
                sl = slot(load_name)
                for k in range(KT):
                    if big:
                        big_ready(eng, big, k)
                    last = nc.tensor.matmul(b[:, 0:w], sl[:, k * 256 + c0:k * 256 + c0 + P], src(k),
                                            start=k == 0, stop=k == KT - 1)
                last.then_inc(tile_filled, 1)

            def down(name, hidden_name, parts, n):
                banks = [open_tile(eng, f"{name}{m}") if m < 4 else bank[m] for m in range(KT)]

                def step(k, m):
                    (a_high, a_low), w = nt(k % 8), [part(x, f"{parts}{k}")[:, m, :] for x in (w_high, w_low)]
                    for p, (w_, a) in enumerate(((w[0], a_high), (w[0], a_low), (w[1], a_high))):
                        ins = nc.tensor.matmul(banks[m][:, :], w_, a, start=k == 0 and p == 0,
                                               stop=k == n - 1 and p == 2)
                    return ins

                for k in range(n):
                    in_parts(eng, f"{hidden_name}{k}")
                    eng.wait_ge(w_split, w_part_at[f"{parts}{k}"] + 1)
                    if k < n - 2:
                        for m in range(KT):
                            last = step(k, m)
                        last.then_inc(hidden_used, 1)
                for m in range(KT):
                    step(n - 2, m)
                    step(n - 1, m).then_inc(tile_filled, 1)

            def bias_tables(h):
                if h == 0:
                    eng.wait_ge(bias_rep, 1)
                    eng.wait_ge(hot_in, 16)
                for n, (y0, w, rows) in enumerate(((0, 320, P), (320, 320, P), (640, 496, N_CMP), (1136, 496, N_CMP))):
                    if h and n % 2 == 0:
                        eng.wait_ge(bias_sb, 2 * h - 1 + n // 2)
                    if h == 0 and n == 2:
                        eng.wait_ge(big_rb, 1)
                    last = nc.tensor.matmul(bank[4 + n][0:rows, 0:w], rel_rep[:, h, 0:rows], hot_sb[:, y0:y0 + w],
                                            start=True, stop=True)
                    if n % 2:
                        last.then_inc(bias_mm, 1)

            for t in ("a_b", "a_c", "a_u", "n_q"):
                for i in range(2):
                    features(f"{t}{i}", big="in1" if (t, i) == ("a_b", 0) else None)
                bias_tables(("a_b", "a_c", "a_u", "n_q").index(t))
            features("kcvc")
            features("kskw")
            features("cq0")
            features("cq1", 96)
            tokens("gates", "cq1", 96, 12)
            eng.wait_ge(bias_sb, 8)
            norm_sums(eng, "q0")
            norm_sums(eng, "q1")
            features("ckv")
            tokens("nv")
            norm_sums(eng, "kskw")
            norm_sums(eng, "cq")
            features("s_q0")
            features("s_q1")
            norm_sums(eng, "ckv")
            features("s_k0")
            features("s_k1")
            tokens_wide("s_v0", "s_v0", (0, 1))
            tokens_wide("s_v1", "s_v0", (2, 3))

            sl = slot("small")
            slot_ready(eng, "small")
            normed(eng, "ckv")
            eng.wait_ge(const1_in, 16)
            for h in range(4):
                b = open_tile(eng, f"mq{h}")
                nc.tensor.matmul(b[0:96, :], sl[:, 96 * h:96 * h + 96], ar(CQ), start=True, stop=False)
                nc.tensor.matmul(b[0:96, :], sl[0:64, 384 + 96 * h:480 + 96 * h], ar(CQ + 1)[0:64], start=False,
                                 stop=True).then_inc(tile_filled, 1)
            for h in range(4):
                b = open_tile(eng, f"mk{h}")
                nc.tensor.matmul(b[0:64, :], sl[:, WKV_AT + P * h:WKV_AT + P * h + 64], ar(CKV), start=True,
                                 stop=True).then_inc(tile_filled, 1)
            taken(eng, "cq1")
            nc.tensor.matmul(bank[7][0:96, :], const("turn96")[64:96, :], ar(CQ + 1)[64:96], start=True,
                             stop=True).then_inc(turned, 1)
            wkv = sl[:, WKV_AT:WKV_AT + S].rearrange("p (h c) -> p h c", c=P)
            for i in range(2):
                b = open_tile(eng, f"mv{i}")
                for j in range(2):
                    t = 2 * i + j
                    last = nc.tensor.matmul(b[:, 256 * j:256 * j + 256], ar(CKV)[:, t * P:(t + 1) * P],
                                            wkv[:, :, 64:P], start=True, stop=True)
                last.then_inc(tile_filled, 1)
            for h in range(4):
                taken(eng, f"mq{h}")
                eng.wait_ge(rope_out, h + 1)
                nc.tensor.matmul(bank[7][0:96, :], const("turn96")[0:96, :], ar(MQ + h)[0:96], start=True,
                                 stop=True).then_inc(turned, 1)
            for kv in range(2):
                b = open_tile(eng, f"hid{kv}")
                eng.wait_ge(blocks_out, kv + 1)
                blk = (blocks, ar(AV + 1))[kv][:, 0:16 * N_CMP].rearrange("p (j n) -> p j n", n=N_CMP)
                slot_ready(eng, f"cmp{kv}0")
                slot_ready(eng, f"cmp{kv}1")
                for m in range(2):
                    for j in range(16):
                        w = slot(f"cmp{kv}{j // 8}")
                        last = nc.tensor.matmul(b[:, 32 * m:32 * m + N_CMP],
                                                w[:, (j % 8) * 256 + m * P:(j % 8) * 256 + (m + 1) * P],
                                                blk[:, j, :], start=j == 0, stop=j == 15)
                last.then_inc(tile_filled, 1)
            for h in range(4):
                norm_sums(eng, f"mq{h}")
            b = open_tile(eng, "kc")
            eng.wait_ge(hid_out, 1)
            for m in range(2):
                last = nc.tensor.matmul(b[0:64, 0:N_CMP], cw2[:, m, :], hidden[:, m, 0:N_CMP], start=m == 0,
                                        stop=m == 1)
            last.then_inc(tile_filled, 1)
            b = open_tile(eng, "vc")
            eng.wait_ge(hid_out, 2)
            for m in range(2):
                last = nc.tensor.matmul(b[0:N_CMP, 0:64], hidden[:, 2 + m, 0:N_CMP], cw2[:, 2 + m, :], start=m == 0,
                                        stop=m == 1)
            last.then_inc(tile_filled, 1)
            for h in range(4):
                norm_sums(eng, f"mk{h}")
            norm_sums(eng, "kc")

            taken(eng, "kc")
            taken(eng, "vc")
            taken(eng, "s_v1")
            eng.wait_ge(gates_out, 1)
            eng.wait_ge(bias_in, 128)
            normed(eng, "kc")
            attend_pe(eng, 0, N_B1)
            eng.wait_ge(head_out, 4)
            stick_scores(eng, 0)
            for h in range(4):
                if h + 1 < 4:
                    stick_scores(eng, h + 1)
                stick_sums(eng, h)
                stick_values(eng, h)
            for g in range(4):
                norm_sums(eng, f"y{g}")
            for m in range(8):
                features(f"wo{m}", parts="y" if m == 0 else None)
            big_total(eng, "ffn1")
            for m in range(32):
                features(f"up{m}", big="ffn1" if m == 0 else None)
            down("dn", "h", "wd", 32)
            big_total(eng, "mix")
            for h in range(4):
                features(f"qr{h}", big="mix" if h == 0 else None)
            for g in range(8):
                features(f"z{g}")
            for i in range(4):
                tokens_wide(f"v{i}", f"v{i // 2 * 2}", (2 * (i % 2), 2 * (i % 2) + 1))
            for h in range(4):
                features(f"g{h}")
            eng.wait_ge(const2_in, 16)
            for h in range(4):
                features(f"qa{h}")
            features("ka")
            tokens("va")
            for i in range(5):
                taken(eng, f"qa{i}" if i < 4 else "ka")
                if i:
                    eng.wait_ge(rope2, i)
                nc.tensor.matmul(bank[7][:, :], const("turn16"), ar(QA + i) if i < 4 else ar(K_RAW), start=True,
                                 stop=True).then_inc(turned2, 1)
            taken(eng, "va")
            eng.wait_ge(rope2, 5)
            attend_pe(eng, N_B1, N_GQA)
            eng.wait_ge(head_out, 10)
            for g in range(8):
                for i in range(8):
                    level_scores(eng, g, i)
                    if i == 1:
                        rec_turn_keys(eng, g)
                    if i == 3:
                        rec_updates(eng, g)
                if g % 2:
                    rec_values(eng, g // 2)
            for h in range(4):
                norm_sums(eng, f"r{h}")
            for i in range(4):
                for n in ("gr", "ga"):
                    for j in range(2):
                        features(f"{n}{2 * i + j}")
                slot_ready(eng, f"br{i}")
                sl = slot(f"br{i}")
                if i == 0:
                    eng.wait_ge(rec_gated, 4)
                for j in range(2):
                    for a, n in enumerate(("rec", "att")):
                        b = open_tile(eng, f"{n}{2 * i + j}")
                        for k in range(4):
                            at = 1024 * a + 256 * k + j * P
                            last = nc.tensor.matmul(b[:, :], sl[:, at:at + P], ar((QH, QA)[a] + k), start=k == 0,
                                                    stop=k == 3)
                        last.then_inc(tile_filled, 1)
            for m in range(8):
                features(f"mx{m}", parts="g" if m == 0 else None)
            eng.wait_ge(mem_in, 16)
            for k in range(8):
                b = open_tile(eng, f"m{k}")
                for t in range(2):
                    last = nc.tensor.transpose(b[:, t * P:(t + 1) * P], mem_tok[:, t, k * P:(k + 1) * P], ident)
                last.then_inc(tile_filled, 1)
            big_total(eng, "memkv")
            for m in range(8):
                features_whole(f"memk{m}", f"mkv{m // 2}", (m % 2) * P, 256, mem_t, "memkv" if m == 0 else None)
            for i in range(4):
                b = open_tile(eng, f"memv{i}")
                slot_ready(eng, f"mkv{4 + i}")
                sl = slot(f"mkv{4 + i}")
                for t in range(2):
                    for k in range(KT):
                        last = nc.tensor.matmul(b[:, t * 256:(t + 1) * 256], mem_t(k)[:, t * P:(t + 1) * P],
                                                sl[:, k * 256:(k + 1) * 256], start=k == 0, stop=k == KT - 1)
                last.then_inc(tile_filled, 1)
            big_total(eng, "mem")
            for m in range(8):
                features(f"memq{m}", big="mem" if m == 0 else None)
            taken(eng, "memq7")
            taken(eng, "memv3")
            attend_pe(eng, N_GQA, N_ALL)
            eng.wait_ge(head_out, 18)
            for m in range(8):
                features(f"memo{m}", parts="o" if m == 0 else None)
            big_total(eng, "ffn2")
            for i in range(11):
                for n in ("g2_", "u2_"):
                    for j in range(2):
                        features(f"{n}{2 * i + j}", big="ffn2" if (i, n, j) == (0, "g2_", 0) else None)
            down("d2n", "e", "we", 22)
            big_total(eng, "fin")
            for i in range(8):
                b = open_tile(eng, f"o{i}")
                t, half = i // 2, i % 2
                for k in range(4):
                    big_ready(eng, "fin", 4 * half + k)
                    last = nc.tensor.transpose(b[:, k * P:(k + 1) * P], ar(8 + 4 * half + k)[:, t * P:(t + 1) * P], ident)
                last.then_inc(tile_filled, 1)

        @block.scalar
        def _(eng):
            nc.scalar.preload_act_table_set("natural_log_exp_and_others")
            eng.wait_ge(cols_zero, 1)
            for dst, src in column_loads:
                eng.dma_start(dst, src).then_inc(cols_in, 16)

            def take(name, dst, rows=P, w=S, func=ACT.Copy, scale=1.0):
                b = filled(eng, name)
                nc.scalar.activation(dst, b[0:rows, 0:w], func, scale=scale).then_inc(taken_act, 1)

            for k in range(KT):
                take(f"x{k}", xt(k))
                taken(eng, f"x{k}")
                big_square(eng, "in1", k)
            round_weights(eng, "a_b1")
            eng.wait_ge(bias_rep, 1)
            big_factor(eng, "in1")
            big_round(eng, "in1")
            for i in range(2):
                take(f"a_b{i}", ar(AB + i))
                ahead(eng, f"a_b{i}")
            for i in range(2):
                take(f"a_c{i}", ar(AV + i))
                ahead(eng, f"a_c{i}")
            for i in range(2):
                ahead(eng, f"a_u{i}")
            for i in range(2):
                take(f"n_q{i}", ar(AQ + i))
                ahead(eng, f"n_q{i}")
            b = filled(eng, "kcvc")
            eng.wait_ge(conv_v, 2)
            nc.scalar.activation(kcd[0:64, :], b[0:64, :], ACT.Copy)
            nc.scalar.activation(kcd[64:P, 0:S - 1], b[0:64, 1:S], ACT.Copy)
            nc.scalar.activation(vcd[0:64, :], b[64:P, :], ACT.Copy)
            nc.scalar.activation(vcd[64:P, 0:S - 1], b[64:P, 1:S], ACT.Copy).then_inc(taken_act, 1)
            ahead(eng, "kcvc")
            take("kskw", ar(KSKW))
            ahead(eng, "kskw")
            taken(eng, "kskw")
            eng.wait_ge(conv_v, 4)
            norm_squares(eng, "q0")
            norm_squares(eng, "q1")
            take("cq0", ar(CQ))
            ahead(eng, "cq0")
            take("cq1", ar(CQ + 1)[0:96], 96)
            take("gates", gates, P, 48, ACT.Exp, -1.0)
            ahead(eng, "cq1")
            norm_factor(eng, "q0")
            norm_squares(eng, "kskw")
            norm_factor(eng, "q1")
            take("ckv", ar(CKV))
            ahead(eng, "ckv")
            taken(eng, "ckv")
            norm_squares(eng, "cq")
            ahead(eng, "nv")
            norm_factor(eng, "kskw")
            take("s_q0", ar(SQT), scale=0.125)
            ahead(eng, "s_q0")
            take("s_q1", ar(SQT + 1), scale=0.125)
            ahead(eng, "s_q1")
            norm_squares(eng, "ckv")
            norm_factor(eng, "cq")
            take("s_k0", ar(SKT))
            ahead(eng, "s_k0")
            norm_factor(eng, "ckv")
            take("s_k1", ar(SKT + 1))
            ahead(eng, "s_k1")
            for h in range(4):
                take(f"mq{h}", ar(MQ + h)[0:96], 96)
            for h in range(4):
                take(f"mk{h}", ar(MK + h)[0:64], 64)
            for kv in range(2):
                b = filled(eng, f"hid{kv}")
                if kv:
                    eng.wait_ge(hid_out, 1)
                nc.scalar.activation(hid_e[:, :, 0:N_CMP], b[:, 0:64].rearrange("p (a n) -> p a n", n=32)[:, :, 0:N_CMP],
                                     ACT.Exp, scale=-1.0).then_inc(hid_exp, 1)
            for h in range(4):
                eng.wait_ge(rope_out, h + 2)
                norm_squares(eng, f"mq{h}")
                if h:
                    norm_factor(eng, f"mq{h - 1}")
            take("kc", kc_raw[0:64, 0:N_CMP], 64, N_CMP)
            taken(eng, "kc")
            for h in range(4):
                norm_squares(eng, f"mk{h}")
                norm_factor(eng, f"mk{h - 1}" if h else "mq3")
            norm_squares(eng, "kc")
            norm_factor(eng, "mk3")
            norm_factor(eng, "kc")
            round_weights(eng, "wo1")
            attend_act(eng, 0, N_B1, pair_end_b1)
            stick_logs(eng, 0)
            for h in range(4):
                if h + 1 < 4:
                    stick_logs(eng, h + 1)
                stick_exps(eng, h)
                if h % 2:
                    take_stick(eng, h // 2)
            eng.wait_ge(head_out, 6)
            eng.wait_ge(conv_v, 4)
            for g in range(4):
                norm_squares(eng, f"y{g}")
                if g:
                    norm_factor(eng, f"y{g - 1}")
                if g >= 2:
                    normed(eng, f"y{g - 2}")
                    for i in range(2):
                        part_round(eng, f"y{2 * (g - 2) + i}")
            norm_factor(eng, "y3")
            for k in range(4, 8):
                normed(eng, f"y{k // 2}")
                part_round(eng, f"y{k}")

            def big_norm(name, tile_name, parts=None, keep_ahead=False, then=None):
                for k in range(KT):
                    if keep_ahead:
                        ahead(eng, f"{tile_name}{k}")
                    if k == 6 and parts:
                        round_weights(eng, parts)
                    taken(eng, f"{tile_name}{k}")
                    big_square(eng, name, k)
                if then:
                    round_weights(eng, then)
                big_factor(eng, name)
                if name in split_big_at:
                    big_round(eng, name)

            big_norm("ffn1", "wo", keep_ahead=True)
            for m in range(32):
                if m == 16:
                    nc.scalar.preload_act_table_set("silu_and_others")
                    for i in range(2):
                        t = (sin16, cos16)[i]
                        eng.wait_ge(trig_dve, i + 1)
                        nc.scalar.activation(t, t, ACT.Sin).then_inc(trig_act, 1)
                    nc.scalar.preload_act_table_set("natural_log_exp_and_others")
                    eng.wait_ge(low_dve, 1)
                    nc.scalar.activation(low_e, low_e, ACT.Exp).then_inc(low_act, 1)
                b = filled(eng, f"up{m}")
                link(eng, "act", nc.scalar.activation(ar(m), b[:, :], ACT.Relu))
                nc.scalar.activation(ar(m), ar(m), ACT.Square).then_inc(taken_act, 1)
                ahead(eng, f"up{m}")
            round_hidden(eng, "h", "wd", 32, 0, "up")
            big_norm("mix", "dn", then="qr1")
            for h in range(4):
                b = filled(eng, f"qr{h}")
                nc.scalar.activation(ar(QH + h), b[:, :], ACT.Exp, scale=-1.0).then_inc(qr_exp, 1)
                ahead(eng, f"qr{h}")
            for g in range(8):
                take(f"z{g}", ar(FG + g), func=ACT.Exp, scale=-1.0)
                ahead(eng, f"z{g}")
            for i in range(4):
                b = filled(eng, f"v{i}")
                dst = ar(VR, 4).rearrange("p (t d) -> p t d", d=S)[:, 2 * (i % 2):2 * (i % 2) + 2,
                                                                  256 * (i // 2):256 * (i // 2) + 256]
                nc.scalar.activation(dst, b[:, :].rearrange("p (t d) -> p t d", d=256), ACT.Copy)\
                    .then_inc(taken_act, 1)
                ahead(eng, f"v{i}")
            for h in range(4):
                b = filled(eng, f"g{h}")
                nc.scalar.activation(ar(GR + h), b[:, :], ACT.Exp, scale=-1.0).then_inc(g_exp, 1)
                ahead(eng, f"g{h}")
            for h in range(4):
                take(f"qa{h}", ar(QA + h))
                ahead(eng, f"qa{h}")
            take("ka", ar(K_RAW))
            ahead(eng, "ka")
            ahead(eng, "va")

            def pair_end_gqa(eng, u):
                _, h, qt = units[u]
                if h % 2 == 1 and qt == TT - 1:
                    take_heads(eng, u, ar(QA + h // 2))

            attend_act(eng, N_B1, N_GQA, pair_end_gqa)
            rec_log(eng, 0)
            for g in range(8):
                rec_end_exp(eng, g)
                for n in range(LEVELS):
                    level_exps(eng, g, n)
                    if n == 1:
                        rec_copy_keys(eng, g)
                    if n == 3 and g + 1 < 8:
                        rec_log(eng, g + 1)
                if g % 2:
                    eng.wait_ge(rec_mm, g // 2 + 1)
                    nc.scalar.activation(ar(QH + g // 2), bank[6 + (g // 2) % 2][:, :], ACT.Copy).then_inc(rec_out, 1)
            for h in range(4):
                eng.wait_ge(rec_out, h + 1)
                norm_squares(eng, f"r{h}")
                if h:
                    norm_factor(eng, f"r{h - 1}")
            norm_factor(eng, "r3")
            for i in range(4):
                for j in range(4):
                    n = f"{('gr', 'ga')[j // 2]}{2 * i + j % 2}"
                    if i:
                        eng.wait_ge(merged, 2 * i)
                    take(n, ar(4 + j), func=ACT.Exp, scale=-1.0)
                    ahead(eng, n)
            for k in range(8):
                eng.wait_ge(merged, k + 1)
                part_round(eng, f"g{k}")
            for m in range(6):
                ahead(eng, f"mx{m}")
            for k in range(8):
                take(f"m{k}", mem_t(k), w=256)
                taken(eng, f"m{k}")
                big_square(eng, "memkv", k)
            big_factor(eng, "memkv")
            for m in range(8):
                take(f"memk{m}", mem_k[:, m, :], w=256)
            big_norm("mem", "mx", "memq1")
            for m in range(8):
                take(f"memq{m}", ar(MEMQ + m))
                ahead(eng, f"memq{m}")

            def pair_end_mem(eng, u):
                _, h, qt = units[u]
                if qt == TT - 1:
                    take_heads(eng, u, [ar(2 * h), ar(2 * h + 1)])
                    eng.wait_ge(head_out, 12 + 2 * h)
                    for i in range(2):
                        part_round(eng, f"o{2 * h + i}")

            attend_act(eng, N_GQA, N_ALL, pair_end_mem)
            big_norm("ffn2", "memo", keep_ahead=True)
            nc.scalar.preload_act_table_set("silu_and_others")
            eng.wait_ge(pads, 1)
            for m in range(22):
                b = filled(eng, f"g2_{m}")
                if m >= 2:
                    eng.wait_ge(conv2_out, m - 1)
                nc.scalar.activation(padded[m % 2][:, 1:S + 1], b[:, :], ACT.Copy).then_inc(taken_act, 1)
                ahead(eng, f"g2_{m}")
                if m % 2:
                    for i in (m - 1, m):
                        eng.wait_ge(conv2_out, i + 1)
                        if i >= 2:
                            taken(eng, f"u2_{i - 2}")
                        nc.scalar.activation(conv_e[i % 2], conv_c[i % 2], ACT.Silu).then_inc(conv2_silu, 1)
                    for i in (m - 1, m):
                        ahead(eng, f"u2_{i}")
            nc.scalar.preload_act_table_set("natural_log_exp_and_others")
            round_hidden(eng, "e", "we", 22, 30, "u2_")
            big_norm("fin", "d2n")
            for i in range(1, 8, 2):
                take(f"o{i}", ar(i))
            for t in range(4):
                taken(eng, f"o{2 * t}")
                taken(eng, f"o{2 * t + 1}")
                eng.dma_start(out[0, t * P:(t + 1) * P, :], ar(2 * t, 2)).then_inc(out_done, 16)

        @block.vector
        def _(eng):
            nc.vector.memset(eps_col, EPS)
            nc.vector.memset(rel_rep[32:33], MASKED)
            nc.vector.memset(one_col, 1.0)
            nc.vector.memset(ar(24)[:, 0:2 * P], 0.0).then_inc(cols_zero, 1)
            eng.wait_ge(cols_turned, 1)
            nc.vector.tensor_copy(col_sb[:, :], bank[7][:, 0:ncol]).then_inc(cols_out, 1)
            eng.wait_ge(const_in, 16)
            for h in range(4):
                last = nc.vector.tensor_scalar(rel_rep[0:32, h, :], ones[0:32], rel_sb[0:32, h:h + 1], 8.0,
                                               ALU.mult, ALU.mult)
            last.then_inc(bias_rep, 1)
            eng.wait_ge(cols_out, 1)
            big_apply(eng, "in1")

            def take(name, dst, rows=P, w=S):
                b = filled(eng, name)
                nc.vector.tensor_copy(dst, b[0:rows, 0:w]).then_inc(taken_dve, 1)

            def take_bias(h):
                eng.wait_ge(bias_mm, 2 * h + 1)
                if h:
                    eng.wait_ge(bias_out, 32 * h)
                nc.vector.tensor_copy(stage_strip[:, 0:320], bank[4][:, 0:320])
                nc.vector.tensor_copy(stage_strip[:, 320:640], bank[5][:, 0:320]).then_inc(bias_sb, 1)
                eng.wait_ge(bias_mm, 2 * h + 2)
                nc.vector.tensor_copy(stage_fwd[:, 0:496], bank[6][0:N_CMP, 0:496])
                nc.vector.tensor_copy(stage_fwd[:, 496:992], bank[7][0:N_CMP, 0:496]).then_inc(bias_sb, 1)

            take_bias(0)
            take_bias(1)
            for i in range(2):
                b = filled(eng, f"a_u{i}")
                taken(eng, f"a_c{i}")
                v, y = ar(AV + i), tile(sq, 2 + i)
                nc.vector.tensor_tensor(v, v, b[:, :], ALU.mult).then_inc(taken_dve, 1)
                taken(eng, f"a_u{i}")
                link(eng, "dve", nc.vector.tensor_scalar(y, v, col("conv_w", 4 + i), col("conv_b", i),
                                                         ALU.mult, ALU.add))
                link(eng, "dve", nc.vector.scalar_tensor_tensor(y[:, 1:S], v[:, 0:S - 1], col("conv_w", 2 + i),
                                                                y[:, 1:S], ALU.mult, ALU.add))
                nc.vector.scalar_tensor_tensor(y[:, 2:S], v[:, 0:S - 2], col("conv_w", i),
                                               y[:, 2:S], ALU.mult, ALU.add).then_inc(conv_v, 1)
            eng.wait_ge(conv_v, 2)
            for i in range(2):
                nc.vector.tensor_tensor(yt(i), tile(sq, 2 + i), ar(AB + i), ALU.mult).then_inc(conv_v, 1)
            take_bias(2)
            take_bias(3)
            norm_apply(eng, "q0")
            taken(eng, "gates")
            link(eng, "dve", nc.vector.tensor_scalar(gates, gates, 1.0, None, ALU.add))
            nc.vector.reciprocal(gates, gates).then_inc(gates_out, 1)
            norm_apply(eng, "q1")
            take("nv", nv)
            norm_apply(eng, "kskw")
            norm_apply(eng, "cq")
            norm_apply(eng, "ckv")
            for i in range(2):
                take(f"s_v{i}", ar(SV + i))

            taken(eng, "kcvc")
            for kv in range(2):
                src = (kcd, vcd)[kv].rearrange("p (n l) -> p l n", l=16)
                dst = (blocks, ar(AV + 1))[kv][:, 0:16 * N_CMP].rearrange("p (j n) -> p j n", n=N_CMP)
                pos = col_sb[:, col_at["pos"] + 16 * kv:col_at["pos"] + 16 * kv + 16].unsqueeze(2)
                for half in range(2):
                    js = slice(8 * half, 8 * half + 8)
                    last = nc.vector.tensor_tensor(dst[:, js, :], src[:, 0:16:2, half:half + N_CMP],
                                                   pos[:, js, :].to_broadcast([P, 8, N_CMP]), ALU.add)
                last.then_inc(blocks_out, 1)

            def rope(r, src, dsts, rows, t):
                eng.wait_ge(turned, r + 1)
                t1, t2 = prob[rows, 0:S], prob[rows, S:2 * S]
                nc.vector.tensor_tensor(t1, src[rows], const("cos96")[rows], ALU.mult)
                link(eng, "dve", nc.vector.tensor_tensor(t2, bank[7][rows, :], const("sin96")[rows], ALU.mult))
                for d in dsts:
                    last = nc.vector.tensor_tensor(d[rows], t1, t2, ALU.add)
                last.then_inc(rope_out, 1)

            eng.wait_ge(bias_out, 128)
            eng.wait_ge(const1_in, 16)
            taken(eng, "cq1")
            rope(0, ar(CQ + 1), [ar(MK + h) for h in range(4)], slice(64, 96), None)
            for i in range(2):
                take(f"mv{i}", ar(MV + i))
            for h in range(4):
                rope(h + 1, ar(MQ + h), [ar(MQ + h)], slice(0, 96), None)
            for kv in range(2):
                b = filled(eng, f"hid{kv}")
                eng.wait_ge(hid_exp, kv + 1)
                e = hid_e[:, :, 0:N_CMP]
                link(eng, "dve", nc.vector.tensor_scalar(e, e, 1.0, None, ALU.add))
                link(eng, "dve", nc.vector.reciprocal(e, e))
                nc.vector.tensor_tensor(hidden[:, 2 * kv:2 * kv + 2, 0:N_CMP],
                                        b[:, 0:64].rearrange("p (a n) -> p a n", n=32)[:, :, 0:N_CMP], e,
                                        ALU.mult).then_inc(taken_dve, 1)
                taken(eng, f"hid{kv}")
                nc.vector.tensor_copy(small[:, 60:61], e[:, 0, 0:1]).then_inc(hid_out, 1)
            for h in range(4):
                norm_apply(eng, f"mq{h}")
            take("vc", vc[0:N_CMP], N_CMP, 64)
            for h in range(4):
                norm_apply(eng, f"mk{h}")
            norm_apply(eng, "kc")
            attend_dve(eng, 0, N_B1)
            stick_softplus(eng, 0)
            for h in range(4):
                if h + 1 < 4:
                    stick_softplus(eng, h + 1)
                stick_shift(eng, h)
            for g in range(4):
                norm_apply(eng, f"y{g}")
                if g:
                    part_rest(eng, f"y{2 * g - 2}")
                    part_rest(eng, f"y{2 * g - 1}")
            part_rest(eng, "y6")
            part_rest(eng, "y7")

            def add_to_residual(name, k):
                b = filled(eng, name)
                nc.vector.tensor_tensor(xt(k), xt(k), b[:, :], ALU.add).then_inc(taken_dve, 1)

            for k in range(KT):
                add_to_residual(f"wo{k}", k)
            big_apply(eng, "ffn1")
            TURN = 2 * math.pi
            C1 = 6.28125
            C2 = float(np.float32(0.0019350051879882812))
            C3 = TURN - C1 - C2
            eng.wait_ge(pos_in, 16)
            eng.wait_ge(const2_in, 16)
            dve = nc.vector
            link(eng, "dve", dve.tensor_copy(angle, pos_i.bitcast(I32)))
            link(eng, "dve", dve.tensor_scalar(angle, angle, const("rate"), None, ALU.mult))
            link(eng, "dve", dve.tensor_scalar(whole_i.bitcast(I32), angle, 1 / TURN, None, ALU.mult))
            link(eng, "dve", dve.tensor_copy(fold, whole_i.bitcast(I32)))
            for c in (C1, C2, C3):
                link(eng, "dve", dve.scalar_tensor_tensor(angle, fold, -c, angle, ALU.mult, ALU.add))
            for i, t in enumerate((sin16, cos16)):
                link(eng, "dve", dve.tensor_scalar(t, angle, math.pi / 2 * i, None, ALU.add))
                for _ in range(2):
                    link(eng, "dve", dve.tensor_scalar(fold, t, math.pi, -TURN, ALU.is_gt, ALU.mult))
                    link(eng, "dve", dve.tensor_tensor(t, t, fold, ALU.add))
                    link(eng, "dve", dve.tensor_scalar(fold, t, -math.pi, TURN, ALU.is_lt, ALU.mult))
                    link(eng, "dve", dve.tensor_tensor(t, t, fold, ALU.add))
                pi = float(np.nextafter(np.float32(math.pi), np.float32(0)))
                dve.tensor_scalar(t, t, pi, -pi, ALU.min, ALU.max).then_inc(trig_dve, 1)
            lb = col_sb[:, col_at["lb"]:col_at["lb"] + 16].rearrange("p (d e h) -> p d e h", e=2, h=4)
            e = low_e.rearrange("p (d e h) -> p d e h", e=2, h=4)
            mx = low_max.rearrange("p (d h) -> p d h", h=4)
            link(eng, "dve", dve.tensor_tensor(mx, lb[:, :, 0, :], lb[:, :, 1, :], ALU.max))
            dve.tensor_tensor(e[:, :, 0, :], lb[:, :, 0, :], mx, ALU.subtract)
            dve.tensor_tensor(e[:, :, 1, :], lb[:, :, 1, :], mx, ALU.subtract).then_inc(low_dve, 1)
            eng.wait_ge(low_act, 1)
            link(eng, "dve", dve.tensor_tensor(mx, e[:, :, 0, :], e[:, :, 1, :], ALU.add))
            link(eng, "dve", dve.reciprocal(low_max, low_max))
            link(eng, "dve", dve.tensor_tensor(low.rearrange("p (d h) -> p d h", h=4), mx, e[:, :, 0, :], ALU.mult))
            link(eng, "dve", dve.tensor_scalar(one_low, low, -1.0, 1.0, ALU.mult, ALU.add))
            link(eng, "dve", dve.tensor_scalar(nsink, sink_sb[:, :], -1.0, None, ALU.mult))
            for k in range(32):
                part_rest(eng, f"h{k}")
            for k in range(KT):
                add_to_residual(f"dn{k}", k)
            big_apply(eng, "mix")
            for h in range(4):
                b = filled(eng, f"qr{h}")
                eng.wait_ge(qr_exp, h + 1)
                q = ar(QH + h)
                link(eng, "dve", dve.tensor_scalar(q, q, 1.0, None, ALU.add))
                link(eng, "dve", dve.reciprocal(q, q))
                dve.scalar_tensor_tensor(q, b[:, :], P ** -0.5, q, ALU.mult, ALU.mult).then_inc(taken_dve, 1)
            for g in range(8):
                taken(eng, f"z{g}")
                f = ar(FG + g)
                link(eng, "dve", dve.tensor_scalar(f, f, 1.0, None, ALU.add))
                link(eng, "dve", dve.reciprocal(f, f))
                dve.tensor_scalar(f, f, one_low[:, g:g + 1], low[:, g:g + 1], ALU.mult, ALU.add).then_inc(f_out, 1)
            for h in range(4):
                b = filled(eng, f"g{h}")
                eng.wait_ge(g_exp, h + 1)
                q = ar(GR + h)
                link(eng, "dve", dve.tensor_scalar(q, q, 1.0, None, ALU.add))
                link(eng, "dve", dve.reciprocal(q, q))
                dve.tensor_tensor(q, b[:, :], q, ALU.mult).then_inc(taken_dve, 1)
            take("va", ar(VA))
            eng.wait_ge(trig_act, 2)
            for i in range(5):
                taken(eng, f"qa{i}" if i < 4 else "ka")
                eng.wait_ge(turned2, i + 1)
                if i:
                    eng.wait_ge(rope2, i)
                src = ar(QA + i) if i < 4 else ar(K_RAW)
                t1, t2 = prob[:, 0:S], prob[:, S:2 * S]
                dve.tensor_tensor(t1, src, cos16, ALU.mult)
                link(eng, "dve", dve.tensor_tensor(t2, bank[7][:, :], sin16, ALU.mult))
                lo, hi = slice(0, 64), slice(64, P)
                outs = [(src, slice(0, P))] if i < 4 else [
                    (ar(KA)[lo], lo), (ar(KA)[hi], lo), (ar(KA + 1)[lo], hi), (ar(KA + 1)[hi], hi)]
                for o, r in outs:
                    last = dve.tensor_tensor(o, t1[r], t2[r], ALU.add)
                last.then_inc(rope2, 1)
            eng.wait_ge(f_out, 8)
            attend_dve(eng, N_B1, N_GQA)
            rec_floor(eng, 0)
            rec_scan(eng, 0)
            for g in range(8):
                rec_end_mul(eng, g)
                level_keep(eng, g, 0)
                for n in range(LEVELS):
                    level_mul(eng, g, n)
                    if n:
                        level_keep(eng, g, n)
                    if n == 3:
                        rec_states(eng, g)
                        if g + 1 < 8:
                            rec_floor(eng, g + 1)
                    if n == 5 and g + 1 < 8:
                        rec_scan(eng, g + 1)
                level_keep(eng, g, LEVELS)
            for h in range(4):
                norm_apply(eng, f"r{h}")
                normed(eng, f"r{h}")
                dve.tensor_tensor(ar(QH + h), ar(QH + h), ar(GR + h), ALU.mult).then_inc(rec_gated, 1)
            for i in range(4):
                for j in range(4):
                    taken(eng, f"{('gr', 'ga')[j // 2]}{2 * i + j % 2}")
                    s = ar(4 + j)
                    link(eng, "dve", dve.tensor_scalar(s, s, 1.0, None, ALU.add))
                    link(eng, "dve", dve.reciprocal(s, s))
                if i == 3:
                    for k in range(6):
                        part_rest(eng, f"g{k}")
                for j in range(2):
                    m = 2 * i + j
                    b = filled(eng, f"rec{m}")
                    dve.tensor_tensor(ar(8 + m), b[:, :], ar(4 + j), ALU.mult).then_inc(taken_dve, 1)
                    b = filled(eng, f"att{m}")
                    dve.tensor_tensor(ar(6 + j), b[:, :], ar(6 + j), ALU.mult).then_inc(taken_dve, 1)
                    taken(eng, f"att{m}")
                    dve.tensor_tensor(ar(8 + m), ar(8 + m), ar(6 + j), ALU.add).then_inc(merged, 1)
            part_rest(eng, "g6")
            part_rest(eng, "g7")
            for k in range(8):
                add_to_residual(f"mx{k}", k)
            big_apply(eng, "memkv")
            for i in range(4):
                b = filled(eng, f"memv{i}")
                dve.tensor_copy(mem_v[:, :, 256 * i:256 * i + 256], b[:, :].rearrange("p (t d) -> p t d", d=256))\
                    .then_inc(taken_dve, 1)
            big_apply(eng, "mem")

            def rests_of_head(eng, u):
                _, h, qt = units[u]
                if h and qt == TT - 2:
                    for i in range(2):
                        part_rest(eng, f"o{2 * h - 2 + i}")

            attend_dve(eng, N_GQA, N_ALL, rests_of_head)
            part_rest(eng, "o6")
            part_rest(eng, "o7")
            for k in range(8):
                add_to_residual(f"memo{k}", k)
            for p in padded:
                dve.memset(p[:, 0:1], 0.0)
                last = dve.memset(p[:, S + 1:S + 2], 0.0)
            last.then_inc(pads, 1)
            big_apply(eng, "ffn2")

            def conv2(m):
                taken(eng, f"g2_{m}")
                g, c = padded[m % 2], conv_c[m % 2]
                w = [col("cw2", 22 * j + m) for j in range(3)]
                link(eng, "dve", dve.tensor_scalar(c, g[:, 0:S], w[0], col("cb2", m), ALU.mult, ALU.add))
                link(eng, "dve", dve.scalar_tensor_tensor(c, g[:, 1:S + 1], w[1], c, ALU.mult, ALU.add))
                dve.scalar_tensor_tensor(c, g[:, 2:S + 2], w[2], c, ALU.mult, ALU.add).then_inc(conv2_out, 1)

            for i in range(11):
                for m in (2 * i, 2 * i + 1):
                    conv2(m)
                for m in (2 * i, 2 * i + 1):
                    x = conv_e[m % 2]
                    eng.wait_ge(conv2_silu, m + 1)
                    b = filled(eng, f"u2_{m}")
                    dve.tensor_tensor(ar(m), x, b[:, :], ALU.mult).then_inc(taken_dve, 1)
            for k in range(22):
                part_rest(eng, f"e{k}")
            for k in range(8):
                add_to_residual(f"d2n{k}", k)
            big_apply(eng, "fin")
            for i in range(0, 8, 2):
                take(f"o{i}", ar(i))


_NAMES = [
    "x", "rel_bias", "norm1_w", "w_in", "conv_w", "conv_b", "nsa_q_norm", "nsa_k_norm", "cmp_pos", "cmp_w1", "cmp_w2",
    "mla_q_a_norm", "mla_kv_norm", "mla_wq_b", "mla_wkv_b", "mla_q_norm", "mla_k_norm", "out_norm_w", "w_out",
    "norm2_w", "ffn_w1", "ffn_w2", "mem_2", "positions_2", "norm_mix_2", "w_in_2", "lower_bounds_2", "hg_norm_2",
    "attn_sink_2", "w_br_rec_2", "w_br_att_2", "w_mix_out_2", "norm_mem_2", "norm_mem_kv_2", "w_mem_q_2",
    "w_mem_kv_2", "w_mem_o_2", "norm_ffn_2", "w_up_2", "conv_w_2", "conv_b_2", "w_down_2", "final_norm_2",
]


def kernel(**inputs):
    import concourse.bacc as bacc
    from concourse.bass_utils import run_bass_kernel_spmd

    nc = bacc.Bacc("TRN2", target_bir_lowering=False, num_devices=1)
    table, _, hot = make_consts()
    arrays = {f"in_{n}": np.ascontiguousarray(inputs[n]) for n in _NAMES}
    arrays["in_consts"], arrays["in_hot"] = table, hot
    aps = {n[3:]: nc.dram_tensor(n, a.shape, mybir.dt.from_np(a.dtype), kind="ExternalInput").ap()
           for n, a in arrays.items()}
    out = nc.dram_tensor("out", (1, S, D), F32, kind="ExternalOutput").ap()
    two_blocks(nc, aps, out)
    r = run_bass_kernel_spmd(nc, [arrays], core_ids=[0])
    return r.results[0]["out"]
```
